# Optimizing a Trainium2 kernel written in Bass

```python
import math
import jax, jax.numpy as jnp
from jax import lax
import numpy as np

D_MODEL = 1024
BATCH = 1
SEQ = 1024
DEPTH = 1

CHUNK = 64
S5_WIDTH = 512
S5_GROUP = 16
S5_GROUPS = S5_WIDTH // S5_GROUP
S5_STATE = 64
CONV_WIDTH = 512
CONV_K = 3
ATTN_HEADS = 8
HEAD_DIM = 64
ATTN_WIDTH = ATTN_HEADS * HEAD_DIM
Q_BLOCK = 128
N_BRANCH = 3
MIX_WIDTH = S5_WIDTH + CONV_WIDTH + ATTN_WIDTH
D_FF = 4 * D_MODEL
IN_WIDTH = S5_WIDTH + 3 * CONV_WIDTH + 3 * ATTN_WIDTH + ATTN_HEADS + N_BRANCH * D_MODEL
EPS = 1e-6
NEG_INF = -1e30


def rmsnorm(x, g):
    xf = x.astype(jnp.float32)
    y = xf * lax.rsqrt(jnp.mean(xf * xf, axis=-1, keepdims=True) + EPS)
    return (y * g.astype(jnp.float32)).astype(x.dtype)

def s5_mixer(u, a_re, a_im, log_dt, b_re, b_im, c_re, c_im, d_skip, w_glu):
    bsz, L, _ = u.shape
    f32 = jnp.float32
    uf = u.astype(f32).reshape(bsz, L, S5_GROUPS, S5_GROUP)
    lam = lax.complex(jnp.minimum(a_re.astype(f32), -1e-4), a_im.astype(f32))
    dt = jnp.exp(log_dt.astype(f32))[:, None]
    a_bar = jnp.exp(lam * dt)
    b = lax.complex(b_re.astype(f32), b_im.astype(f32))
    b_bar = ((a_bar - 1.0) / lam)[..., None] * b
    bu = lax.complex(jnp.einsum('gph,blgh->blgp', jnp.real(b_bar), uf),
                     jnp.einsum('gph,blgh->blgp', jnp.imag(b_bar), uf))
    a_seq = jnp.broadcast_to(a_bar, bu.shape)

    def combine(left, right):
        a_l, s_l = left
        a_r, s_r = right
        return a_r * a_l, a_r * s_l + s_r

    _, states = lax.associative_scan(combine, (a_seq, bu), axis=1)
    y = (jnp.einsum('ghp,blgp->blgh', c_re.astype(f32), jnp.real(states))
         - jnp.einsum('ghp,blgp->blgh', c_im.astype(f32), jnp.imag(states))
         + d_skip.astype(f32) * uf)
    y = jax.nn.gelu(y)
    y = y * jax.nn.sigmoid(jnp.einsum('blgh,ghk->blgk', y, w_glu.astype(f32)))
    return y.reshape(bsz, L, S5_WIDTH).astype(u.dtype)

def short_conv_mixer(x_in, gate_b, gate_c, conv_w):
    L = x_in.shape[1]
    v = gate_c * x_in
    vp = jnp.pad(v, ((0, 0), (CONV_K - 1, 0), (0, 0)))
    conv = vp[:, 0:L] * conv_w[0]
    for tap in range(1, CONV_K):
        conv = conv + vp[:, tap:tap + L] * conv_w[tap]
    return gate_b * conv

def forgetting_attention(q, k, v, f_logit, b_f):
    bsz, L, _ = q.shape
    q = q.reshape(bsz, L, ATTN_HEADS, HEAD_DIM)
    k = k.reshape(bsz, L, ATTN_HEADS, HEAD_DIM)
    v = v.reshape(bsz, L, ATTN_HEADS, HEAD_DIM)
    log_f = jax.nn.log_sigmoid((f_logit + b_f).astype(jnp.float32))
    cum = jnp.cumsum(log_f, axis=1).transpose(0, 2, 1)
    scale = HEAD_DIM ** -0.5
    outs = []
    for blk in range(L // Q_BLOCK):
        q0 = blk * Q_BLOCK
        kend = q0 + Q_BLOCK
        s = jnp.einsum('bqhd,bkhd->bhqk', q[:, q0:kend], k[:, :kend]).astype(jnp.float32) * scale
        s = s + cum[:, :, q0:kend, None] - cum[:, :, None, :kend]
        q_pos = q0 + jnp.arange(Q_BLOCK)
        k_pos = jnp.arange(kend)
        s = jnp.where(k_pos[None, :] <= q_pos[:, None], s, NEG_INF)
        p = jax.nn.softmax(s, axis=-1)
        outs.append(jnp.einsum('bhqk,bkhd->bqhd', p.astype(v.dtype), v[:, :kend]))
    return jnp.concatenate(outs, axis=1).reshape(bsz, L, ATTN_WIDTH)

def hybrid_layer(x, g_pre_mix, w_in, b_gate, a_re, a_im, log_dt, b_re, b_im, c_re, c_im,
                 d_skip, w_glu, conv_w, b_f, w_branch, w_out, g_post_mix, g_pre_mlp,
                 w_ff1, w_ff2, g_post_mlp):
    bsz, L, _ = x.shape
    h = rmsnorm(x, g_pre_mix)
    proj = jnp.einsum('bld,dn->bln', h, w_in)
    widths = [S5_WIDTH, CONV_WIDTH, CONV_WIDTH, CONV_WIDTH, ATTN_WIDTH, ATTN_WIDTH,
              ATTN_WIDTH, ATTN_HEADS, N_BRANCH * D_MODEL]
    offsets = np.cumsum(widths)[:-1].tolist()
    (u_s5, x_conv, b_conv, c_conv, q, k, v, f_logit, gate_logits) = jnp.split(proj, offsets, axis=-1)

    y_a = s5_mixer(u_s5, a_re, a_im, log_dt, b_re, b_im, c_re, c_im, d_skip, w_glu)
    y_b = short_conv_mixer(x_conv, b_conv, c_conv, conv_w)
    y_c = forgetting_attention(q, k, v, f_logit, b_f)

    gates = jax.nn.sigmoid((gate_logits + b_gate).astype(jnp.float32)).astype(x.dtype)
    gates = gates.reshape(bsz, L, N_BRANCH, D_MODEL)
    wa = w_branch[:S5_WIDTH]
    wb = w_branch[S5_WIDTH:S5_WIDTH + CONV_WIDTH]
    wc = w_branch[S5_WIDTH + CONV_WIDTH:]
    merged = (gates[:, :, 0] * jnp.einsum('blc,cd->bld', y_a, wa)
              + gates[:, :, 1] * jnp.einsum('blc,cd->bld', y_b, wb)
              + gates[:, :, 2] * jnp.einsum('blc,cd->bld', y_c, wc))
    mix = jnp.einsum('bld,de->ble', merged, w_out)
    x = x + rmsnorm(mix, g_post_mix)

    h = rmsnorm(x, g_pre_mlp)
    ff = jnp.einsum('blf,fd->bld', jnp.square(jax.nn.relu(jnp.einsum('bld,df->blf', h, w_ff1))), w_ff2)
    return x + rmsnorm(ff, g_post_mlp)

def first_inputs(seed: int = 0) -> dict:
    key = jax.random.key(seed)
    ks = jax.random.split(key, 24)
    f32 = jnp.float32
    nrm = lambda k, shape, s: (jax.random.normal(k, shape, f32) * s)
    G, P, H = S5_GROUPS, S5_STATE, S5_GROUP
    x = jax.random.normal(ks[0], (BATCH, SEQ, D_MODEL), f32)
    g_pre_mix = 1.0 + nrm(ks[1], (DEPTH, D_MODEL), 0.05)
    w_in = nrm(ks[2], (DEPTH, D_MODEL, IN_WIDTH), D_MODEL ** -0.5)
    b_gate = nrm(ks[3], (DEPTH, N_BRANCH * D_MODEL), 0.01)
    n_idx = jnp.arange(P, dtype=f32)
    s5_a_re = -0.5 + nrm(ks[4], (DEPTH, G, P), 0.01)
    s5_a_im = math.pi * n_idx + nrm(ks[5], (DEPTH, G, P), 0.01)
    s5_log_dt = jax.random.uniform(ks[6], (DEPTH, G), f32, math.log(1e-3), math.log(1e-1))
    s5_b_re = nrm(ks[7], (DEPTH, G, P, H), (2.0 * H) ** -0.5)
    s5_b_im = nrm(ks[8], (DEPTH, G, P, H), (2.0 * H) ** -0.5)
    s5_c_re = nrm(ks[9], (DEPTH, G, H, P), (2.0 * P) ** -0.5)
    s5_c_im = nrm(ks[10], (DEPTH, G, H, P), (2.0 * P) ** -0.5)
    s5_d = nrm(ks[11], (DEPTH, G, H), 1.0)
    s5_w_glu = nrm(ks[12], (DEPTH, G, H, H), H ** -0.5)
    conv_w = nrm(ks[13], (DEPTH, CONV_K, CONV_WIDTH), CONV_K ** -0.5)
    fox_b_f = jnp.linspace(1.0, 6.0, ATTN_HEADS, dtype=f32)[None, :] + nrm(ks[14], (DEPTH, ATTN_HEADS), 0.1)
    w_branch = nrm(ks[15], (DEPTH, MIX_WIDTH, D_MODEL), S5_WIDTH ** -0.5)
    w_out = nrm(ks[16], (DEPTH, D_MODEL, D_MODEL), D_MODEL ** -0.5)
    g_post_mix = 1.0 + nrm(ks[17], (DEPTH, D_MODEL), 0.05)
    g_pre_mlp = 1.0 + nrm(ks[18], (DEPTH, D_MODEL), 0.05)
    w_ff1 = nrm(ks[19], (DEPTH, D_MODEL, D_FF), D_MODEL ** -0.5)
    w_ff2 = nrm(ks[20], (DEPTH, D_FF, D_MODEL), D_FF ** -0.5)
    g_post_mlp = 1.0 + nrm(ks[21], (DEPTH, D_MODEL), 0.05)
    return {"x": x, "g_pre_mix": g_pre_mix, "w_in": w_in, "b_gate": b_gate,
            "s5_a_re": s5_a_re, "s5_a_im": s5_a_im, "s5_log_dt": s5_log_dt,
            "s5_b_re": s5_b_re, "s5_b_im": s5_b_im, "s5_c_re": s5_c_re, "s5_c_im": s5_c_im,
            "s5_d": s5_d, "s5_w_glu": s5_w_glu, "conv_w": conv_w, "fox_b_f": fox_b_f,
            "w_branch": w_branch, "w_out": w_out, "g_post_mix": g_post_mix,
            "g_pre_mlp": g_pre_mlp, "w_ff1": w_ff1, "w_ff2": w_ff2, "g_post_mlp": g_post_mlp}

def first_block(x, g_pre_mix, w_in, b_gate, s5_a_re, s5_a_im, s5_log_dt, s5_b_re, s5_b_im,
              s5_c_re, s5_c_im, s5_d, s5_w_glu, conv_w, fox_b_f, w_branch, w_out,
              g_post_mix, g_pre_mlp, w_ff1, w_ff2, g_post_mlp):
    for layer in range(DEPTH):
        x = hybrid_layer(x, g_pre_mix[layer], w_in[layer], b_gate[layer],
                         s5_a_re[layer], s5_a_im[layer], s5_log_dt[layer],
                         s5_b_re[layer], s5_b_im[layer], s5_c_re[layer], s5_c_im[layer],
                         s5_d[layer], s5_w_glu[layer], conv_w[layer], fox_b_f[layer],
                         w_branch[layer], w_out[layer], g_post_mix[layer], g_pre_mlp[layer],
                         w_ff1[layer], w_ff2[layer], g_post_mlp[layer])
    return x


N_HEADS = 4
MIX_W = N_HEADS * HEAD_DIM
N_BRANCH_2 = 4
ATT_LEFT_CHUNKS = 8
ATT_BAND = (ATT_LEFT_CHUNKS + 1) * CHUNK
REL_MAX = 256
REL_SIZE = REL_MAX + CHUNK
NEG_BIG = -1e30
HG_BLOCK = 16
LOG_FLOOR = 1e-30
GM_BLOCK = 128
GM_GROUPS = N_HEADS
GM_GROUP_W = MIX_W // GM_GROUPS
CONV_W = 4
LRU_C = 8.0
FFN_HIDDEN = ((8 * D_MODEL // 3 + 255) // 256) * 256
IN_SIZES = [MIX_W] * 11 + [N_BRANCH_2 * D_MODEL]
IN_COLS = sum(IN_SIZES)


def rms_norm(x, g):
    xf = x.astype(jnp.float32)
    y = xf * lax.rsqrt(jnp.mean(xf * xf, axis=-1, keepdims=True) + EPS)
    return (y * g.astype(jnp.float32)).astype(x.dtype)

def split_in(z):
    idx = np.cumsum(IN_SIZES)[:-1].tolist()
    return jnp.split(z, idx, axis=-1)

def chunk_band_attention(q, k, v, rel_bias):
    B, S, _ = q.shape
    nc = S // CHUNK
    L = ATT_LEFT_CHUNKS
    pad = L * CHUNK
    qc = q.reshape(B, nc, CHUNK, N_HEADS, HEAD_DIM)

    def band(t):
        tp = jnp.pad(t, ((0, 0), (pad, 0), (0, 0))).reshape(B, nc + L, CHUNK, N_HEADS, HEAD_DIM)
        return jnp.concatenate([tp[:, j:j + nc] for j in range(L + 1)], axis=2)

    kb, vb = band(k), band(v)
    s = jnp.einsum('bcqhd,bckhd->bchqk', qc, kb).astype(jnp.float32) * (HEAD_DIM ** -0.5)
    dist = pad + jnp.arange(CHUNK)[:, None] - jnp.arange(ATT_BAND)[None, :]
    idx = jnp.clip(dist, -(CHUNK - 1), REL_MAX) + (CHUNK - 1)
    bias = rel_bias.astype(jnp.float32)[:, idx]
    key_pos = jnp.arange(nc)[:, None] * CHUNK + jnp.arange(ATT_BAND)[None, :] - pad
    valid = key_pos >= 0
    s = jnp.where(valid[None, :, None, None, :], s + bias[None, None], NEG_BIG)
    p = jax.nn.softmax(s, axis=-1).astype(v.dtype)
    o = jnp.einsum('bchqk,bckhd->bcqhd', p, vb)
    return o.reshape(B, S, MIX_W)

def hgrn2(q, fz, i, g, lb, norm_g):
    B, S, _ = q.shape
    n = S // HG_BLOCK
    f32 = jnp.float32
    fz = fz.astype(f32)
    lb = lb.astype(f32)
    qf = jax.nn.silu(q.astype(f32))
    f = lb + (1.0 - lb) * jax.nn.sigmoid(fz)
    log_f = jnp.log(jnp.maximum(f, LOG_FLOOR))
    kf = (1.0 - lb) * jax.nn.sigmoid(-fz)
    shp = (B, n, HG_BLOCK, N_HEADS, HEAD_DIM)
    qf, kf, log_f = qf.reshape(shp), kf.reshape(shp), log_f.reshape(shp)
    vf = i.astype(f32).reshape(shp)
    b = jnp.cumsum(log_f, axis=2)
    causal = jnp.tril(jnp.ones((HG_BLOCK, HG_BLOCK), bool))[:, :, None, None]
    diff = b[:, :, :, None] - b[:, :, None, :]
    decay = jnp.where(causal, jnp.exp(jnp.where(causal, diff, 0.0)), 0.0)
    scores = jnp.einsum('bntshk,bnthk,bnshk->bnhts', decay, qf, kf)
    intra = jnp.einsum('bnhts,bnshv->bnthv', scores, vf)
    b_last = b[:, :, -1:]
    qd = qf * jnp.exp(b)
    kd = kf * jnp.exp(b_last - b)
    dec = jnp.exp(b_last[:, :, 0])

    def step(state, xs):
        qd_c, kd_c, v_c, dec_c = xs
        inter_c = jnp.einsum('bthk,bhkv->bthv', qd_c, state)
        state = dec_c[..., None] * state + jnp.einsum('bshk,bshv->bhkv', kd_c, v_c)
        return state, inter_c

    s0 = jnp.zeros((B, N_HEADS, HEAD_DIM, HEAD_DIM), f32)
    xs = (jnp.moveaxis(qd, 1, 0), jnp.moveaxis(kd, 1, 0), jnp.moveaxis(vf, 1, 0), jnp.moveaxis(dec, 1, 0))
    _, inter = lax.scan(step, s0, xs)
    o = (intra + jnp.moveaxis(inter, 0, 1)).reshape(B, S, N_HEADS, HEAD_DIM)
    o = o * lax.rsqrt(jnp.mean(o * o, axis=-1, keepdims=True) + EPS)
    o = o * norm_g.astype(f32).reshape(N_HEADS, HEAD_DIM)
    o = o.reshape(B, S, MIX_W) * jax.nn.silu(g.astype(f32))
    return o.astype(q.dtype)

def spatial_gating(u, v, norm_g, ws, bs):
    B, S, _ = u.shape
    n = S // GM_BLOCK
    vn = rms_norm(v, norm_g).reshape(B, n, GM_BLOCK, GM_GROUPS, GM_GROUP_W)
    w = ws * jnp.tril(jnp.ones((GM_BLOCK, GM_BLOCK), ws.dtype))
    mixed = jnp.einsum('gpq,bnqgc->bnpgc', w, vn) + bs.T[:, :, None]
    return u * mixed.reshape(B, S, MIX_W)

def rg_lru_branch(xin, gate, conv_w, conv_b, wa, ba, wx, bx, lam):
    B, S, _ = xin.shape
    f32 = jnp.float32
    xp = jnp.pad(xin, ((0, 0), (CONV_W - 1, 0), (0, 0)))
    xc = conv_b + xp[:, 0:S] * conv_w[0]
    for j in range(1, CONV_W):
        xc = xc + xp[:, j:j + S] * conv_w[j]
    xh = xc.reshape(B, S, N_HEADS, HEAD_DIM)
    r = jax.nn.sigmoid(jnp.einsum('bshi,hij->bshj', xh, wa).reshape(B, S, MIX_W) + ba)
    ig = jax.nn.sigmoid(jnp.einsum('bshi,hij->bshj', xh, wx).reshape(B, S, MIX_W) + bx)
    log_a = -LRU_C * r.astype(f32) * jax.nn.softplus(-lam.astype(f32))
    a = jnp.exp(log_a)
    mult = jnp.sqrt(jnp.maximum(-jnp.expm1(2.0 * log_a), 0.0))
    mult = jnp.where(jnp.arange(S)[None, :, None] == 0, 1.0, mult)
    bt = mult * (ig * xc).astype(f32)

    def combine(left, right):
        a1, b1 = left
        a2, b2 = right
        return a1 * a2, a2 * b1 + b2

    _, h = lax.associative_scan(combine, (a, bt), axis=1)
    return (h * jax.nn.gelu(gate.astype(f32))).astype(xin.dtype)

def hybrid_mixer(h, w_in, rel_bias, lb, hg_norm_g, gm_norm_g, gm_ws, gm_bs,
                 conv_w, conv_b, wa, ba, wx, bx, lam, w_branch, w_out):
    B, S, _ = h.shape
    z = h @ w_in
    aq, ak, av, bq, bf, bi, bg, cu, cv, dx, dg, gates = split_in(z)
    o_a = chunk_band_attention(aq, ak, av, rel_bias)
    o_b = hgrn2(bq, bf, bi, bg, lb, hg_norm_g)
    o_c = spatial_gating(jax.nn.gelu(cu), jax.nn.gelu(cv), gm_norm_g, gm_ws, gm_bs)
    o_d = rg_lru_branch(dx, dg, conv_w, conv_b, wa, ba, wx, bx, lam)
    outs = jnp.stack([o_a, o_b, o_c, o_d], axis=2)
    proj = jnp.einsum('bsnw,nwd->bsnd', outs, w_branch)
    g = jax.nn.sigmoid(gates.reshape(B, S, N_BRANCH_2, D_MODEL))
    merged = jnp.sum(g * proj, axis=2)
    return merged @ w_out

def swiglu(h, w1, w2):
    gt, up = jnp.split(h @ w1, 2, axis=-1)
    return (jax.nn.silu(gt) * up) @ w2

def second_inputs(seed: int = 0) -> dict:
    key = jax.random.key(seed)
    ks = jax.random.split(key, 24)
    f32 = jnp.float32

    def nrm(k, shape, scale):
        return jax.random.normal(k, shape, f32) * scale

    u = jax.random.uniform(ks[18], (DEPTH, MIX_W), f32, 0.9, 0.999)
    sa = u ** (1.0 / LRU_C)
    return {
        'x': nrm(ks[0], (BATCH, SEQ, D_MODEL), 1.0),
        'norm_mix_pre': 1.0 + nrm(ks[1], (DEPTH, D_MODEL), 0.02),
        'norm_mix_post': 1.0 + nrm(ks[2], (DEPTH, D_MODEL), 0.02),
        'norm_ffn_pre': 1.0 + nrm(ks[3], (DEPTH, D_MODEL), 0.02),
        'norm_ffn_post': 1.0 + nrm(ks[4], (DEPTH, D_MODEL), 0.02),
        'w_in': nrm(ks[5], (DEPTH, D_MODEL, IN_COLS), D_MODEL ** -0.5),
        'attn_rel_bias': nrm(ks[6], (DEPTH, N_HEADS, REL_SIZE), 0.1),
        'hgrn_lb_logits': nrm(ks[7], (DEPTH, MIX_W), 1.0),
        'hgrn_norm_g': 1.0 + nrm(ks[8], (DEPTH, MIX_W), 0.02),
        'gmlp_norm_g': 1.0 + nrm(ks[9], (DEPTH, MIX_W), 0.02),
        'gmlp_ws': nrm(ks[10], (DEPTH, GM_GROUPS, GM_BLOCK, GM_BLOCK), 0.5 * GM_BLOCK ** -0.5),
        'gmlp_bs': 1.0 + nrm(ks[11], (DEPTH, GM_GROUPS, GM_BLOCK), 0.01),
        'lru_conv_w': nrm(ks[12], (DEPTH, CONV_W, MIX_W), CONV_W ** -0.5),
        'lru_conv_b': nrm(ks[13], (DEPTH, MIX_W), 0.01),
        'lru_wa': nrm(ks[14], (DEPTH, N_HEADS, HEAD_DIM, HEAD_DIM), HEAD_DIM ** -0.5),
        'lru_ba': nrm(ks[15], (DEPTH, MIX_W), 0.01),
        'lru_wx': nrm(ks[16], (DEPTH, N_HEADS, HEAD_DIM, HEAD_DIM), HEAD_DIM ** -0.5),
        'lru_bx': nrm(ks[17], (DEPTH, MIX_W), 0.01),
        'lru_lambda': jnp.log(sa) - jnp.log1p(-sa),
        'w_branch': nrm(ks[19], (DEPTH, N_BRANCH_2, MIX_W, D_MODEL), MIX_W ** -0.5),
        'w_out': nrm(ks[20], (DEPTH, D_MODEL, D_MODEL), D_MODEL ** -0.5),
        'w_ffn_in': nrm(ks[21], (DEPTH, D_MODEL, 2 * FFN_HIDDEN), D_MODEL ** -0.5),
        'w_ffn_out': nrm(ks[22], (DEPTH, FFN_HIDDEN, D_MODEL), FFN_HIDDEN ** -0.5),
    }

def second_block(x, norm_mix_pre, norm_mix_post, norm_ffn_pre, norm_ffn_post, w_in,
              attn_rel_bias, hgrn_lb_logits, hgrn_norm_g, gmlp_norm_g, gmlp_ws, gmlp_bs,
              lru_conv_w, lru_conv_b, lru_wa, lru_ba, lru_wx, lru_bx, lru_lambda,
              w_branch, w_out, w_ffn_in, w_ffn_out):
    p = jax.nn.softmax(hgrn_lb_logits.astype(jnp.float32), axis=0)
    lbs = jnp.cumsum(p, axis=0) - p[0]
    for l in range(DEPTH):
        h = rms_norm(x, norm_mix_pre[l])
        y = hybrid_mixer(h, w_in[l], attn_rel_bias[l], lbs[l], hgrn_norm_g[l], gmlp_norm_g[l],
                         gmlp_ws[l], gmlp_bs[l], lru_conv_w[l], lru_conv_b[l], lru_wa[l],
                         lru_ba[l], lru_wx[l], lru_bx[l], lru_lambda[l], w_branch[l], w_out[l])
        x = x + rms_norm(y, norm_mix_post[l])
        h = rms_norm(x, norm_ffn_pre[l])
        x = x + rms_norm(swiglu(h, w_ffn_in[l], w_ffn_out[l]), norm_ffn_post[l])
    return x


_first_inputs = second_inputs


def second_inputs(seed=0):
    import zlib

    import numpy as np

    out = dict(_first_inputs(seed))
    spreads = {}
    factors = {'norm_mix_post': 3.39,
     'norm_ffn_pre': 3.617,
     'norm_ffn_post': 4.975,
     'attn_rel_bias': 7.787,
     'hgrn_norm_g': 6.148,
     'gmlp_norm_g': 8.0,
     'gmlp_bs': 8.0,
     'lru_ba': 8.0,
     'lru_bx': 8.0}
    for name, (base, spread) in spreads.items():
        noise = np.random.default_rng([zlib.crc32(name.encode()), seed]).standard_normal(out[name].shape)
        drawn = base * np.exp(spread * noise) if base else spread * noise
        out[name] = __import__('jax').numpy.asarray(drawn.astype(out[name].dtype))
    for name, factor in factors.items():
        out[name] = (out[name] * factor).astype(out[name].dtype)
    return out


_narrow_inputs = second_inputs


def second_inputs(seed=0):

    out = dict(_narrow_inputs(seed))
    wider = {'norm_ffn_post': 3.98,
     'attn_rel_bias': 4.6,
     'hgrn_norm_g': 4.87,
     'gmlp_norm_g': 9.14,
     'gmlp_bs': 7.1,
     'lru_conv_b': 9.61,
     'lru_ba': 12.0,
     'lru_bx': 12.0}
    for name, times in wider.items():
        mean = out[name].mean()
        out[name] = (mean + times * (out[name] - mean)).astype(out[name].dtype)
    return out


def setup_inputs(seed=0):
    out = dict(first_inputs(seed))
    for name, value in second_inputs(seed + 1).items():
        if name != "x":
            out[name + "_2"] = value
    return out


def reference(
    x, g_pre_mix, w_in, b_gate, s5_a_re, s5_a_im, s5_log_dt, s5_b_re, s5_b_im, s5_c_re, s5_c_im,
    s5_d, s5_w_glu, conv_w, fox_b_f, w_branch, w_out, g_post_mix, g_pre_mlp, w_ff1, w_ff2,
    g_post_mlp, norm_mix_pre_2, norm_mix_post_2, norm_ffn_pre_2, norm_ffn_post_2, w_in_2,
    attn_rel_bias_2, hgrn_lb_logits_2, hgrn_norm_g_2, gmlp_norm_g_2, gmlp_ws_2, gmlp_bs_2,
    lru_conv_w_2, lru_conv_b_2, lru_wa_2, lru_ba_2, lru_wx_2, lru_bx_2, lru_lambda_2,
    w_branch_2, w_out_2, w_ffn_in_2, w_ffn_out_2,
):
    x = first_block(
        x, g_pre_mix, w_in, b_gate, s5_a_re, s5_a_im, s5_log_dt, s5_b_re, s5_b_im, s5_c_re,
        s5_c_im, s5_d, s5_w_glu, conv_w, fox_b_f, w_branch, w_out, g_post_mix, g_pre_mlp, w_ff1,
        w_ff2, g_post_mlp,
    )
    return second_block(
        x, norm_mix_pre_2, norm_mix_post_2, norm_ffn_pre_2, norm_ffn_post_2, w_in_2,
        attn_rel_bias_2, hgrn_lb_logits_2, hgrn_norm_g_2, gmlp_norm_g_2, gmlp_ws_2, gmlp_bs_2,
        lru_conv_w_2, lru_conv_b_2, lru_wa_2, lru_ba_2, lru_wx_2, lru_bx_2, lru_lambda_2,
        w_branch_2, w_out_2, w_ffn_in_2, w_ffn_out_2,
    )


_drawn_inputs = setup_inputs


def setup_inputs(seed=0):
    import zlib

    import numpy as np

    out = dict(_drawn_inputs(seed))
    spreads = {}
    factors = {'b_gate': 8.0,
     's5_a_re': 8.0,
     's5_b_re': 3.307,
     's5_b_im': 3.329,
     's5_c_re': 3.293,
     's5_c_im': 3.295}
    for name, (base, spread) in spreads.items():
        noise = np.random.default_rng([zlib.crc32(name.encode()), seed]).standard_normal(out[name].shape)
        drawn = base * np.exp(spread * noise) if base else spread * noise
        out[name] = __import__('jax').numpy.asarray(drawn.astype(out[name].dtype))
    for name, factor in factors.items():
        out[name] = (out[name] * factor).astype(out[name].dtype)
    return out
```

```python
import math
from contextlib import ExitStack, contextmanager

import numpy as np
import concourse.bass as bass
from concourse import mybir
from concourse.alu_op_type import AluOpType as ALU

P = 128
L = 1024
D = 1024
KT = D // P
HALF = 512
HD = 64
EPS = 1e-6
S5_G, S5_P, S5_H = 32, 64, 16
PAIRS = S5_G // 2
T = 8
CH = L // T
FOX_HEADS = 8
FF1 = 4096
BAND_HEADS = 4
LEFT = 512
BAND = LEFT + P
HID2 = 2816
LOG_FLOOR = 1e-30
LRU_C = 8.0
LEVELS = 7

F32 = mybir.dt.float32
F32R = mybir.dt.float32r
ACT = mybir.ActivationFunctionType
AX = mybir.AxisListType

U_, X_, B_, C_, Q_, K_, V_, F_, GATE1 = 0, 4, 8, 12, 16, 20, 24, 28, 29
N1 = 53
AQ, AK, AV, BQ, BF, BI, BG, CU, CV, DX, DG, GATE2 = 0, 2, 4, 6, 8, 10, 12, 14, 16, 18, 20, 22
N2 = 54

VEC_NAMES = (("g_pre_mix", 8), ("g_post_mix", 8), ("g_pre_mlp", 8), ("g_post_mlp", 8), ("b_gate", 24),
             ("conv_w", 12), ("a_re", 16), ("a_im", 16), ("log_dt", 16),
             ("norm_mix_pre", 8), ("norm_mix_post", 8), ("norm_ffn_pre", 8), ("norm_ffn_post", 8),
             ("lb", 2), ("hgrn_g", 2), ("gmlp_g", 2), ("lru_cw", 8), ("lru_cb", 2), ("lru_ba", 2),
             ("lru_bx", 2), ("lru_lam", 2), ("b_f", 1))
VEC = {}
for _name, _n in VEC_NAMES:
    VEC[_name] = sum(VEC[m][1] for m in VEC), _n
NVEC = sum(n for _, n in VEC_NAMES)


COUNTERS = []


class Lane:

    def __init__(self, engine, sem, start):
        self.engine, self.sem = engine, sem
        self.n = start
        self.here = self.per = 0
        self.unit = 1
        COUNTERS.append(self)
        engine.sem_inc(sem, start)

    def after(self, *marks):
        for m in marks:
            if m is not None:
                self.engine.wait_ge(m[0], m[1])
        return self.engine

    def then(self, *marks):
        return self.after((self.sem, self.n), *marks)

    def mark(self, instruction):
        instruction.then_inc(self.sem, self.unit)
        self.n = self.n + self.unit
        self.here += self.unit
        return (self.sem, self.n)

    def last(self):
        return (self.sem, self.n)

    def turn_ago(self, mark):
        return (self.sem, mark[1] - self.per)


class Count(Lane):

    def __init__(self, sem, unit=16):
        self.sem, self.unit = sem, unit
        COUNTERS.append(self)
        self.n = self.here = self.per = 0


@contextmanager
def loop(nc, turns, per):
    start = {c: c.n for c in per}
    fixed = {c: c.n for c in COUNTERS if c not in per}
    with nc.Fori(0, turns) as i:
        for c in per:
            c.n, c.here, c.per = start[c] + i * per[c], 0, per[c]
        yield i
        assert all(c.here == per[c] for c in per), [(c.sem.name, c.here) for c in per]
        assert all(c.n is fixed[c] for c in fixed), [c.sem.name for c in fixed if c.n is not fixed[c]]
    for c in per:
        c.n, c.per = start[c] + turns * per[c], 0


def build(nc, t, out):
    COUNTERS.clear()
    with ExitStack() as ctx:
        _build(nc, ctx, t, out)


def _build(nc, ctx, t, out):
    def sb(at, name, shape, dt=F32):
        return at.enter_context(nc.sbuf_tensor(name, shape, dt))

    def sem(name):
        return ctx.enter_context(nc.semaphore(name))

    def scratch(name, shape):
        return nc.dram_tensor(name, shape, F32, kind="Internal").ap()

    proj1, proj2 = scratch("proj1", (N1 + 1, P, L)), scratch("proj2", (N2 + 1, P, L))
    mixed1 = scratch("mixed1", (12, P, L))
    mixed2 = scratch("mixed2", (8, P, L))
    x1, x2, x3 = (scratch(n, (KT, P, L)) for n in ("x1", "x2", "x3"))
    fox_cum = scratch("fox_cum", (FOX_HEADS, L))
    fox_log = scratch("fox_log", (P, L * FOX_HEADS // P))
    s5_u, s5_y = scratch("s5_u", (4 * P, T, CH)), scratch("s5_y", (4 * P, T, CH))

    V = Lane(nc.vector, sem("vector"), 1024)
    A = Lane(nc.scalar, sem("scalar"), 1024)
    G = Lane(nc.gpsimd, sem("gpsimd"), 1024)
    PE = Lane(nc.tensor, sem("tensor"), 1024)
    load = Count(sem("load"))
    store = Count(sem("store"))
    loads = [Count(sem(f"load{n}")) for n in range(2)]
    stores = [Count(sem(f"store{n}")) for n in range(2)]
    SP = nc.sync

    def barrier():
        marks = [x.last() for x in (V, A, G, PE, load, store, *loads, *stores, *pair_read)]
        marks.append((s_mm, used["units"] + 2))
        for e in (nc.vector, nc.scalar, nc.gpsimd, nc.tensor, nc.sync):
            for s, n in marks:
                e.wait_ge(s, n)

    raw = sb(ctx, "w_raw", [P, 2, KT * P])
    whi = sb(ctx, "w_hi", [P, 2, KT * P], F32R)
    wlo = sb(ctx, "w_lo", [P, 2, KT * P], F32R)
    vec = sb(ctx, "vec", [P, NVEC])
    ident = sb(ctx, "ident", [P, P])
    causal = sb(ctx, "causal", [P, P])
    ones = sb(ctx, "ones", [P, P])
    pair = [ctx.enter_context(nc.psum_tensor(f"pair{i}", [P, L], F32)) for i in range(2)]
    wide = ctx.enter_context(nc.psum_tensor("wide", [P, L], F32))
    bank = [ctx.enter_context(nc.psum_tensor(f"bank{i}", [P, HALF], F32)) for i in (6, 7)]
    act_hi = sb(ctx, "act_hi", [P, KT, L], F32R)
    act_lo = sb(ctx, "act_lo", [P, KT, L], F32R)

    def col(name, i):
        at = VEC[name][0]
        return vec[:, at + i:at + i + 1]

    load.mark(SP.dma_start(vec[:], t["vec"]))
    G.mark(G.then().memset(ident[:], 0.0))
    G.mark(G.then().affine_select(out=ident[:], in_=ident[:], compare_op=ALU.not_equal, fill=1.0, base=0,
                                  pattern=[[-1, P]], channel_multiplier=1))
    G.mark(G.then().memset(causal[:], 0.0))
    G.mark(G.then().affine_select(out=causal[:], in_=causal[:], compare_op=ALU.is_ge, fill=-1e30, base=0,
                                  pattern=[[-1, P]], channel_multiplier=1))
    G.mark(G.then().memset(ones[:], 1.0))

    s_raw = [sem("raw0"), sem("raw1")]
    s_whi = sem("whi")
    s_split = sem("split")
    s_mm = sem("mm")
    for s, e in ((s_whi, nc.scalar), (s_split, nc.gpsimd), (s_mm, nc.tensor)):
        e.sem_inc(s, 2)
    used = {"units": 0, "blocks": 0}

    def split_unit(b, slot, fills):
        nc.scalar.wait_ge(s_raw[slot], 16 * fills)
        nc.scalar.wait_ge(s_mm, b + 1)
        nc.scalar.copy(whi[:, slot, :], raw[:, slot, :]).then_inc(s_whi, 1)
        nc.gpsimd.wait_ge(s_whi, b + 3)
        nc.gpsimd.tensor_tensor(wlo[:, slot, :], raw[:, slot, :], whi[:, slot, :].bitcast(F32),
                                ALU.subtract).then_inc(s_split, 1)

    def fetch_unit(b, slot):
        SP.wait_ge(s_split, b + 1)
        SP.dma_start(raw[:, slot, :], t["stream"][b]).then_inc(s_raw[slot], 16)

    for n in range(2):
        fetch_unit(n, n)
    split_unit(0, 0, 1)
    fetch_unit(2, 0)

    def products(i, base, per_turn, n_out, tiles, rhs, evict):
        packed = n_out * tiles == 8 * per_turn
        for o in range(n_out):
            at = (used["blocks"] + o) % 2
            reads, out_pair = pair_read[at], pair[at]
            for k in range(tiles):
                n = o * tiles + k if packed else 8 * o + k
                w, slot = n % 8, (base + n // 8) % 2
                b = i * per_turn + (base + n // 8)
                if w == 0:
                    split_unit(b + 1, 1 - slot, i * (per_turn // 2) + ((base + n // 8 + 1) // 2 + 1))
                    fetch_unit(b + 3, 1 - slot)
                    nc.tensor.wait_ge(s_split, b + 3)
                if k == 0:
                    nc.tensor.wait_ge(reads.sem, reads.n)
                hi, lo = rhs(o, k)
                w_hi, w_lo = (x[:, slot, w * P:(w + 1) * P] for x in (whi, wlo))
                for n_pass, (wt, a) in enumerate(((w_hi, hi), (w_hi, lo), (w_lo, hi))):
                    for h in range(2):
                        last = nc.tensor.matmul(out_pair[:, h * HALF:(h + 1) * HALF], wt, a[:, h * HALF:(h + 1) * HALF],
                                                start=k == 0 and n_pass == 0, stop=k == tiles - 1 and n_pass == 2)
                if w == 7 or (not packed and k == tiles - 1):
                    last.then_inc(s_mm, 1)
                    ready = (s_mm, b + 3)
                elif k == tiles - 1:
                    ready = PE.mark(last)
                if k < tiles - 1:
                    yield

            evict(i, o, out_pair, ready, reads.mark)
            yield

    def stage(turns, per_turn, n_out, tiles, rhs, evict, per=None):
        if turns == 1:
            for _ in products(0, used["units"], per_turn, n_out, tiles, rhs, evict):
                pass
        else:
            assert per_turn % 2 == 0 and n_out % 2 == 0
            per = dict(per or {})
            per.update({c: n_out // 2 for c in pair_read})
            with loop(nc, turns, per) as i:
                for _ in products(i, used["units"], per_turn, n_out, tiles, rhs, evict):
                    pass
        used["units"] += turns * per_turn
        used["blocks"] += turns * n_out

    pair_read = [Count(sem(f"pair_read{n}"), 1) for n in range(2)]
    for c in pair_read:
        nc.vector.sem_inc(c.sem, 1)
        c.n = 1

    def act_rhs(o, k):
        return act_hi[:, k, :], act_lo[:, k, :]

    def split_act(src, hi, lo, mark):
        a = A.mark(A.after(mark).copy(hi, src))
        return V.mark(V.after(a).tensor_tensor(lo, src, hi.bitcast(F32), ALU.subtract))

    def sum_rows(psum, ones_t, tiles, sq, mark):
        done = []
        for n, x in enumerate(tiles):
            a = A.mark(A.after(mark, done[n - 2] if n > 1 else None).activation(sq[:, n % 2, :], x, ACT.Square))
            PE.after(a)
            for h in range(2):
                last = nc.tensor.matmul(psum[:, h * HALF:(h + 1) * HALF], ones_t, sq[:, n % 2, h * HALF:(h + 1) * HALF],
                                        start=n == 0, stop=n == len(tiles) - 1)
            done.append(PE.mark(last))
        return done[-1]

    def inv_sqrt(rstd, psum, scale, mark):
        v = V.mark(V.after(mark).tensor_scalar(rstd, psum, scale, EPS, ALU.mult, ALU.add))
        a = A.mark(A.after(v).activation(rstd, rstd, ACT.Sqrt))
        return V.mark(V.after(a).reciprocal(rstd, rstd))

    def rms_scale(tiles, sq, rstd, scale, mark):
        return inv_sqrt(rstd[:], wide[:], scale, sum_rows(wide, ones[:], tiles, sq, mark))

    def norm_in(x_dram, gain, name):
        barrier()
        with ExitStack() as at:
            x, sq, rstd = sb(at, name + "x", [P, KT, L]), sb(at, name + "sq", [P, 2, L]), sb(at, name + "r", [P, L])
            arrived = load.mark(SP.dma_start(x[:], x_dram.rearrange("k p n -> p k n")))
            r = rms_scale([x[:, k, :] for k in range(KT)], sq, rstd, 1.0 / D, arrived)
            for k in range(KT):
                v = V.mark(V.after(r).scalar_tensor_tensor(x[:, k, :], x[:, k, :], col(gain, k), rstd[:],
                                                           ALU.mult, ALU.mult))
                split_act(x[:, k, :], act_hi[:, k, :], act_lo[:, k, :], v)
            barrier()

    def norm_out(y, x_dram, gain, out_dram, name):
        barrier()
        with ExitStack() as at:
            x, sq, rstd = (sb(at, name + n, s) for n, s in (("ox", [P, 2, L]), ("os", [P, 2, L]), ("or", [P, L])))
            r = rms_scale([y[:, k, :] for k in range(KT)], sq, rstd, 1.0 / D, None)
            for k in range(KT):
                s = k % 2
                SP.wait_ge(stores[s].sem, stores[s].n)
                arrived = loads[s].mark(SP.dma_start(x[:, s, :], x_dram[k]))
                v = V.mark(V.after(r).scalar_tensor_tensor(y[:, k, :], y[:, k, :], col(gain, k), rstd[:],
                                                           ALU.mult, ALU.mult))
                g = G.mark(G.after(v, arrived).tensor_tensor(x[:, s, :], x[:, s, :], y[:, k, :], ALU.add))
                SP.wait_ge(*g)
                stores[s].mark(SP.dma_start(out_dram[k], x[:, s, :]))
            barrier()

    def to_dram(dst, row, buf, gate=None):
        def evict(i, o, psum, ready, read):
            slot = o % 2
            stored = stores[slot].last()
            if gate is None:
                done = read(V.after(ready, stored).tensor_copy(buf[:, slot, :], psum[:]))
            else:
                bias = vec[:, bass.ds(i * 2 + (VEC[gate][0] + o), 1)] if gate else 0.0
                done = read(A.after(ready, stored).activation(buf[:, slot, :], psum[:], ACT.Sigmoid, bias=bias))
            SP.wait_ge(*done)
            stores[slot].mark(SP.dma_start(dst[i * 2 + (row + o)], buf[:, slot, :]))
        return evict

    def log1p(x, tmp, mark):
        z, z2 = tmp
        V.mark(V.after(mark).tensor_scalar_add(z, x, 2.0))
        V.mark(V.then().reciprocal(z, z))
        V.mark(V.then().tensor_tensor(z, z, x, ALU.mult))
        V.mark(V.then().tensor_tensor(z2, z, z, ALU.mult))
        V.mark(V.then().memset(x, 2.0 / 17))
        for n in range(15, 0, -2):
            V.mark(V.then().tensor_tensor(x, x, z2, ALU.mult))
            V.mark(V.then().tensor_scalar_add(x, x, 2.0 / n))
        return V.mark(V.then().tensor_tensor(x, x, z, ALU.mult))

    def transposes(dst, src, n, width, src_mark, rows=P, free=None):
        done = free
        for j0 in range(0, n, 4):
            m = min(4, n - j0)
            PE.after(src_mark, done)
            for j in range(m):
                dst_j = bank[0][:, j * width:(j + 1) * width]
                if rows == P:
                    last = nc.tensor.transpose(dst_j, src(j0 + j), ident[:])
                else:
                    last = nc.tensor.matmul(dst_j, src(j0 + j), ident[0:rows, 0:rows], start=True, stop=True)
            ready = PE.mark(last)
            done = A.mark(A.after(ready).copy(dst[:, j0:j0 + m, :], bank[0][:, 0:m * width]
                                              .rearrange("p (j n) -> p j n", j=m)))
        return done

    def short_conv():
        barrier()
        with ExitStack() as at:
            xin, gb, gc, y = (sb(at, "cv" + n, [P, 2, L]) for n in "xbcy")
            with loop(nc, 2, {V: 10, loads[0]: 48, loads[1]: 48, stores[0]: 16, stores[1]: 16}) as i:
                for s in range(2):
                    SP.wait_ge(*V.turn_ago((V.sem, V.n + 5)))
                    for buf, row in ((xin, X_), (gb, B_), (gc, C_)):
                        arrived = loads[s].mark(SP.dma_start(buf[:, s, :], proj1[i * 2 + (row + s)]))
                    x, o = xin[:, s, :], y[:, s, :]

                    def w(tap):
                        return vec[:, bass.ds(i * 2 + (VEC["conv_w"][0] + tap * 4 + s), 1)]

                    V.mark(V.after(arrived).tensor_tensor(x, gc[:, s, :], x, ALU.mult))
                    V.mark(V.then(stores[s].last()).tensor_scalar(o, x, w(2), None, ALU.mult))
                    for back in (1, 2):
                        V.mark(V.then().scalar_tensor_tensor(o[:, back:], x[:, :L - back], w(2 - back), o[:, back:],
                                                             ALU.mult, ALU.add))
                    v = V.mark(V.then().tensor_tensor(o, o, gb[:, s, :], ALU.mult))
                    SP.wait_ge(*v)
                    stores[s].mark(SP.dma_start(mixed1[i * 2 + (4 + s)], o))
            barrier()

    def attention(heads, tiles, src, rows, mixed, row0, head_bias, add_bias, name, per):
        barrier()
        halves = src.rearrange("b (h p) n -> (b h) p n", h=2)
        out_h = mixed.rearrange("b (h p) n -> (b h) p n", h=2)
        with ExitStack() as at:
            q, k, v = (sb(at, name + n, [HD, L]) for n in "qkv")
            vt = sb(at, name + "vt", [P, L // P, HD])
            s = sb(at, name + "s", [P, 2, L])
            pt = sb(at, name + "pt", [P, 2, L])
            o = sb(at, name + "o", [HD, L])
            st = sb(at, name + "st", [P, 2, 4])
            bias = head_bias(at)
            with loop(nc, heads, per) as i:
                for m in (A, V, PE):
                    SP.wait_ge(*m.last())
                for buf, row in ((q, rows[0]), (k, rows[1]), (v, rows[2])):
                    arrived = load.mark(SP.dma_start(buf[:], halves[i + 2 * row]))
                arrived = bias[1](i) or arrived
                arrived = load.last()
                v_ready = copied = transposes(vt, lambda j: v[:, j * P:(j + 1) * P], L // P, HD, arrived, rows=HD)
                stored = stores[0].last()
                pv_done, st_read, o_read = [], None, None
                pend = []

                def second(n, q0, k0, k1, e):
                    nonlocal o_read, copied
                    sl, nk = n % 2, (k1 - k0) // P
                    copied = transposes(pt[:, sl, :].rearrange("p (j n) -> p j n", n=P),
                                        lambda j: s[:, sl, j * P:(j + 1) * P], nk, P, e, free=copied)
                    PE.after(copied, o_read)
                    for j in range(nk):
                        last = nc.tensor.matmul(bank[1][0:HD, 0:P], vt[:, k0 // P + j, :], pt[:, sl, j * P:(j + 1) * P],
                                                start=j == 0, stop=j == nk - 1)
                    pv = PE.mark(last)
                    pv_done.append(pv)
                    o_read = V.mark(V.after(pv, stored).tensor_copy(o[:, q0:q0 + P], bank[1][0:HD, 0:P]))

                for n, (q0, k0, k1) in enumerate(tiles):
                    w, sl = k1 - k0, n % 2
                    PE.after(arrived, v_ready, st_read)
                    for c in range(0, w, HALF):
                        e = min(w, c + HALF)
                        last = nc.tensor.matmul(wide[:, c:e], q[:, q0:q0 + P], k[:, k0 + c:k0 + e], start=True, stop=True)
                    ready = PE.mark(last)
                    sc = s[:, sl, 0:w]
                    V.after(ready, arrived, pv_done[n - 2] if n > 1 else None)
                    st_read = add_bias(sc, wide[:, 0:w], bias[0], q0, k0, k1)
                    V.mark(V.then().reduce_max(st[:, sl, 0:1], sc, AX.X))
                    x = V.mark(V.then().tensor_scalar(st[:, sl, 1:2], st[:, sl, 0:1], -1.0, None, ALU.mult))
                    x = A.mark(A.after(x).activation(sc, sc, ACT.Exp, bias=st[:, sl, 1:2], accum_out=st[:, sl, 2:3]))
                    V.mark(V.after(x).reciprocal(st[:, sl, 3:4], st[:, sl, 2:3]))
                    x = V.mark(V.then().tensor_scalar(sc, sc, st[:, sl, 3:4], None, ALU.mult))
                    if pend:
                        second(*pend.pop())
                    pend.append((n, q0, k0, k1, x))
                second(*pend.pop())
                SP.wait_ge(*o_read)
                stores[0].mark(SP.dma_start(out_h[i + 2 * row0], o[:]))
            barrier()

    def fox():
        barrier()
        n_log = L * FOX_HEADS // P
        with ExitStack() as at:
            f, e, z, z2 = (sb(at, "fx" + n, [P, n_log]) for n in ("f", "e", "z", "y"))
            cum, one = sb(at, "fx_cum", [FOX_HEADS, L]), sb(at, "fx_one", [FOX_HEADS, L])
            a = load.mark(SP.dma_start(f[:], proj1[F_, 0:FOX_HEADS, :].rearrange("h (a n) -> (h a) n", a=16)))
            v = V.mark(V.after(a).tensor_scalar(f[:], f[:], col("b_f", 0), None, ALU.add))
            a = A.mark(A.after(v).activation(e[:], f[:], ACT.Abs))
            a = A.mark(A.then().activation(e[:], e[:], ACT.Exp, scale=-1.0))
            log1p(e[:], (z[:], z2[:]), a)
            V.mark(V.then().tensor_scalar(f[:], f[:], 0.0, None, ALU.min))
            v = V.mark(V.then().tensor_tensor(f[:], f[:], e[:], ALU.subtract))
            SP.wait_ge(*v)
            s = store.mark(SP.dma_start(fox_log, f[:]))
            SP.wait_ge(*s)
            a = load.mark(SP.dma_start(cum[:], fox_log.rearrange("(h a) n -> h (a n)", h=FOX_HEADS)))
            V.mark(V.then().memset(one[:], 1.0))
            v = V.mark(V.then(a).tensor_tensor_scan(cum[:], one[:], cum[:], 0.0, ALU.mult, ALU.add))
            SP.wait_ge(*v)
            store.mark(SP.dma_start(fox_cum, cum[:]))
            barrier()

        def head_bias(at):
            cb = sb(at, "fx_cb", [P, L])
            return cb, lambda i: load.mark(SP.dma_start(cb[:], fox_cum[i].partition_broadcast(P)))

        def add_bias(sc, psum, cb, q0, k0, k1):
            v = V.mark(nc.vector.scalar_tensor_tensor(sc, psum, HD ** -0.5, cb[:, k0:k1], ALU.mult, ALU.subtract))
            V.mark(V.then().tensor_tensor(sc[:, k1 - k0 - P:], sc[:, k1 - k0 - P:], causal[:], ALU.add))
            return v

        attention(FOX_HEADS, [(n * P, 0, (n + 1) * P) for n in range(8)], proj1, (Q_, K_, V_), mixed1, 8,
                  head_bias, add_bias, "fox", {V: 56, A: 22, PE: 30, load: 64, stores[0]: 16})

    def band():
        with ExitStack() as outer:
            edge = sb(outer, "bd_edge", [P, BAND])
            barrier()
            G.mark(G.then().memset(edge[:], 0.0))
            G.mark(G.then().memset(edge[0:64, LEFT + 64:], -1e30))
            G.mark(G.then().memset(edge[64:P, 0:64], -1e30))
            barrier()

            def head_bias(at):
                rel = sb(at, "bd_rel", [P, BAND])
                return rel, lambda i: load.mark(SP.dma_start(rel[:], t["rel"][i]))

            def add_bias(sc, psum, rel, q0, k0, k1):
                off = k0 - (q0 - LEFT)
                v = V.mark(nc.vector.scalar_tensor_tensor(sc, psum, HD ** -0.5, rel[:, off:], ALU.mult, ALU.add))
                V.mark(V.then().tensor_tensor(sc, sc, edge[:, off:], ALU.add))
                return v

            attention(BAND_HEADS, [(n * P, max(0, n * P - LEFT), (n + 1) * P) for n in range(8)], proj2,
                      (AQ, AK, AV), mixed2, 0, head_bias, add_bias, "band", {V: 56, A: 22, PE: 30, load: 64, stores[0]: 16})

    def s5():
        barrier()
        RE, IM = 0, 1
        with ExitStack() as keep:
            wl = sb(keep, "s5_wl", [P, PAIRS, 2, P])
            cl = sb(keep, "s5_cl", [P, PAIRS, 2, T + 1, S5_H])
            dl = sb(keep, "s5_dl", [P, S5_G, P])
            scan = sb(keep, "s5_scan", [P, LEVELS, 3, PAIRS])
            with ExitStack() as at:
                pw = sb(at, "s5_pw", [P, T + 1, 2, PAIRS])
                tm = sb(at, "s5_tm", [P, 12, PAIRS])
                bb = sb(at, "s5_b", [P, 4, PAIRS, S5_H])
                cc = sb(at, "s5_c", [P, 2, PAIRS, S5_H])
                wp = sb(at, "s5_wp", [P, 2, PAIRS, T, S5_H])
                tmp = sb(at, "s5_tmp", [P, 2, PAIRS, S5_H])
                kp = sb(at, "s5_kp", [S5_H, S5_G, 2 * T - 1, S5_H])
                dg = sb(at, "s5_dg", [S5_H, S5_G])
                load.mark(SP.dma_start(bb[:, 0:2, :, :], t["s5_b"]))
                load.mark(SP.dma_start(cc[:], t["s5_c"]))
                got = load.mark(SP.dma_start(dg[:], t["s5_d"]))
                G.mark(G.then().memset(kp[:], 0.0))
                v0 = VEC["a_re"][0]
                a_re, a_im, log_dt = (vec[:, VEC[n][0]:VEC[n][0] + PAIRS] for n in ("a_re", "a_im", "log_dt"))

                def tt(o, x, y, op):
                    return V.mark(V.then().tensor_tensor(o, x, y, op))

                def ts(o, x, s1, op, s2=None, op2=None):
                    if op2 is None:
                        return V.mark(V.then().tensor_scalar(o, x, s1, None, op))
                    return V.mark(V.then().tensor_scalar(o, x, s1, s2, op, op2))

                def cmul(ore, oim, xre, xim, yre, yim, t0, t1):
                    tt(t0, xre, yre, ALU.mult)
                    tt(t1, xim, yim, ALU.mult)
                    tt(ore, t0, t1, ALU.subtract)
                    tt(t0, xre, yim, ALU.mult)
                    tt(t1, xim, yre, ALU.mult)
                    return tt(oim, t0, t1, ALU.add)

                r = [tm[:, n, :] for n in range(12)]
                V.after(got)
                lre, dt, ang, turn, mag, cos, sin = r[0:7]
                ts(lre, a_re, -1e-4, ALU.min)
                a = A.mark(A.after(V.last()).activation(dt, log_dt, ACT.Exp))
                V.after(a)
                tt(mag, lre, dt, ALU.mult)
                a = A.mark(A.after(V.last()).activation(mag, mag, ACT.Exp))
                tt(ang, a_im, dt, ALU.mult)
                ts(turn, ang, 1.0 / (2 * math.pi), ALU.mult)
                ts(turn, turn, 12582912.0, ALU.add)
                ts(turn, turn, 12582912.0, ALU.subtract)
                for part in (6.28125, 1.9353071693331003e-3, 1.0253259e-11):
                    V.mark(V.then().scalar_tensor_tensor(ang, turn, -part, ang, ALU.mult, ALU.add))
                ts(ang, ang, 3.1415925, ALU.min, -3.1415925, ALU.max)
                a = A.mark(A.after(V.last()).activation(sin, ang, ACT.Sin))
                a = A.mark(A.then().activation(cos, ang, ACT.Abs))
                V.after(a)
                ts(cos, cos, -1.0, ALU.mult, math.pi / 2, ALU.add)
                a = A.mark(A.after(V.last()).activation(cos, cos, ACT.Sin))
                V.after(a)
                V.mark(V.then().memset(pw[:, 0, RE, :], 1.0))
                V.mark(V.then().memset(pw[:, 0, IM, :], 0.0))
                tt(pw[:, 1, RE, :], mag, cos, ALU.mult)
                tt(pw[:, 1, IM, :], mag, sin, ALU.mult)
                for j in range(2, T + 1):
                    cmul(pw[:, j, RE, :], pw[:, j, IM, :], pw[:, j - 1, RE, :], pw[:, j - 1, IM, :],
                         pw[:, 1, RE, :], pw[:, 1, IM, :], r[7], r[8])
                V.mark(V.then().tensor_copy(scan[:, 0, 0:2, :], pw[:, T, :, :]))
                for n in range(1, LEVELS):
                    cmul(scan[:, n, RE, :], scan[:, n, IM, :], scan[:, n - 1, RE, :], scan[:, n - 1, IM, :],
                         scan[:, n - 1, RE, :], scan[:, n - 1, IM, :], r[7], r[8])
                nre, d, cre, cim, nim = r[7], r[8], r[9], r[10], r[11]
                tt(d, lre, lre, ALU.mult)
                tt(nim, a_im, a_im, ALU.mult)
                tt(d, d, nim, ALU.add)
                V.mark(V.then().reciprocal(d, d))
                ts(nre, pw[:, 1, RE, :], 1.0, ALU.subtract)
                tt(cre, nre, lre, ALU.mult)
                tt(nim, pw[:, 1, IM, :], a_im, ALU.mult)
                tt(cre, cre, nim, ALU.add)
                tt(cim, pw[:, 1, IM, :], lre, ALU.mult)
                tt(nim, nre, a_im, ALU.mult)
                tt(cim, cim, nim, ALU.subtract)
                tt(cre, cre, d, ALU.mult)
                tt(cim, cim, d, ALU.mult)

                def over_h(x):
                    return x.unsqueeze(2).to_broadcast([P, PAIRS, S5_H])

                t0, t1 = tmp[:, 0, :, :], tmp[:, 1, :, :]
                cmul(bb[:, 2, :, :], bb[:, 3, :, :], bb[:, 0, :, :], bb[:, 1, :, :], over_h(cre), over_h(cim), t0, t1)
                for j in range(T):
                    cmul(wp[:, RE, :, j, :], wp[:, IM, :, j, :], bb[:, 2, :, :], bb[:, 3, :, :],
                         over_h(pw[:, T - 1 - j, RE, :]), over_h(pw[:, T - 1 - j, IM, :]), t0, t1)
                for j in range(T + 1):
                    cmul(cl[:, :, RE, j, :], cl[:, :, IM, j, :], cc[:, 0, :, :], cc[:, 1, :, :],
                         over_h(pw[:, j, RE, :]), over_h(pw[:, j, IM, :]), t0, t1)
                    ts(cl[:, :, IM, j, :], cl[:, :, IM, j, :], -1.0, ALU.mult)
                v = V.last()
                wl_ready = transposes(wl[:].rearrange("p a c n -> p (a c) n"),
                                      lambda j: wp[:, j % 2, j // 2, :, :].rearrange("p a b -> p (a b)"),
                                      2 * PAIRS, P, v)
                copied = wl_ready
                for p0 in range(0, PAIRS, 4):
                    PE.after(v, copied)
                    for pr in range(p0, p0 + 4):
                        for g in range(2):
                            row = S5_P * g
                            for c in (RE, IM):
                                last = nc.tensor.matmul(bank[g][0:S5_H, (pr - p0) * P:(pr - p0 + 1) * P],
                                                        bb[row:row + S5_P, 2 + c, pr, :],
                                                        cl[row:row + S5_P, pr, c, 0:T, :].rearrange("p a b -> p (a b)"),
                                                        start=c == RE, stop=c == IM)
                    ready = PE.mark(last)
                    for g in range(2):
                        copied = V.mark(V.after(ready, G.last()).tensor_copy(
                            kp[:, 2 * p0 + g:2 * p0 + 8:2, T - 1:, :].rearrange("p g a b -> p g (a b)"),
                            bank[g][0:S5_H, :].rearrange("p (g n) -> p g n", g=4)))
                skip = tmp[0:S5_H, :, :, :].rearrange("p a b c -> p (a b) c")
                tt(skip, ident[0:S5_H, 0:S5_H].unsqueeze(1).to_broadcast([S5_H, S5_G, S5_H]),
                   dg[:].unsqueeze(2).to_broadcast([S5_H, S5_G, S5_H]), ALU.mult)
                v = tt(kp[:, :, T - 1, :], kp[:, :, T - 1, :], skip, ALU.add)
                SP.wait_ge(*v)
                for j in range(T):
                    load.mark(SP.dma_start(dl[j * S5_H:(j + 1) * S5_H, :, :].rearrange("p g (a b) -> p g a b", a=T),
                                           kp[:, :, T - 1 - j:2 * T - 1 - j, :]))
                barrier()
            with ExitStack() as at:
                u = sb(at, "s5_ut", [P, 2, L])
                uc = sb(at, "s5_uc", [P, S5_G, CH])
                x = [[sb(at, f"s5_x{n}{c}", [P, PAIRS, CH]) for c in "ri"] for n in range(2)]
                tq = [sb(at, f"s5_t{n}", [P, PAIRS, CH]) for n in range(2)] if 0 else None
                for n in range(4):
                    s = n % 2
                    SP.wait_ge(*stores[s].last())
                    a = loads[s].mark(SP.dma_start(u[:, s, :], proj1[U_ + n]))
                    v = V.mark(V.after(a).tensor_copy(x[0][s][:, 0:T, :], u[:, s, :].rearrange("p (m j) -> p j m", j=T)))
                    SP.wait_ge(*v)
                    stores[s].mark(SP.dma_start(s5_u.rearrange("(n p) j m -> n p j m", p=P)[n], x[0][s][:, 0:T, :]))
                for s in stores:
                    SP.wait_ge(*s.last())
                for j in range(T):
                    got = load.mark(SP.dma_start(uc[j * S5_H:(j + 1) * S5_H, :, :],
                                                 s5_u[:, j, :].rearrange("(g h) m -> h g m", h=S5_H)))
                read = V.last()
                for pr in range(0, PAIRS, 4):
                    for c in (RE, IM):
                        PE.after(got, read)
                        for n in range(4):
                            for g in range(2):
                                last = nc.tensor.matmul(bank[c][g * S5_P:(g + 1) * S5_P, n * CH:(n + 1) * CH],
                                                        wl[:, pr + n, c, g * S5_P:(g + 1) * S5_P],
                                                        uc[:, 2 * (pr + n) + g, :], start=True, stop=True)
                        ready = PE.mark(last)
                        read = V.mark(V.after(ready).tensor_copy(
                            x[0][c][:, pr:pr + 4, :], bank[c][:].rearrange("p (n m) -> p n m", n=4)))
                t0, t1 = (u[:, n, :].rearrange("p (a b) -> p a b", a=8) for n in range(2))
                for n in range(LEVELS):
                    sh = 1 << n
                    old, new = x[n % 2], x[(n + 1) % 2]
                    w = CH - sh
                    for c in range(2):
                        V.mark(V.then().tensor_copy(new[c][:, :, 0:sh], old[c][:, :, 0:sh]))
                    for half in range(2):
                        p0, p1 = half * 8, half * 8 + 8
                        ar, ai = (scan[:, n, c, p0:p1].unsqueeze(2).to_broadcast([P, 8, w]) for c in range(2))
                        xr, xi = (old[c][:, p0:p1, 0:w] for c in range(2))
                        for c, (f0, f1, op) in enumerate((((xr, ar), (xi, ai), ALU.subtract),
                                                          ((xi, ar), (xr, ai), ALU.add))):
                            V.mark(V.then().tensor_tensor(t0[:, :, 0:w], *f0, ALU.mult))
                            V.mark(V.then().tensor_tensor(t1[:, :, 0:w], *f1, ALU.mult))
                            V.mark(V.then().tensor_tensor(t0[:, :, 0:w], t0[:, :, 0:w], t1[:, :, 0:w], op))
                            V.mark(V.then().tensor_tensor(new[c][:, p0:p1, sh:], old[c][:, p0:p1, sh:],
                                                          t0[:, :, 0:w], ALU.add))
                state = x[LEVELS % 2]
                scanned = V.last()
                y = [x[(LEVELS + 1) % 2][c][:] for c in range(2)]
                read = None
                for p0 in range(0, PAIRS, 4):
                    PE.after(scanned, read)
                    for pr in range(p0, p0 + 4):
                        for g in range(2):
                            row, o, ps = S5_P * g, (pr - p0) * CH, bank[g]
                            nc.tensor.matmul(ps[:, o:o + CH], dl[:, 2 * pr + g, :], uc[:, 2 * pr + g, :],
                                             start=True, stop=False)
                            for c in (RE, IM):
                                last = nc.tensor.matmul(ps[:, o + 1:o + CH],
                                                        cl[row:row + S5_P, pr, c, 1:, :].rearrange("p a b -> p (a b)"),
                                                        state[c][row:row + S5_P, pr, 0:CH - 1],
                                                        start=False, stop=c == IM)
                    ready = PE.mark(last)
                    for g in range(2):
                        g0 = 2 * p0 % 16 + g
                        read = V.mark(V.after(ready).tensor_copy(y[p0 // 8][:, g0:g0 + 7:2, :],
                                                                 bank[g][:].rearrange("p (n m) -> p n m", n=4)))
                SP.wait_ge(*read)
                s5_y_v = s5_y.rearrange("(c g h) j m -> c j h g m", c=2, h=S5_H)
                for c in range(2):
                    for j in range(T):
                        store.mark(SP.dma_start(s5_y_v[c, j], y[c][j * S5_H:(j + 1) * S5_H, :, :]))
                SP.wait_ge(*store.last())
                barrier()
                z = [state[c][:, 0:T, :].rearrange("p a b -> p (a b)") for c in range(2)]
                gates = [x[(LEVELS + 1) % 2][c][:, 0:T, :].rearrange("p a b -> p (a b)") for c in range(2)]
                glu = sb(at, "s5_glu", [P, 4, P])
                w_here = load.mark(SP.dma_start(glu[:], t["glu"].rearrange("n p k -> p n k")))
                read = None
                for n in range(4):
                    s = n % 2
                    SP.wait_ge(*V.last())
                    a = loads[s].mark(SP.dma_start(z[s], s5_y.rearrange("(n p) j m -> n p (j m)", p=P)[n]))
                    a = A.mark(A.after(a).activation(z[s], z[s], ACT.Gelu_apprx_tanh))
                    PE.after(a, w_here, read)
                    for h in range(2):
                        last = nc.tensor.matmul(wide[:, h * HALF:(h + 1) * HALF], glu[:, n, :],
                                                z[s][:, h * HALF:(h + 1) * HALF], start=True, stop=True)
                    ready = PE.mark(last)
                    read = A.mark(A.after(ready).activation(gates[s], wide[:], ACT.Sigmoid))
                    v = V.mark(V.after(read, stores[s].last()).tensor_tensor(
                        u[:, s, :].rearrange("p (m j) -> p j m", j=T), z[s].rearrange("p (j m) -> p j m", j=T),
                        gates[s].rearrange("p (j m) -> p j m", j=T), ALU.mult))
                    SP.wait_ge(*v)
                    stores[s].mark(SP.dma_start(mixed1[n], u[:, s, :]))
                barrier()

    def hgrn():
        barrier()
        NT = L // P
        with ExitStack() as at:
            q, f, vi, g, kf, b, e, t0, t1, o = (sb(at, "hg_" + n, [P, L]) for n in
                                                ("q", "f", "v", "g", "k", "b", "e", "t0", "t1", "o"))
            sc = sb(at, "hg_sc", [P, NT, 2, P])
            masks = sb(at, "hg_mask", [P, LEVELS + 1, P])
            reset = sb(at, "hg_reset", [P, L])
            vt, kt = sb(at, "hg_vt", [P, NT, P]), sb(at, "hg_kt", [P, NT, P])
            st = sb(at, "hg_st", [P, NT + 1, HD])
            dec = sb(at, "hg_dec", [P, NT])
            heads = sb(at, "hg_heads", [P, P])
            lb = sb(at, "hg_lb", [P, 3, 2])
            for n in range(LEVELS):
                w = P >> (n + 1)
                m = masks[:, n, :].rearrange("p (a b c) -> p a b c", b=2, c=w)[:, :, 1, :]
                G.mark(G.then().memset(masks[:, n, :], 0.0))
                G.mark(G.then().memset(m, 1.0))
                G.mark(G.then().affine_select(out=m, in_=m, compare_op=ALU.is_ge, fill=0.0, base=0,
                                              pattern=[[-2 * w, P // (2 * w)], [0, w]], channel_multiplier=1))
                G.mark(G.then().affine_select(out=m, in_=m, compare_op=ALU.is_ge, fill=0.0, base=w - 1,
                                              pattern=[[2 * w, P // (2 * w)], [0, w]], channel_multiplier=-1))
            G.mark(G.then().tensor_copy(masks[:, LEVELS, :], ident[:]))
            G.mark(G.then().memset(reset[:], 1.0))
            G.mark(G.then().memset(reset[:].rearrange("p (a b) -> p a b", b=P)[:, :, 0:1], 0.0))
            G.mark(G.then().memset(heads[:], 0.0))
            G.mark(G.then().memset(heads[0:HD, 0:HD], 1.0))
            G.mark(G.then().memset(heads[HD:P, HD:P], 1.0))
            G.mark(G.then().memset(st[:, 0, :], 0.0))
            x, oml, tmp = lb[:, 0, :], lb[:, 1, :], lb[:, 2, :]
            logits = vec[:, VEC["lb"][0]:VEC["lb"][0] + 2]
            v = V.mark(nc.vector.tensor_tensor(x, logits, logits, ALU.subtract))
            a = A.mark(A.after(v).activation(x, x, ACT.Exp))
            V.mark(V.after(a).reciprocal(tmp, x))
            V.mark(V.then().tensor_tensor(tmp, tmp, x, ALU.mult))
            V.mark(V.then().tensor_tensor(x, tmp, tmp, ALU.subtract))
            V.mark(V.then().tensor_scalar(oml, x, -1.0, 1.0, ALU.mult, ALU.add))
            barrier()

            def tt(out, x, y, op, *after):
                return V.mark(V.then(*after).tensor_tensor(out, x, y, op))

            def act(out, x, fn, *after, **kw):
                return A.mark(A.then(V.last(), *after).activation(out, x, fn, **kw))

            with loop(nc, 2, {V: 83, A: 22, G: 28, PE: 39, load: 64, stores[0]: 16}) as i:
                for m in (V, A, G, PE):
                    SP.wait_ge(*m.last())
                for buf, row in ((q, BQ), (f, BF), (vi, BI), (g, BG)):
                    load.mark(SP.dma_start(buf[:], proj2[i + row]))
                got = load.last()
                V.after(got)
                lbc, omc = (lb[:, n, bass.ds(i, 1)] for n in range(2))
                act(q[:], q[:], ACT.Silu, got)
                act(g[:], g[:], ACT.Silu)
                act(kf[:], f[:], ACT.Sigmoid, scale=-1.0)
                a = act(f[:], f[:], ACT.Sigmoid)
                V.mark(V.then(a).tensor_scalar(kf[:], kf[:], omc, None, ALU.mult))
                V.mark(V.then().tensor_scalar(f[:], f[:], omc, lbc, ALU.mult, ALU.add))
                V.mark(V.then().tensor_scalar(t0[:], f[:], LOG_FLOOR, 2.0 ** -60, ALU.max, ALU.max))
                V.mark(V.then().tensor_scalar(t1[:], f[:], LOG_FLOOR, 2.0 ** 60, ALU.max, ALU.mult))
                V.mark(V.then().tensor_scalar(t1[:], t1[:], 1.0, None, ALU.min))
                act(t0[:], t0[:], ACT.Ln)
                a = act(t1[:], t1[:], ACT.Ln)
                tt(t0[:], t0[:], t1[:], ALU.add, a)
                V.mark(V.then().tensor_tensor_scan(b[:], reset[:], t0[:], 0.0, ALU.mult, ALU.add))
                for n in range(LEVELS + 1):
                    if n < LEVELS:
                        w = P >> (n + 1)
                        b4, e4 = (x[:].rearrange("p (a c w) -> p a c w", c=2, w=w) for x in (b, e))
                        mid = b4[:, :, 0, w - 1:w].to_broadcast([P, L // (2 * w), w])
                        PE_done = PE.last()
                        tt(e4[:, :, 1, :], b4[:, :, 1, :], mid, ALU.subtract)
                        tt(e4[:, :, 0, :], mid, b4[:, :, 0, :], ALU.subtract)
                        a = act(e[:], e[:], ACT.Exp)
                        tt(t0[:], q[:], e[:], ALU.mult, a, PE_done)
                        ready = tt(t1[:], kf[:], e[:], ALU.mult)
                        qx, kx = t0, t1
                    else:
                        ready, (qx, kx) = V.last(), (q, kf)
                    for n2 in range(4):
                        ps = (wide[:, 0:HALF], wide[:, HALF:L], bank[0][:], bank[1][:])[n2]
                        PE.after(ready, sc_read[n2] if n else None)
                        for m in range(4):
                            tile, h = 4 * (n2 // 2) + m, n2 % 2
                            last = nc.tensor.matmul(ps[:, m * P:(m + 1) * P],
                                                    kx[h * HD:(h + 1) * HD, tile * P:(tile + 1) * P],
                                                    qx[h * HD:(h + 1) * HD, tile * P:(tile + 1) * P],
                                                    start=True, stop=True)
                        pr = PE.mark(last)
                        dst = sc[:, 4 * (n2 // 2):4 * (n2 // 2) + 4, n2 % 2, :]
                        src = ps.rearrange("p (m n) -> p m n", n=P)
                        mk = masks[:, n, :].unsqueeze(1).to_broadcast([P, 4, P])
                        if n == 0:
                            sc_read[n2] = tt(dst, src, mk, ALU.mult, pr)
                        else:
                            part = o[:, (n2 % 2) * HALF:(n2 % 2 + 1) * HALF].rearrange("p (m n) -> p m n", n=P)
                            sc_read[n2] = tt(part, src, mk, ALU.mult, pr, sc_add[n2 % 2])
                            sc_add[n2 % 2] = G.mark(G.then(sc_read[n2]).tensor_tensor(dst, dst, part, ALU.add))
                    if n == 0:
                        sc_add[0] = sc_add[1] = V.last()
                b3, t3 = (x[:].rearrange("p (a n) -> p a n", n=P) for x in (b, t1))
                blast = b3[:, :, P - 1:P]
                tt(t3, blast.to_broadcast([P, NT, P]), b3, ALU.subtract, PE.last())
                act(t1[:], t1[:], ACT.Exp)
                act(e[:], b[:], ACT.Exp)
                a = act(dec[:], blast.rearrange("p a n -> p (a n)"), ACT.Exp)
                tt(t1[:], t1[:], kf[:], ALU.mult, a)
                ready = tt(t0[:], q[:], e[:], ALU.mult)
                transposes(vt, lambda j: vi[:, j * P:(j + 1) * P], NT, P, ready)
                done = transposes(kt, lambda j: t1[:, j * P:(j + 1) * P], NT, P, A.last())
                PE.after(done)
                for n in range(NT):
                    for h in range(2):
                        last = nc.tensor.matmul(bank[1][h * HD:(h + 1) * HD, n * HD:(n + 1) * HD],
                                                kt[:, n, h * HD:(h + 1) * HD], vt[:, n, h * HD:(h + 1) * HD],
                                                start=True, stop=True)
                pr = PE.mark(last)
                V.after(pr)
                for n in range(NT):
                    V.mark(V.then().scalar_tensor_tensor(st[:, n + 1, :], st[:, n, :], dec[:, n:n + 1],
                                                         bank[1][:, n * HD:(n + 1) * HD], ALU.mult, ALU.add))
                PE.after(V.last(), sc_add[0], sc_add[1])
                for n in range(NT):
                    for h in range(2):
                        row = slice(h * HD, (h + 1) * HD)
                        nc.tensor.matmul(wide[row, n * P:(n + 1) * P], vt[:, n, row], sc[:, n, h, :],
                                         start=True, stop=False)
                        last = nc.tensor.matmul(wide[row, n * P:(n + 1) * P], st[row, n, :], t0[row, n * P:(n + 1) * P],
                                                start=False, stop=True)
                pr = PE.mark(last)
                v = V.mark(V.then(pr).tensor_copy(o[:], wide[:]))
                a = act(t1[:], o[:], ACT.Square)
                PE.after(a)
                for h in range(2):
                    last = nc.tensor.matmul(wide[:, h * HALF:(h + 1) * HALF], heads[:], t1[:, h * HALF:(h + 1) * HALF],
                                            start=True, stop=True)
                inv_sqrt(e[:], wide[:], 1.0 / HD, PE.mark(last))
                gain = vec[:, bass.ds(i + VEC["hgrn_g"][0], 1)]
                V.mark(V.then().scalar_tensor_tensor(o[:], o[:], gain, e[:], ALU.mult, ALU.mult))
                v = tt(o[:], o[:], g[:], ALU.mult)
                SP.wait_ge(*v)
                st_ = stores[0].mark(SP.dma_start(mixed2[i + 2], o[:]))
                V.after(st_)
            barrier()

    sc_read, sc_add = {}, {}

    def gmlp():
        barrier()
        NT = L // P
        with ExitStack() as at:
            u, v = sb(at, "gm_u", [P, 2, L]), sb(at, "gm_v", [P, 2, L])
            sq, rstd = sb(at, "gm_sq", [P, 2, L]), sb(at, "gm_r", [P, L])
            vt = sb(at, "gm_vt", [P, 2, NT, P])
            w, b = sb(at, "gm_w", [P, 4, P]), sb(at, "gm_b", [P, 2, P])
            load.mark(SP.dma_start(u[:], proj2[CU:CU + 2].rearrange("k p n -> p k n")))
            load.mark(SP.dma_start(v[:], proj2[CV:CV + 2].rearrange("k p n -> p k n")))
            load.mark(SP.dma_start(w[:], t["gm_w"].rearrange("g q p -> q g p")))
            for g in range(4):
                got = load.mark(SP.dma_start(b[(g % 2) * HD:(g % 2 + 1) * HD, g // 2, :],
                                             t["gm_b"][g].partition_broadcast(HD)))
            causal_w = G.mark(G.after(got).affine_select(out=w[:], in_=w[:], compare_op=ALU.is_ge, fill=0.0, base=0,
                                                         pattern=[[0, 4], [1, P]], channel_multiplier=-1))
            A.mark(A.after(got).activation(v[:], v[:], ACT.Gelu_apprx_tanh))
            a = A.mark(A.then().activation(u[:], u[:], ACT.Gelu_apprx_tanh))
            r = rms_scale([v[:, 0, :], v[:, 1, :]], sq, rstd, 1.0 / 256, a)
            for k in range(2):
                n = V.mark(V.after(r).scalar_tensor_tensor(v[:, k, :], v[:, k, :], col("gmlp_g", k), rstd[:],
                                                           ALU.mult, ALU.mult))
            vt_ready = None
            for k in range(2):
                vt_ready = transposes(vt[:, k, :, :], lambda j, k=k: v[:, k, j * P:(j + 1) * P], NT, P, n, free=vt_ready)
            PE.after(vt_ready, causal_w)
            for k in range(2):
                for n in range(NT):
                    for g in range(2):
                        last = nc.tensor.matmul(wide[g * HD:(g + 1) * HD, n * P:(n + 1) * P],
                                                vt[:, k, n, g * HD:(g + 1) * HD], w[:, 2 * k + g, :],
                                                start=True, stop=True)
                ready = PE.mark(last)
                o = V.mark(V.after(ready).tensor_tensor(
                    sq[:, k, :].rearrange("p (n m) -> p n m", m=P), wide[:].rearrange("p (n m) -> p n m", m=P),
                    b[:, k, :].unsqueeze(1).to_broadcast([P, NT, P]), ALU.add))
                PE.after(o)
                o = V.mark(V.then().tensor_tensor(sq[:, k, :], sq[:, k, :], u[:, k, :], ALU.mult))
                SP.wait_ge(*o)
                store.mark(SP.dma_start(mixed2[4 + k], sq[:, k, :]))
            barrier()

    def lru():
        barrier()
        with ExitStack() as at:
            x, gate, xc, r, ig, la, m = (sb(at, "lr_" + n, [P, L]) for n in ("x", "g", "xc", "r", "i", "la", "m"))
            wa, wx = sb(at, "lr_wa", [P, 2, P]), sb(at, "lr_wx", [P, 2, P])
            sp = sb(at, "lr_sp", [P, 4, 2])
            load.mark(SP.dma_start(wa[:], t["lru_w"][0].rearrange("k p n -> p k n")))
            w_here = load.mark(SP.dma_start(wx[:], t["lru_w"][1].rearrange("k p n -> p k n")))
            lam = vec[:, VEC["lru_lam"][0]:VEC["lru_lam"][0] + 2]
            a = A.mark(nc.scalar.activation(sp[:, 0, :], lam, ACT.Abs))
            a = A.mark(A.then().activation(sp[:, 0, :], sp[:, 0, :], ACT.Exp, scale=-1.0))
            log1p(sp[:, 0, :], (sp[:, 1, :], sp[:, 2, :]), a)
            V.mark(V.then().tensor_scalar(sp[:, 1, :], lam, -1.0, 0.0, ALU.mult, ALU.max))
            V.mark(V.then().tensor_tensor(sp[:, 0, :], sp[:, 0, :], sp[:, 1, :], ALU.add))
            V.mark(V.then().tensor_scalar(sp[:, 3, :], sp[:, 0, :], -LRU_C, None, ALU.mult))
            for k in range(2):
                for mm in (V, A, PE):
                    SP.wait_ge(*mm.last())
                SP.wait_ge(*store.last())
                load.mark(SP.dma_start(x[:], proj2[DX + k]))
                got = load.mark(SP.dma_start(gate[:], proj2[DG + k]))
                V.after(got)
                V.mark(V.then().tensor_scalar(xc[:], x[:], col("lru_cw", 3 * 2 + k), col("lru_cb", k), ALU.mult, ALU.add))
                for back in (1, 2, 3):
                    V.mark(V.then().scalar_tensor_tensor(xc[:, back:], x[:, :L - back], col("lru_cw", (3 - back) * 2 + k),
                                                         xc[:, back:], ALU.mult, ALU.add))
                c = V.last()
                read = None
                for w, dst, bias in ((wa, r, "lru_ba"), (wx, ig, "lru_bx")):
                    PE.after(c, w_here, read)
                    for h in range(2):
                        last = nc.tensor.matmul(wide[:, h * HALF:(h + 1) * HALF], w[:, k, :],
                                                xc[:, h * HALF:(h + 1) * HALF], start=True, stop=True)
                    ready = PE.mark(last)
                    read = A.mark(A.then(ready).activation(dst[:], wide[:], ACT.Sigmoid, bias=col(bias, k)))
                decay = sp[:, 3, k:k + 1]
                A.mark(A.then(V.last()).activation(la[:], r[:], ACT.Tanh, scale=decay))
                a = A.mark(A.then().activation(r[:], r[:], ACT.Exp, scale=decay))
                V.mark(V.then(a).tensor_tensor(m[:], r[:], r[:], ALU.mult))
                V.mark(V.then().scalar_tensor_tensor(m[:], m[:], 1.0, la[:], ALU.add, ALU.mult))
                v = V.mark(V.then().tensor_scalar(m[:], m[:], -1.0, 0.0, ALU.mult, ALU.max))
                a = A.mark(A.then(v).activation(m[:], m[:], ACT.Sqrt))
                V.mark(V.then(a).memset(m[:, 0:1], 1.0))
                V.mark(V.then().tensor_tensor(ig[:], ig[:], xc[:], ALU.mult))
                V.mark(V.then().tensor_tensor(m[:], m[:], ig[:], ALU.mult))
                V.mark(V.then().tensor_tensor_scan(xc[:], r[:], m[:], 0.0, ALU.mult, ALU.add))
                a = A.mark(A.then().activation(gate[:], gate[:], ACT.Gelu_apprx_tanh))
                v = V.mark(V.then(a).tensor_tensor(xc[:], xc[:], gate[:], ALU.mult))
                SP.wait_ge(*v)
                store.mark(SP.dma_start(mixed2[6 + k], xc[:]))
            barrier()

    def merge(mixed, proj, gate_row, branches, name):
        tiles = 12 // branches if branches == 3 else 2
        blocks = 4 if branches == 3 else 2
        units = branches * tiles * blocks // 8
        n_in = branches * tiles
        barrier()
        with ExitStack() as at:
            mh, ml = sb(at, name + "h", [P, n_in, L], F32R), sb(at, name + "l", [P, n_in, L], F32R)
            with ExitStack() as inner:
                x = sb(inner, name + "x", [P, 2, L])
                for n in range(n_in):
                    s = n % 2
                    SP.wait_ge(*V.last())
                    a = loads[s].mark(SP.dma_start(x[:, s, :], mixed[n]))
                    split_act(x[:, s, :], mh[:, n, :], ml[:, n, :], a)
                barrier()
            gates = sb(at, name + "g", [P, branches, L])
            m, part = sb(at, name + "m", [P, L]), sb(at, name + "p", [P, L])
            for br in range(branches):
                gate_in[br].mark(SP.dma_start(gates[:, br, :], proj[gate_row + 8 * br]))

            def rhs(o, k):
                n = (o % branches) * tiles + k
                return mh[:, n, :], ml[:, n, :]

            def evict(i, o, psum, ready, read):
                block, br = o // branches, o % branches
                if br == 0:
                    done = read(V.then(ready, gate_in[br].last()).tensor_tensor(m[:], gates[:, br, :], psum[:], ALU.mult))
                else:
                    done = read(V.after(ready, gate_in[br].last(), G.last())
                                .tensor_tensor(part[:], gates[:, br, :], psum[:], ALU.mult))
                    G.mark(G.then(done).tensor_tensor(m[:], m[:], part[:], ALU.add))
                SP.wait_ge(*done)
                gate_in[br].mark(SP.dma_start(gates[:, br, :], proj[i * blocks + (gate_row + 8 * br + block + 1)]))
                if br == branches - 1:
                    at_ = bass.ds(i * blocks + block, 1)
                    hi, lo = (x[:, at_, :].rearrange("p a n -> p (a n)") for x in (act_hi, act_lo))
                    a = A.mark(A.after(G.last()).copy(hi, m[:]))
                    V.mark(V.after(a).tensor_tensor(lo, m[:], hi.bitcast(F32), ALU.subtract))

            per = {G: blocks * (branches - 1), A: blocks, V: blocks, PE: blocks * branches - units}
            per.update({gate_in[br]: 16 * blocks for br in range(branches)})
            stage(KT // blocks, units, blocks * branches, tiles, rhs, evict, per=per)
            for br in range(branches):
                SP.wait_ge(*gate_in[br].last())
            barrier()

    gate_in = [Count(sem(f"gate_in{n}")) for n in range(4)]

    def mix_out(x_dram, gain, out_dram, name):
        with ExitStack() as at:
            y = sb(at, name + "y", [P, KT, L])

            def evict(i, o, psum, ready, read):
                read(V.after(ready).tensor_copy(y[:, bass.ds(i * 2 + o, 1), :].rearrange("p a n -> p (a n)"), psum[:]))

            stage(4, 2, 2, KT, act_rhs, evict)
            for e in (nc.scalar, nc.vector, nc.tensor):
                for c in pair_read:
                    e.wait_ge(*c.last())
            norm_out(y, x_dram, gain, out_dram, name)

    def mlp(x_dram, gain, out_dram, groups, gated, name):
        barrier()
        with ExitStack() as at:
            acc = sb(at, name + "acc", [P, KT, L])
            with ExitStack() as inner:
                hh, hl = sb(inner, name + "hh", [P, 8, L], F32R), sb(inner, name + "hl", [P, 8, L], F32R)
                x = sb(inner, name + "x", [P, 2, L])

                def hidden_done(index, s, mark):
                    hi, lo = (h[:, bass.ds(index, 1), :].rearrange("p a n -> p (a n)") for h in (hh, hl))
                    a = A.mark(A.after(mark).copy(hi, x[:, s, :]))
                    V.mark(V.after(a).tensor_tensor(lo, x[:, s, :], hi.bitcast(F32), ALU.subtract))

                def evict_relu2(i, o, psum, ready, read):
                    s = o % 2
                    a = read(A.after(ready, V.turn_ago((V.sem, V.n + 2))).activation(x[:, s, :], psum[:], ACT.Relu))
                    v = V.mark(V.after(a).tensor_tensor(x[:, s, :], x[:, s, :], x[:, s, :], ALU.mult))
                    hidden_done(i * 2 + o, s, v)

                def evict_swiglu(i, o, psum, ready, read):
                    if o == 0:
                        gate_done["m"] = read(A.after(ready, V.last()).activation(x[:, 0, :], psum[:], ACT.Silu))
                    else:
                        v = read(V.after(ready, gate_done["m"]).tensor_tensor(x[:, 1, :], x[:, 0, :], psum[:], ALU.mult))
                        hidden_done(i, 1, v)

                gate_done = {}
                for n, tiles in enumerate(groups):
                    if gated:
                        stage(tiles, 2, 2, KT, act_rhs, evict_swiglu, per={A: 1, V: 1})
                    else:
                        stage(tiles // 2, 2, 2, KT, act_rhs, evict_relu2, per={A: 2, V: 4})
                    nc.tensor.wait_ge(*V.last())

                    def evict(i, o, psum, ready, read, n=n):
                        dst = acc[:, bass.ds(i * 2 + o, 1), :].rearrange("p a n -> p (a n)")
                        if n == 0:
                            read(V.after(ready).tensor_copy(dst, psum[:]))
                        else:
                            read(V.after(ready).tensor_tensor(dst, dst, psum[:], ALU.add))

                    stage(4, 2, 2, tiles, lambda o, k: (hh[:, k, :], hl[:, k, :]), evict)
                    for e in (nc.scalar, nc.vector, nc.tensor, nc.gpsimd):
                        for c in pair_read:
                            e.wait_ge(*c.last())
            norm_out(acc, x_dram, gain, out_dram, name)

    x_in = t["x"]
    SP.wait_ge(*load.last())
    for n, d in enumerate((proj1[N1], proj2[N2])):
        stores[n].mark(SP.dma_start(d, x_in[0]))
    norm_in(x_in, "g_pre_mix", "n1")
    with ExitStack() as at:
        buf = sb(at, "p1", [P, 2, L])
        per = {stores[0]: 16, stores[1]: 16}
        stage(14, 2, 2, KT, act_rhs, to_dram(proj1, U_, buf), per=per)
        stage(1, 1, 1, KT, act_rhs, to_dram(proj1, F_, buf))
        stage(12, 2, 2, KT, act_rhs, to_dram(proj1, GATE1, buf, gate="b_gate"), per=per)
        barrier()
    short_conv()
    fox()
    s5()
    merge(mixed1, proj1, GATE1, 3, "m1")
    mix_out(x_in, "g_post_mix", x1, "o1")
    norm_in(x1, "g_pre_mlp", "n2")
    mlp(x1, "g_post_mlp", x2, (8, 8, 8, 8), False, "f1")

    norm_in(x2, "norm_mix_pre", "n3")
    with ExitStack() as at:
        buf = sb(at, "p2", [P, 2, L])
        stage(11, 2, 2, KT, act_rhs, to_dram(proj2, AQ, buf), per=per)
        stage(16, 2, 2, KT, act_rhs, to_dram(proj2, GATE2, buf, gate=""), per=per)
        barrier()
    band()
    hgrn()
    gmlp()
    lru()
    merge(mixed2, proj2, GATE2, 4, "m2")
    mix_out(x2, "norm_mix_post", x3, "o2")
    norm_in(x3, "norm_ffn_pre", "n4")
    mlp(x3, "norm_ffn_post", out, (8, 8, 6), True, "f2")

    for s, n in ((0, (used["units"] + 4) // 2), (1, (used["units"] + 3) // 2)):
        SP.wait_ge(s_raw[s], 16 * n)
    barrier()


def _tiles(w):
    k, n = w.shape
    return w.reshape(k // P, P, n // P, P).transpose(2, 0, 1, 3)


def _units(tiles):
    n = tiles.shape[0] // 8
    return tiles.reshape(n, 8, P, P).transpose(0, 2, 1, 3).reshape(n, P, 8 * P)


def _stream(x):
    w_in = x["w_in"][0]
    n_f = 28 * P
    f = np.pad(w_in[:, n_f:n_f + FOX_HEADS], ((0, 0), (0, P - FOX_HEADS)))
    parts = [_tiles(w_in[:, :n_f]), _tiles(f), _tiles(w_in[:, n_f + FOX_HEADS:])]
    wb = _tiles(x["w_branch"][0])
    parts += [wb, _tiles(x["w_out"][0])]
    w1, w2 = _tiles(x["w_ff1"][0]), _tiles(x["w_ff2"][0])
    for g in range(4):
        parts += [w1[8 * g:8 * g + 8], w2[:, 8 * g:8 * g + 8]]
    parts.append(_tiles(x["w_in_2"][0]))
    parts.append(_tiles(x["w_branch_2"][0].reshape(D, D)))
    parts.append(_tiles(x["w_out_2"][0]))
    w1, w2 = _tiles(x["w_ffn_in_2"][0]), _tiles(x["w_ffn_out_2"][0])
    n = HID2 // P
    w1 = np.stack([w1[:n], w1[n:]], 1)
    for g in (0, 8, 16):
        m = min(8, n - g)
        parts += [w1[g:g + m], np.pad(w2[:, g:g + m], ((0, 0), (0, 8 - m), (0, 0), (0, 0)))]
    tiles = np.concatenate([p.reshape(-1, P, P) for p in parts] + [np.zeros((3 * 8, P, P), np.float32)])
    return _units(tiles)


def _lay_out(x):
    def cols(v):
        return v.reshape(-1, P).T

    pairs = lambda v: v.reshape(PAIRS, P).T
    v = {
        "g_pre_mix": cols(x["g_pre_mix"]), "g_post_mix": cols(x["g_post_mix"]), "g_pre_mlp": cols(x["g_pre_mlp"]),
        "g_post_mlp": cols(x["g_post_mlp"]), "b_gate": cols(x["b_gate"]), "conv_w": cols(x["conv_w"]),
        "a_re": pairs(x["s5_a_re"]), "a_im": pairs(x["s5_a_im"]),
        "log_dt": np.repeat(x["s5_log_dt"].reshape(PAIRS, 2).T, S5_P, axis=0),
        "norm_mix_pre": cols(x["norm_mix_pre_2"]), "norm_mix_post": cols(x["norm_mix_post_2"]),
        "norm_ffn_pre": cols(x["norm_ffn_pre_2"]), "norm_ffn_post": cols(x["norm_ffn_post_2"]),
        "lb": cols(x["hgrn_lb_logits_2"]), "hgrn_g": cols(x["hgrn_norm_g_2"]), "gmlp_g": cols(x["gmlp_norm_g_2"]),
        "lru_cw": cols(x["lru_conv_w_2"]), "lru_cb": cols(x["lru_conv_b_2"]), "lru_ba": cols(x["lru_ba_2"]),
        "lru_bx": cols(x["lru_bx_2"]), "lru_lam": cols(x["lru_lambda_2"]),
        "b_f": np.repeat(x["fox_b_f"].reshape(FOX_HEADS, 1), P // FOX_HEADS, axis=0),
    }

    def diagonal(blocks, n):
        m, k, _ = blocks.shape
        out = np.zeros((m // n, n, k, n, k), np.float32)
        for i in range(n):
            out[:, i, :, i, :] = blocks.reshape(m // n, n, k, k)[:, i]
        return out.reshape(m // n, n * k, n * k)

    dist = np.clip(LEFT + np.arange(P)[:, None] - np.arange(BAND)[None, :], -63, 256) + 63
    b = np.stack([x["s5_b_re"][0], x["s5_b_im"][0]])
    c = np.stack([x["s5_c_re"][0], x["s5_c_im"][0]]).transpose(0, 1, 3, 2)

    def by_pair(v):
        return v.reshape(2, PAIRS, P, S5_H).transpose(2, 0, 1, 3)

    return {
        "x": x["x"][0].T.reshape(KT, P, L),
        "vec": np.concatenate([v[n] for n, _ in VEC_NAMES], axis=1),
        "stream": _stream(x),
        "s5_b": by_pair(b), "s5_c": by_pair(c),
        "s5_d": x["s5_d"][0].T,
        "glu": diagonal(x["s5_w_glu"][0], 8),
        "rel": x["attn_rel_bias_2"][0][:, dist],
        "gm_w": x["gmlp_ws_2"][0].transpose(0, 2, 1), "gm_b": x["gmlp_bs_2"][0],
        "lru_w": np.stack([diagonal(x["lru_wa_2"][0], 2), diagonal(x["lru_wx_2"][0], 2)]),
    }


def kernel(**inputs):
    import concourse.bacc as bacc
    from concourse.bass_utils import run_bass_kernel_spmd

    nc = bacc.Bacc("TRN2", target_bir_lowering=False, num_devices=1)
    arrays, t = {}, {}
    for name, a in _lay_out({n: np.asarray(v) for n, v in inputs.items()}).items():
        a = np.ascontiguousarray(a)
        arrays["in_" + name] = a
        t[name] = nc.dram_tensor("in_" + name, a.shape, mybir.dt.from_np(a.dtype), kind="ExternalInput").ap()
    out = nc.dram_tensor("out", (KT, P, L), F32, kind="ExternalOutput").ap()
    build(nc, t, out)
    r = run_bass_kernel_spmd(nc, [arrays], core_ids=[0])
    y = r.results[0]["out"]
    return np.ascontiguousarray(y.reshape(D, L).T).reshape(1, L, D)
```

```python
import math
from contextlib import ExitStack, contextmanager

import numpy as np
import concourse.bass as bass
from concourse import mybir
from concourse.alu_op_type import AluOpType as ALU

P = 128
L = 1024
D = 1024
KT = D // P
HALF = 512
HD = 64
EPS = 1e-6
S5_G, S5_P, S5_H = 32, 64, 16
PAIRS = S5_G // 2
T = 8
CH = L // T
FOX_HEADS = 8
FF1 = 4096
BAND_HEADS = 4
LEFT = 512
BAND = LEFT + P
HID2 = 2816
LOG_FLOOR = 1e-30
LRU_C = 8.0
LEVELS = 7

F32 = mybir.dt.float32
F32R = mybir.dt.float32r
ACT = mybir.ActivationFunctionType
AX = mybir.AxisListType

U_, X_, B_, C_, Q_, K_, V_, F_, GATE1 = 0, 4, 8, 12, 16, 20, 24, 28, 29
N1 = 53
AQ, AK, AV, BQ, BF, BI, BG, CU, CV, DX, DG, GATE2 = 0, 2, 4, 6, 8, 10, 12, 14, 16, 18, 20, 22
N2 = 54

VEC_NAMES = (("g_pre_mix", 8), ("g_post_mix", 8), ("g_pre_mlp", 8), ("g_post_mlp", 8), ("b_gate", 24),
             ("conv_w", 12), ("a_re", 16), ("a_im", 16), ("log_dt", 16),
             ("norm_mix_pre", 8), ("norm_mix_post", 8), ("norm_ffn_pre", 8), ("norm_ffn_post", 8),
             ("lb", 2), ("hgrn_g", 2), ("gmlp_g", 2), ("lru_cw", 8), ("lru_cb", 2), ("lru_ba", 2),
             ("lru_bx", 2), ("lru_lam", 2), ("b_f", 1))
VEC = {}
for _name, _n in VEC_NAMES:
    VEC[_name] = sum(VEC[m][1] for m in VEC), _n
NVEC = sum(n for _, n in VEC_NAMES)


COUNTERS = []


class Lane:

    def __init__(self, engine, sem, start):
        self.engine, self.sem = engine, sem
        self.n = start
        self.here = self.per = 0
        self.unit = 1
        COUNTERS.append(self)
        engine.sem_inc(sem, start)

    def after(self, *marks):
        for m in marks:
            if m is not None:
                self.engine.wait_ge(m[0], m[1])
        return self.engine

    def then(self, *marks):
        return self.after((self.sem, self.n), *marks)

    def mark(self, instruction):
        instruction.then_inc(self.sem, self.unit)
        self.n = self.n + self.unit
        self.here += self.unit
        return (self.sem, self.n)

    def last(self):
        return (self.sem, self.n)

    def turn_ago(self, mark):
        return (self.sem, mark[1] - self.per)


class Count(Lane):

    def __init__(self, sem, unit=16):
        self.sem, self.unit = sem, unit
        COUNTERS.append(self)
        self.n = self.here = self.per = 0


@contextmanager
def loop(nc, turns, per):
    start = {c: c.n for c in per}
    fixed = {c: c.n for c in COUNTERS if c not in per}
    with nc.Fori(0, turns) as i:
        for c in per:
            c.n, c.here, c.per = start[c] + i * per[c], 0, per[c]
        yield i
        assert all(c.here == per[c] for c in per), [(c.sem.name, c.here) for c in per]
        assert all(c.n is fixed[c] for c in fixed), [c.sem.name for c in fixed if c.n is not fixed[c]]
    for c in per:
        c.n, c.per = start[c] + turns * per[c], 0


def build(nc, t, out):
    COUNTERS.clear()
    with ExitStack() as ctx:
        _build(nc, ctx, t, out)


def _build(nc, ctx, t, out):
    def sb(at, name, shape, dt=F32):
        return at.enter_context(nc.sbuf_tensor(name, shape, dt))

    def sem(name):
        return ctx.enter_context(nc.semaphore(name))

    def scratch(name, shape):
        return nc.dram_tensor(name, shape, F32, kind="Internal").ap()

    proj1, proj2 = scratch("proj1", (N1 + 1, P, L)), scratch("proj2", (N2 + 1, P, L))
    mixed1 = scratch("mixed1", (12, P, L))
    mixed2 = scratch("mixed2", (8, P, L))
    x1, x2, x3 = (scratch(n, (KT, P, L)) for n in ("x1", "x2", "x3"))
    fox_cum = scratch("fox_cum", (FOX_HEADS, L))
    fox_log = scratch("fox_log", (P, L * FOX_HEADS // P))
    s5_u, s5_y = scratch("s5_u", (4 * P, T, CH)), scratch("s5_y", (4 * P, T, CH))

    V = Lane(nc.vector, sem("vector"), 1024)
    A = Lane(nc.scalar, sem("scalar"), 1024)
    G = Lane(nc.gpsimd, sem("gpsimd"), 1024)
    PE = Lane(nc.tensor, sem("tensor"), 1024)
    load = Count(sem("load"))
    store = Count(sem("store"))
    loads = [Count(sem(f"load{n}")) for n in range(2)]
    stores = [Count(sem(f"store{n}")) for n in range(2)]
    outs = [Count(sem(f"out{n}")) for n in range(2)]
    SP = nc.sync

    background = []

    class Woven:

        def __init__(self, tiles, n_tiles, points):
            self.tiles, self.n_tiles, self.points = tiles, n_tiles, points
            self.done = self.passed = 0

        def __enter__(self):
            background.append(self)
            return self

        def point(self, n):
            self.passed += n
            self.upto(self.n_tiles * self.passed // self.points)

        def upto(self, n):
            while self.done < min(n, self.n_tiles):
                next(self.tiles)
                self.done += 1

        def __exit__(self, *failed):
            if not failed[0]:
                self.upto(self.n_tiles)
                for _ in self.tiles:
                    raise AssertionError("tiles left over")
            background.pop()

    def point(n=1):
        for b in background:
            b.point(n)

    def barrier(but=None):
        marks = [x.last() for x in (V, A, G, PE, load, store, *loads, *stores)]
        if not background:
            marks += [x.last() for x in (*pair_read, *outs)] + [(s_mm, used["units"] + 2)]
        for e in (nc.vector, nc.scalar, nc.gpsimd, nc.tensor, nc.sync):
            for s, n in marks:
                if e is not but:
                    e.wait_ge(s, n)

    raw = sb(ctx, "w_raw", [P, 2, KT * P])
    whi = sb(ctx, "w_hi", [P, 2, KT * P], F32R)
    wlo = sb(ctx, "w_lo", [P, 2, KT * P], F32R)
    vec = sb(ctx, "vec", [P, NVEC])
    ident = sb(ctx, "ident", [P, P])
    causal = sb(ctx, "causal", [P, P])
    ones = sb(ctx, "ones", [P, P])
    pair = [ctx.enter_context(nc.psum_tensor(f"pair{i}", [P, L], F32)) for i in range(2)]
    wide = ctx.enter_context(nc.psum_tensor("wide", [P, L], F32))
    bank = [ctx.enter_context(nc.psum_tensor(f"bank{i}", [P, HALF], F32)) for i in (6, 7)]
    act_hi = sb(ctx, "act_hi", [P, KT, L], F32R)
    act_lo = sb(ctx, "act_lo", [P, KT, L], F32R)
    rs = sb(ctx, "rs", [P, L])

    def col(name, i):
        at = VEC[name][0]
        return vec[:, at + i:at + i + 1]

    load.mark(SP.dma_start(vec[:], t["vec"]))
    G.mark(G.then().memset(ident[:], 0.0))
    G.mark(G.then().affine_select(out=ident[:], in_=ident[:], compare_op=ALU.not_equal, fill=1.0, base=0,
                                  pattern=[[-1, P]], channel_multiplier=1))
    G.mark(G.then().memset(causal[:], 0.0))
    G.mark(G.then().affine_select(out=causal[:], in_=causal[:], compare_op=ALU.is_ge, fill=-1e30, base=0,
                                  pattern=[[-1, P]], channel_multiplier=1))
    G.mark(G.then().memset(ones[:], 1.0))

    s_raw = [sem("raw0"), sem("raw1")]
    s_whi = sem("whi")
    s_split = sem("split")
    s_mm = sem("mm")
    for s, e in ((s_whi, nc.scalar), (s_split, nc.gpsimd), (s_mm, nc.tensor)):
        e.sem_inc(s, 2)
    used = {"units": 0, "blocks": 0}

    def split_unit(b, slot, fills):
        nc.scalar.wait_ge(s_raw[slot], 16 * fills)
        nc.scalar.wait_ge(s_mm, b + 1)
        nc.scalar.copy(whi[:, slot, :], raw[:, slot, :]).then_inc(s_whi, 1)
        nc.gpsimd.wait_ge(s_whi, b + 3)
        nc.gpsimd.tensor_tensor(wlo[:, slot, :], raw[:, slot, :], whi[:, slot, :].bitcast(F32),
                                ALU.subtract).then_inc(s_split, 1)

    def fetch_unit(b, slot):
        SP.wait_ge(s_split, b + 1)
        SP.dma_start(raw[:, slot, :], t["stream"][b]).then_inc(s_raw[slot], 16)

    for n in range(2):
        fetch_unit(n, n)
    split_unit(0, 0, 1)
    fetch_unit(2, 0)

    def products(i, base, per_turn, n_out, tiles, rhs, evict):
        packed = n_out * tiles == 8 * per_turn
        for o in range(n_out):
            at = (used["blocks"] + o) % 2
            reads, out_pair = pair_read[at], pair[at]
            for k in range(tiles):
                n = o * tiles + k if packed else 8 * o + k
                w, slot = n % 8, (base + n // 8) % 2
                b = i * per_turn + (base + n // 8)
                if w == 0:
                    split_unit(b + 1, 1 - slot, i * (per_turn // 2) + ((base + n // 8 + 1) // 2 + 1))
                    fetch_unit(b + 3, 1 - slot)
                    nc.tensor.wait_ge(s_split, b + 3)
                if k == 0:
                    nc.tensor.wait_ge(reads.sem, reads.n)
                hi, lo = rhs(o, k)
                w_hi, w_lo = (x[:, slot, w * P:(w + 1) * P] for x in (whi, wlo))
                for n_pass, (wt, a) in enumerate(((w_hi, hi), (w_hi, lo), (w_lo, hi))):
                    for h in range(2):
                        last = nc.tensor.matmul(out_pair[:, h * HALF:(h + 1) * HALF], wt, a[:, h * HALF:(h + 1) * HALF],
                                                start=k == 0 and n_pass == 0, stop=k == tiles - 1 and n_pass == 2)
                if w == 7 or (not packed and k == tiles - 1):
                    last.then_inc(s_mm, 1)
                    ready = (s_mm, b + 3)
                elif k == tiles - 1:
                    ready = PE.mark(last)
                if k < tiles - 1:
                    yield

            evict(i, o, out_pair, ready, reads.mark)
            yield

    def stage(turns, per_turn, n_out, tiles, rhs, evict, per=None):
        if turns == 1:
            for _ in products(0, used["units"], per_turn, n_out, tiles, rhs, evict):
                pass
        else:
            assert per_turn % 2 == 0 and n_out % 2 == 0
            per = dict(per or {})
            per.update({c: n_out // 2 for c in pair_read})
            with loop(nc, turns, per) as i:
                for _ in products(i, used["units"], per_turn, n_out, tiles, rhs, evict):
                    pass
        advance(turns * per_turn, turns * n_out)

    class Ahead:

        def __init__(self, turns):
            self.turns = turns
            self.tiles = products(0, used["units"], 2, 2, KT, act_rhs, lambda *a: self.evict(*a))

        def tile(self, mark):
            PE.after(mark)
            next(self.tiles)

        def run(self, evict, per):
            self.evict = evict
            for _ in self.tiles:
                pass
            advance(2, 2)
            stage(self.turns - 1, 2, 2, KT, act_rhs, lambda i, *a: evict(i + 1, *a), per=per)

    def advance(units, blocks):
        used["units"] += units
        used["blocks"] += blocks

    pair_read = [Count(sem(f"pair_read{n}"), 1) for n in range(2)]
    for c in pair_read:
        nc.vector.sem_inc(c.sem, 1)
        c.n = 1

    def act_rhs(o, k):
        return act_hi[:, k, :], act_lo[:, k, :]

    def split_act(src, hi, lo, mark):
        a = A.mark(A.after(mark).copy(hi, src))
        return V.mark(V.after(a).tensor_tensor(lo, src, hi.bitcast(F32), ALU.subtract))

    def sum_rows(psum, ones_t, tiles, sq, mark):
        done = []
        for n, x in enumerate(tiles):
            a = A.mark(A.after(mark, done[n - 2] if n > 1 else None).activation(sq[:, n % 2, :], x, ACT.Square))
            PE.after(a)
            for h in range(2):
                last = nc.tensor.matmul(psum[:, h * HALF:(h + 1) * HALF], ones_t, sq[:, n % 2, h * HALF:(h + 1) * HALF],
                                        start=n == 0, stop=n == len(tiles) - 1)
            done.append(PE.mark(last))
        return done[-1]

    def inv_sqrt(rstd, psum, scale, mark):
        v = V.mark(V.after(mark).tensor_scalar(rstd, psum, scale, EPS, ALU.mult, ALU.add))
        a = A.mark(A.after(v).activation(rstd, rstd, ACT.Sqrt))
        return V.mark(V.after(a).reciprocal(rstd, rstd))

    def rms_scale(tiles, sq, rstd, scale, mark):
        return inv_sqrt(rstd[:], wide[:], scale, sum_rows(wide, ones[:], tiles, sq, mark))

    def norm_start(x_dram, gain, name, ahead):
        with ExitStack() as at:
            x, sq = sb(at, name + "x", [P, KT, L]), sb(at, name + "s", [P, 2, L])
            arrived = []
            for k in range(KT):
                if k > 1:
                    SP.wait_ge(*arrived[k - 2])
                arrived.append(loads[k % 2].mark(SP.dma_start(x[:, k, :], x_dram[k])))
            done = []
            for k in range(KT):
                split = scaled_split(x[:, k, :], gain, k, arrived[k], sq, done)
                if k < KT - 1:
                    ahead(k, split)
            inv_sqrt(rs[:], wide[:], 1.0 / D, done[-1])
            barrier(but=nc.tensor)
            PE.after(V.last())

    def scaled_split(x, gain, k, mark, sq, done):
        g = col(gain, k)
        a = A.mark(A.after(mark).activation(act_hi[:, k, :], x, ACT.Copy, scale=g))
        split = V.mark(V.after(a).scalar_tensor_tensor(act_lo[:, k, :], x, g, act_hi[:, k, :].bitcast(F32),
                                                       ALU.mult, ALU.subtract))
        a = A.mark(A.after(done[k - 2] if k > 1 else None).activation(sq[:, k % 2, :], x, ACT.Square))
        PE.after(a)
        for h in range(2):
            last = nc.tensor.matmul(wide[:, h * HALF:(h + 1) * HALF], ones[:], sq[:, k % 2, h * HALF:(h + 1) * HALF],
                                    start=k == 0, stop=k == KT - 1)
        done.append(PE.mark(last))
        return split

    def bridge(y, squares, x_dram, gain, out_dram, next_gain, name, ahead=None):
        barrier()
        with ExitStack() as at:
            x, r = sb(at, name + "x", [P, 4, L]), sb(at, name + "r", [P, L])
            sq = sb(at, name + "s", [P, 2, L])
            scaled, added, split, stored = [], [], [], []

            def fetch(k):
                if k > 3 and next_gain:
                    SP.wait_ge(*split[k - 4])
                    SP.wait_ge(*done[k - 4])
                return loads[k % 2].mark(SP.dma_start(x[:, k % 4, :], x_dram[k]))

            done = []
            arrived = [fetch(0), fetch(1)]
            for h in range(2):
                part = slice(h * HALF, (h + 1) * HALF)
                m = PE.mark(nc.tensor.matmul(wide[:, part], ones[:], squares[:, part], start=True, stop=True))
                y_scale = inv_sqrt(r[:, part], wide[:, part], 1.0 / D, m)

            def scale(k):
                scaled.append(V.mark(V.after(y_scale).scalar_tensor_tensor(y[:, k, :], y[:, k, :], col(gain, k), r[:],
                                                                           ALU.mult, ALU.mult)))

            scale(0)
            for k in range(KT):
                xk = x[:, k % 4, :]
                if k < KT - 1:
                    scale(k + 1)
                added.append(G.mark(G.after(scaled[k], arrived[k]).tensor_tensor(xk, xk, y[:, k, :], ALU.add)))
                if next_gain:
                    split.append(scaled_split(xk, next_gain, k, added[k], sq, done))
                    if k < KT - 1:
                        ahead.tile(split[k])
                if k > 1:
                    SP.wait_ge(*stored[k - 2])
                SP.wait_ge(*added[k])
                if k + 2 < KT:
                    arrived.append(fetch(k + 2))
                stored.append(stores[k % 2].mark(SP.dma_start(out_dram[k], xk)))
            if next_gain:
                inv_sqrt(rs[:], wide[:], 1.0 / D, done[-1])
            barrier(but=nc.tensor)
            PE.after(V.last())

    def square_sum(y, sq, squares, mark):
        a = A.mark(A.after(mark, G.last()).activation(sq, y, ACT.Square))
        G.mark(G.after(a).tensor_tensor(squares, squares, sq, ALU.add))

    def to_dram(dst, row, buf, gate=None, n=2, first=0):
        def evict(i, o, psum, ready, read):
            slot = o % 2
            stored = outs[slot].last()
            done = read(V.after(ready, stored).tensor_tensor(buf[:, slot, :], psum[:], rs[:], ALU.mult))
            if gate is not None:
                bias = vec[:, bass.ds(i * n + (VEC[gate][0] + first + o), 1)] if gate else 0.0
                done = A.mark(A.after(done).activation(buf[:, slot, :], buf[:, slot, :], ACT.Sigmoid, bias=bias))
            SP.wait_ge(*done)
            outs[slot].mark(SP.dma_start(dst[i * n + (row + o)], buf[:, slot, :]))
        return evict

    def log1p(x, tmp, mark):
        z, z2 = tmp
        V.mark(V.after(mark).tensor_scalar_add(z, x, 2.0))
        V.mark(V.then().reciprocal(z, z))
        V.mark(V.then().tensor_tensor(z, z, x, ALU.mult))
        V.mark(V.then().tensor_tensor(z2, z, z, ALU.mult))
        V.mark(V.then().memset(x, 2.0 / 17))
        for n in range(15, 0, -2):
            V.mark(V.then().tensor_tensor(x, x, z2, ALU.mult))
            V.mark(V.then().tensor_scalar_add(x, x, 2.0 / n))
        return V.mark(V.then().tensor_tensor(x, x, z, ALU.mult))

    def transposes(dst, src, n, width, src_mark, rows=P, free=None, between=None):
        done = free
        for j0 in range(0, n, 4):
            m = min(4, n - j0)
            if between:
                between()
            PE.after(src_mark, done)
            for j in range(m):
                dst_j = bank[0][:, j * width:(j + 1) * width]
                if rows == P:
                    last = nc.tensor.transpose(dst_j, src(j0 + j), ident[:])
                else:
                    last = nc.tensor.matmul(dst_j, src(j0 + j), ident[0:rows, 0:rows], start=True, stop=True)
            ready = PE.mark(last)
            done = A.mark(A.after(ready).copy(dst[:, j0:j0 + m, :], bank[0][:, 0:m * width]
                                              .rearrange("p (j n) -> p j n", j=m)))
        return done

    def short_conv(at):
        xin, gb, gc = (sb(at, "cv" + n, [P, L]) for n in "xbc")
        y = sb(at, "cvy", [P, L])

        def fetch(i):
            for buf, row in ((xin, X_), (gb, B_), (gc, C_)):
                loads[0].mark(SP.dma_start(buf[:], proj1[i + row]))

        def tile(i):
            arrived = loads[0].last()

            def w(tap):
                return vec[:, bass.ds(i + (VEC["conv_w"][0] + tap * 4), 1)]

            V.mark(V.after(arrived).tensor_tensor(xin[:], gc[:], xin[:], ALU.mult))
            V.mark(V.then(stores[1].last()).tensor_scalar(y[:], xin[:], w(2), None, ALU.mult))
            for back in (1, 2):
                V.mark(V.then().scalar_tensor_tensor(y[:, back:], xin[:, :L - back], w(2 - back), y[:, back:],
                                                     ALU.mult, ALU.add))
            v = V.mark(V.then().tensor_tensor(y[:], y[:], gb[:], ALU.mult))
            SP.wait_ge(*v)
            stores[1].mark(SP.dma_start(mixed1[i + 4], y[:]))
        return fetch, tile

    def attention(heads, in_turn, tiles, src, rows, mixed, row0, head_bias, add_bias, name, per, woven, extra=None):
        barrier()
        halves = src.rearrange("b (h p) n -> (b h) p n", h=2)
        out_h = mixed.rearrange("b (h p) n -> (b h) p n", h=2)
        with ExitStack() as at:
            q, k, v = (sb(at, name + n, [HD, L]) for n in "qkv")
            vt = sb(at, name + "vt", [P, L // P, HD])
            s = sb(at, name + "s", [P, 2, L])
            pt = sb(at, name + "pt", [P, 2, L])
            ot = sb(at, name + "ot", [P, L // P, HD])
            o = sb(at, name + "o", [HD, L])
            st = sb(at, name + "st", [P, 2, 3])
            bias = head_bias(at)

            def head(i, aside=None):
                for buf, row in ((q, rows[0]), (k, rows[1]), (v, rows[2])):
                    load.mark(SP.dma_start(buf[:], halves[i + 2 * row]))
                bias_ready = bias[1](i)
                arrived = load.last()
                if aside:
                    aside()
                point(4)
                copied = transposes(vt, lambda j: v[:, j * P:(j + 1) * P], L // P, HD, arrived, rows=HD)
                scores_read, o_read, pend = None, None, None
                pv_done = []

                def weigh(n, k0, nk, e):
                    sl = n % 2
                    copied = transposes(pt[:, sl, :].rearrange("p (j n) -> p j n", n=P),
                                        lambda j: s[:, sl, j * P:(j + 1) * P], nk, P, e, free=weigh.copied, between=point)
                    weigh.copied = copied
                    if nk > 3:
                        point()
                    PE.after(copied, o_read)
                    for j in range(nk):
                        last = nc.tensor.matmul(bank[1][:, 0:HD], pt[:, sl, j * P:(j + 1) * P], vt[:, k0 // P + j, :],
                                                start=j == 0, stop=j == nk - 1)
                    pv_done.append(PE.mark(last))

                def scale(n):
                    sl = n % 2
                    V.mark(V.after(pv_done[n]).reciprocal(st[:, sl, 2:3], st[:, sl, 1:2]))
                    return V.mark(V.then().tensor_scalar(ot[:, n, :], bank[1][:, 0:HD], st[:, sl, 2:3], None, ALU.mult))

                weigh.copied = copied
                for n, (q0, k0, k1) in enumerate(tiles):
                    w, sl = k1 - k0, n % 2
                    PE.after(arrived, scores_read)
                    for c in range(0, w, HALF):
                        e = min(w, c + HALF)
                        last = nc.tensor.matmul(wide[:, c:e], q[:, q0:q0 + P], k[:, k0 + c:k0 + e], start=True, stop=True)
                    ready = PE.mark(last)
                    if pend:
                        weigh(*pend)
                    sc = s[:, sl, 0:w]
                    V.after(ready, bias_ready, pv_done[n - 2] if n > 1 else None)
                    scores_read = add_bias(sc, wide[:, 0:w], bias[0], q0, k0, k1)
                    V.mark(V.then().reduce_max(st[:, sl, 0:1], sc, AX.X))
                    x = V.mark(V.then().tensor_scalar(st[:, sl, 0:1], st[:, sl, 0:1], -1.0, None, ALU.mult))
                    if pend:
                        o_read = scale(n - 1)
                    x = A.mark(A.after(x).activation(sc, sc, ACT.Exp, bias=st[:, sl, 0:1], accum_out=st[:, sl, 1:2]))
                    pend = (n, k0, w // P, x)
                for _ in range(3):
                    point()
                weigh(*pend)
                scaled = scale(n)
                PE.after(scaled, scores_read)
                for n in range(L // P):
                    last = nc.tensor.matmul(wide[0:HD, n * P:(n + 1) * P], ot[:, n, :], ident[:], start=True, stop=True)
                v_o = V.mark(V.after(PE.mark(last), stores[0].last()).tensor_copy(o[:], wide[0:HD, :]))
                SP.wait_ge(*v_o)
                stores[0].mark(SP.dma_start(out_h[i + 2 * row0], o[:]))
                PE.after(v_o)

            beside = extra(at) if extra else None
            with loop(nc, heads // in_turn, per) as i, woven(i):
                if beside:
                    beside[0](i)
                for n in range(in_turn):
                    head(i * in_turn + n, (lambda: beside[1](i)) if beside and n == in_turn - 1 else None)
            barrier()

    def fox_logs():
        barrier()
        n_log = L * FOX_HEADS // P
        with ExitStack() as at:
            f, e, z, z2 = (sb(at, "fx" + n, [P, n_log]) for n in ("f", "e", "z", "y"))
            cum, one = sb(at, "fx_cum", [FOX_HEADS, L]), sb(at, "fx_one", [FOX_HEADS, L])
            for o in outs:
                SP.wait_ge(*o.last())
            a = load.mark(SP.dma_start(f[:], proj1[F_, 0:FOX_HEADS, :].rearrange("h (a n) -> (h a) n", a=16)))
            v = V.mark(V.after(a).tensor_scalar(f[:], f[:], col("b_f", 0), None, ALU.add))
            a = A.mark(A.after(v).activation(e[:], f[:], ACT.Abs))
            a = A.mark(A.then().activation(e[:], e[:], ACT.Exp, scale=-1.0))
            log1p(e[:], (z[:], z2[:]), a)
            V.mark(V.then().tensor_scalar(f[:], f[:], 0.0, None, ALU.min))
            v = V.mark(V.then().tensor_tensor(f[:], f[:], e[:], ALU.subtract))
            SP.wait_ge(*v)
            s = store.mark(SP.dma_start(fox_log, f[:]))
            SP.wait_ge(*s)
            a = load.mark(SP.dma_start(cum[:], fox_log.rearrange("(h a) n -> h (a n)", h=FOX_HEADS)))
            V.mark(V.then().memset(one[:], 1.0))
            v = V.mark(V.then(a).tensor_tensor_scan(cum[:], one[:], cum[:], 0.0, ALU.mult, ALU.add))
            SP.wait_ge(*v)
            store.mark(SP.dma_start(fox_cum, cum[:]))
            barrier()

    def fox(woven):
        def head_bias(at):
            cb = sb(at, "fx_cb", [P, L])
            return cb, lambda i: load.mark(SP.dma_start(cb[:], fox_cum[i].partition_broadcast(P)))

        def add_bias(sc, psum, cb, q0, k0, k1):
            v = V.mark(nc.vector.scalar_tensor_tensor(sc, psum, HD ** -0.5, cb[:, k0:k1], ALU.mult, ALU.subtract))
            V.mark(V.then().tensor_tensor(sc[:, k1 - k0 - P:], sc[:, k1 - k0 - P:], causal[:], ALU.add))
            return v

        attention(FOX_HEADS, 2, [(n * P, 0, (n + 1) * P) for n in range(8)], proj1, (Q_, K_, V_), mixed1, 8,
                  head_bias, add_bias, "fox", {V: 103, A: 50, PE: 62, load: 128, loads[0]: 48, stores[0]: 32,
                                               stores[1]: 16, outs[0]: 48, outs[1]: 48, pair_read[0]: 3,
                                               pair_read[1]: 3}, woven, short_conv)

    def band(woven):
        with ExitStack() as outer:
            edge = sb(outer, "bd_edge", [P, BAND])
            barrier()
            G.mark(G.then().memset(edge[:], 0.0))
            G.mark(G.then().memset(edge[0:64, LEFT + 64:], -1e30))
            G.mark(G.then().memset(edge[64:P, 0:64], -1e30))
            barrier()

            def head_bias(at):
                rel = sb(at, "bd_rel", [P, BAND])

                def ready(i):
                    got = load.mark(SP.dma_start(rel[:], t["rel"][i]))
                    return V.mark(V.after(got).tensor_tensor(rel[:], rel[:], edge[:], ALU.add))
                return rel, ready

            def add_bias(sc, psum, rel, q0, k0, k1):
                off = k0 - (q0 - LEFT)
                return V.mark(nc.vector.scalar_tensor_tensor(sc, psum, HD ** -0.5, rel[:, off:], ALU.mult, ALU.add))

            attention(BAND_HEADS, 2, [(n * P, max(0, n * P - LEFT), (n + 1) * P) for n in range(8)], proj2,
                      (AQ, AK, AV), mixed2, 0, head_bias, add_bias, "band",
                      {V: 84, A: 44, PE: 62, load: 128, stores[0]: 32, outs[0]: 64, outs[1]: 64, pair_read[0]: 4,
                       pair_read[1]: 4}, woven)

    def s5(w):
        barrier()
        RE, IM = 0, 1
        with ExitStack() as keep:
            wl = sb(keep, "s5_wl", [P, PAIRS, 2, P])
            cl = sb(keep, "s5_cl", [P, PAIRS, 2, T + 1, S5_H])
            dl = sb(keep, "s5_dl", [P, S5_G, P])
            scan = sb(keep, "s5_scan", [P, LEVELS, 3, PAIRS])
            with ExitStack() as at:
                pw = sb(at, "s5_pw", [P, T + 1, 2, PAIRS])
                tm = sb(at, "s5_tm", [P, 12, PAIRS])
                bb = sb(at, "s5_b", [P, 4, PAIRS, S5_H])
                cc = sb(at, "s5_c", [P, 2, PAIRS, S5_H])
                tmp = sb(at, "s5_tmp", [P, 2, PAIRS, S5_H])
                dg = sb(at, "s5_dg", [S5_H, S5_G])
                load.mark(SP.dma_start(bb[:, 0:2, :, :], t["s5_b"]))
                load.mark(SP.dma_start(cc[:], t["s5_c"]))
                got = load.mark(SP.dma_start(dg[:], t["s5_d"]))
                a_re, a_im, log_dt = (vec[:, VEC[n][0]:VEC[n][0] + PAIRS] for n in ("a_re", "a_im", "log_dt"))

                def tt(o, x, y, op):
                    point()
                    return V.mark(V.then().tensor_tensor(o, x, y, op))

                def ts(o, x, s1, op, s2=None, op2=None):
                    if op2 is None:
                        return V.mark(V.then().tensor_scalar(o, x, s1, None, op))
                    return V.mark(V.then().tensor_scalar(o, x, s1, s2, op, op2))

                def cmul(ore, oim, xre, xim, yre, yim, t0, t1):
                    tt(t0, xre, yre, ALU.mult)
                    tt(t1, xim, yim, ALU.mult)
                    tt(ore, t0, t1, ALU.subtract)
                    tt(t0, xre, yim, ALU.mult)
                    tt(t1, xim, yre, ALU.mult)
                    return tt(oim, t0, t1, ALU.add)

                r = [tm[:, n, :] for n in range(12)]
                V.after(got)
                lre, dt, ang, turn, mag, cos, sin = r[0:7]
                ts(lre, a_re, -1e-4, ALU.min)
                a = A.mark(A.after(V.last()).activation(dt, log_dt, ACT.Exp))
                V.after(a)
                tt(mag, lre, dt, ALU.mult)
                a = A.mark(A.after(V.last()).activation(mag, mag, ACT.Exp))
                tt(ang, a_im, dt, ALU.mult)
                ts(turn, ang, 1.0 / (2 * math.pi), ALU.mult)
                ts(turn, turn, 12582912.0, ALU.add)
                ts(turn, turn, 12582912.0, ALU.subtract)
                for part in (6.28125, 1.9353071693331003e-3, 1.0253259e-11):
                    V.mark(V.then().scalar_tensor_tensor(ang, turn, -part, ang, ALU.mult, ALU.add))
                ts(ang, ang, 3.1415925, ALU.min, -3.1415925, ALU.max)
                a = A.mark(A.after(V.last()).activation(sin, ang, ACT.Sin))
                a = A.mark(A.then().activation(cos, ang, ACT.Abs))
                V.after(a)
                ts(cos, cos, -1.0, ALU.mult, math.pi / 2, ALU.add)
                a = A.mark(A.after(V.last()).activation(cos, cos, ACT.Sin))
                V.after(a)
                V.mark(V.then().memset(pw[:, 0, RE, :], 1.0))
                V.mark(V.then().memset(pw[:, 0, IM, :], 0.0))
                tt(pw[:, 1, RE, :], mag, cos, ALU.mult)
                tt(pw[:, 1, IM, :], mag, sin, ALU.mult)
                for j in range(2, T + 1):
                    cmul(pw[:, j, RE, :], pw[:, j, IM, :], pw[:, j - 1, RE, :], pw[:, j - 1, IM, :],
                         pw[:, 1, RE, :], pw[:, 1, IM, :], r[7], r[8])
                V.mark(V.then().tensor_copy(scan[:, 0, 0:2, :], pw[:, T, :, :]))
                for n in range(1, LEVELS):
                    cmul(scan[:, n, RE, :], scan[:, n, IM, :], scan[:, n - 1, RE, :], scan[:, n - 1, IM, :],
                         scan[:, n - 1, RE, :], scan[:, n - 1, IM, :], r[7], r[8])
                nre, d, cre, cim, nim = r[7], r[8], r[9], r[10], r[11]
                tt(d, lre, lre, ALU.mult)
                tt(nim, a_im, a_im, ALU.mult)
                tt(d, d, nim, ALU.add)
                V.mark(V.then().reciprocal(d, d))
                ts(nre, pw[:, 1, RE, :], 1.0, ALU.subtract)
                tt(cre, nre, lre, ALU.mult)
                tt(nim, pw[:, 1, IM, :], a_im, ALU.mult)
                tt(cre, cre, nim, ALU.add)
                tt(cim, pw[:, 1, IM, :], lre, ALU.mult)
                tt(nim, nre, a_im, ALU.mult)
                tt(cim, cim, nim, ALU.subtract)
                tt(cre, cre, d, ALU.mult)
                tt(cim, cim, d, ALU.mult)

                def over_h(x):
                    return x.unsqueeze(2).to_broadcast([P, PAIRS, S5_H])

                t0, t1 = tmp[:, 0, :, :], tmp[:, 1, :, :]
                cmul(bb[:, 2, :, :], bb[:, 3, :, :], bb[:, 0, :, :], bb[:, 1, :, :], over_h(cre), over_h(cim), t0, t1)
                short = ExitStack()
                wp = sb(short, "s5_wp", [P, 2, PAIRS, T, S5_H])
                for j in range(T):
                    cmul(wp[:, RE, :, j, :], wp[:, IM, :, j, :], bb[:, 2, :, :], bb[:, 3, :, :],
                         over_h(pw[:, T - 1 - j, RE, :]), over_h(pw[:, T - 1 - j, IM, :]), t0, t1)
                for j in range(T + 1):
                    cmul(cl[:, :, RE, j, :], cl[:, :, IM, j, :], cc[:, 0, :, :], cc[:, 1, :, :],
                         over_h(pw[:, j, RE, :]), over_h(pw[:, j, IM, :]), t0, t1)
                    ts(cl[:, :, IM, j, :], cl[:, :, IM, j, :], -1.0, ALU.mult)
                v = V.last()
                wl_ready = transposes(wl[:].rearrange("p a c n -> p (a c) n"),
                                      lambda j: wp[:, j % 2, j // 2, :, :].rearrange("p a b -> p (a b)"),
                                      2 * PAIRS, P, v)
                short.close()
                kp = sb(at, "s5_kp", [S5_H, S5_G, 2 * T - 1, S5_H])
                V.mark(V.then(wl_ready).memset(kp[:, :, 0:T - 1, :], 0.0))
                copied = wl_ready
                for p0 in range(0, PAIRS, 4):
                    PE.after(v, copied)
                    for pr in range(p0, p0 + 4):
                        for g in range(2):
                            row = S5_P * g
                            for c in (RE, IM):
                                last = nc.tensor.matmul(bank[g][0:S5_H, (pr - p0) * P:(pr - p0 + 1) * P],
                                                        bb[row:row + S5_P, 2 + c, pr, :],
                                                        cl[row:row + S5_P, pr, c, 0:T, :].rearrange("p a b -> p (a b)"),
                                                        start=c == RE, stop=c == IM)
                    ready = PE.mark(last)
                    for g in range(2):
                        copied = V.mark(V.after(ready).tensor_copy(
                            kp[:, 2 * p0 + g:2 * p0 + 8:2, T - 1:, :].rearrange("p g a b -> p g (a b)"),
                            bank[g][0:S5_H, :].rearrange("p (g n) -> p g n", g=4)))
                skip = tmp[0:S5_H, :, :, :].rearrange("p a b c -> p (a b) c")
                tt(skip, ident[0:S5_H, 0:S5_H].unsqueeze(1).to_broadcast([S5_H, S5_G, S5_H]),
                   dg[:].unsqueeze(2).to_broadcast([S5_H, S5_G, S5_H]), ALU.mult)
                v = tt(kp[:, :, T - 1, :], kp[:, :, T - 1, :], skip, ALU.add)
                SP.wait_ge(*v)
                for j in range(T):
                    load.mark(SP.dma_start(dl[j * S5_H:(j + 1) * S5_H, :, :].rearrange("p g (a b) -> p g a b", a=T),
                                           kp[:, :, T - 1 - j:2 * T - 1 - j, :]))
                barrier()
            w.upto(5 * KT)
            fox_logs()
            point(40)
            with ExitStack() as at:
                u = sb(at, "s5_ut", [P, 2, L])
                uc = sb(at, "s5_uc", [P, S5_G, CH])
                x = [[sb(at, f"s5_x{c}", [P, PAIRS, CH]) for c in "ri"], [wl[:, :, c, :] for c in range(2)]]
                for o in outs:
                    SP.wait_ge(*o.last())
                for n in range(4):
                    s = n % 2
                    SP.wait_ge(*stores[s].last())
                    a = loads[s].mark(SP.dma_start(u[:, s, :], proj1[U_ + n]))
                    v = V.mark(V.after(a).tensor_copy(x[0][s][:, 0:T, :], u[:, s, :].rearrange("p (m j) -> p j m", j=T)))
                    SP.wait_ge(*v)
                    stores[s].mark(SP.dma_start(s5_u.rearrange("(n p) j m -> n p j m", p=P)[n], x[0][s][:, 0:T, :]))
                for s in stores:
                    SP.wait_ge(*s.last())
                for j in range(T):
                    got = load.mark(SP.dma_start(uc[j * S5_H:(j + 1) * S5_H, :, :],
                                                 s5_u[:, j, :].rearrange("(g h) m -> h g m", h=S5_H)))
                read = V.last()
                for pr in range(0, PAIRS, 4):
                    for c in (RE, IM):
                        point()
                        PE.after(got, read)
                        for n in range(4):
                            for g in range(2):
                                last = nc.tensor.matmul(bank[c][g * S5_P:(g + 1) * S5_P, n * CH:(n + 1) * CH],
                                                        wl[:, pr + n, c, g * S5_P:(g + 1) * S5_P],
                                                        uc[:, 2 * (pr + n) + g, :], start=True, stop=True)
                        ready = PE.mark(last)
                        read = V.mark(V.after(ready).tensor_copy(
                            x[0][c][:, pr:pr + 4, :], bank[c][:].rearrange("p (n m) -> p n m", n=4)))
                t0, t1 = (u[:, n, :].rearrange("p (a b) -> p a b", a=8) for n in range(2))
                for n in range(LEVELS):
                    sh = 1 << n
                    old, new = x[n % 2], x[(n + 1) % 2]
                    w = CH - sh
                    for c in range(2):
                        V.mark(V.then().tensor_copy(new[c][:, :, 0:sh], old[c][:, :, 0:sh]))
                    for half in range(2):
                        p0, p1 = half * 8, half * 8 + 8
                        ar, ai = (scan[:, n, c, p0:p1].unsqueeze(2).to_broadcast([P, 8, w]) for c in range(2))
                        xr, xi = (old[c][:, p0:p1, 0:w] for c in range(2))
                        for c, (f0, f1, op) in enumerate((((xr, ar), (xi, ai), ALU.subtract),
                                                          ((xi, ar), (xr, ai), ALU.add))):
                            for _ in range(4):
                                point()
                            V.mark(V.then().tensor_tensor(t0[:, :, 0:w], *f0, ALU.mult))
                            V.mark(V.then().tensor_tensor(t1[:, :, 0:w], *f1, ALU.mult))
                            V.mark(V.then().tensor_tensor(t0[:, :, 0:w], t0[:, :, 0:w], t1[:, :, 0:w], op))
                            V.mark(V.then().tensor_tensor(new[c][:, p0:p1, sh:], old[c][:, p0:p1, sh:],
                                                          t0[:, :, 0:w], ALU.add))
                state = x[LEVELS % 2]
                scanned = V.last()
                y = [x[(LEVELS + 1) % 2][c][:] for c in range(2)]
                read = None
                for p0 in range(0, PAIRS, 4):
                    point()
                    PE.after(scanned, read)
                    for pr in range(p0, p0 + 4):
                        for g in range(2):
                            row, o, ps = S5_P * g, (pr - p0) * CH, bank[g]
                            nc.tensor.matmul(ps[:, o:o + CH], dl[:, 2 * pr + g, :], uc[:, 2 * pr + g, :],
                                             start=True, stop=False)
                            for c in (RE, IM):
                                last = nc.tensor.matmul(ps[:, o + 1:o + CH],
                                                        cl[row:row + S5_P, pr, c, 1:, :].rearrange("p a b -> p (a b)"),
                                                        state[c][row:row + S5_P, pr, 0:CH - 1],
                                                        start=False, stop=c == IM)
                    ready = PE.mark(last)
                    for g in range(2):
                        g0 = 2 * p0 % 16 + g
                        read = V.mark(V.after(ready).tensor_copy(y[p0 // 8][:, g0:g0 + 7:2, :],
                                                                 bank[g][:].rearrange("p (n m) -> p n m", n=4)))
                SP.wait_ge(*read)
                s5_y_v = s5_y.rearrange("(c g h) j m -> c j h g m", c=2, h=S5_H)
                for c in range(2):
                    for j in range(T):
                        store.mark(SP.dma_start(s5_y_v[c, j], y[c][j * S5_H:(j + 1) * S5_H, :, :]))
                SP.wait_ge(*store.last())
                barrier()
                z, gates = ([uc[:, g + T * c:g + T * c + T, :].rearrange("p a b -> p (a b)") for c in range(2)]
                            for g in (0, 2 * T))
                glu = sb(at, "s5_glu", [P, 4, P])
                w_here = load.mark(SP.dma_start(glu[:], t["glu"].rearrange("n p k -> p n k")))
                read = None
                for n in range(4):
                    s = n % 2
                    for _ in range(8):
                        point()
                    SP.wait_ge(*V.last())
                    a = loads[s].mark(SP.dma_start(z[s], s5_y.rearrange("(n p) j m -> n p (j m)", p=P)[n]))
                    a = A.mark(A.after(a).activation(z[s], z[s], ACT.Gelu_apprx_tanh))
                    PE.after(a, w_here, read)
                    for h in range(2):
                        last = nc.tensor.matmul(wide[:, h * HALF:(h + 1) * HALF], glu[:, n, :],
                                                z[s][:, h * HALF:(h + 1) * HALF], start=True, stop=True)
                    ready = PE.mark(last)
                    read = A.mark(A.after(ready).activation(gates[s], wide[:], ACT.Sigmoid))
                    v = V.mark(V.after(read, stores[s].last()).tensor_tensor(
                        u[:, s, :].rearrange("p (m j) -> p j m", j=T), z[s].rearrange("p (j m) -> p j m", j=T),
                        gates[s].rearrange("p (j m) -> p j m", j=T), ALU.mult))
                    SP.wait_ge(*v)
                    stores[s].mark(SP.dma_start(mixed1[n], u[:, s, :]))
                barrier()

    def hgrn(woven):
        barrier()
        NT = L // P
        with ExitStack() as at:
            q, f, vi, g, kf, b, e, t0, t1, o = (sb(at, "hg_" + n, [P, L]) for n in
                                                ("q", "f", "v", "g", "k", "b", "e", "t0", "t1", "o"))
            sc = sb(at, "hg_sc", [P, NT, 2, P])
            masks = sb(at, "hg_mask", [P, LEVELS + 1, P])
            reset = sb(at, "hg_reset", [P, L])
            vt, kt = sb(at, "hg_vt", [P, NT, P]), sb(at, "hg_kt", [P, NT, P])
            st = sb(at, "hg_st", [P, NT + 1, HD])
            dec = sb(at, "hg_dec", [P, NT])
            heads = sb(at, "hg_heads", [P, P])
            lb = sb(at, "hg_lb", [P, 3, 2])
            for n in range(LEVELS):
                w = P >> (n + 1)
                m = masks[:, n, :].rearrange("p (a b c) -> p a b c", b=2, c=w)[:, :, 1, :]
                G.mark(G.then().memset(masks[:, n, :], 0.0))
                G.mark(G.then().memset(m, 1.0))
                G.mark(G.then().affine_select(out=m, in_=m, compare_op=ALU.is_ge, fill=0.0, base=0,
                                              pattern=[[-2 * w, P // (2 * w)], [0, w]], channel_multiplier=1))
                G.mark(G.then().affine_select(out=m, in_=m, compare_op=ALU.is_ge, fill=0.0, base=w - 1,
                                              pattern=[[2 * w, P // (2 * w)], [0, w]], channel_multiplier=-1))
            G.mark(G.then().tensor_copy(masks[:, LEVELS, :], ident[:]))
            G.mark(G.then().memset(reset[:], 1.0))
            G.mark(G.then().memset(reset[:].rearrange("p (a b) -> p a b", b=P)[:, :, 0:1], 0.0))
            G.mark(G.then().memset(heads[:], 0.0))
            G.mark(G.then().memset(heads[0:HD, 0:HD], 1.0))
            G.mark(G.then().memset(heads[HD:P, HD:P], 1.0))
            G.mark(G.then().memset(st[:, 0, :], 0.0))
            x, oml, tmp = lb[:, 0, :], lb[:, 1, :], lb[:, 2, :]
            logits = vec[:, VEC["lb"][0]:VEC["lb"][0] + 2]
            v = V.mark(nc.vector.tensor_tensor(x, logits, logits, ALU.subtract))
            a = A.mark(A.after(v).activation(x, x, ACT.Exp))
            V.mark(V.after(a).reciprocal(tmp, x))
            V.mark(V.then().tensor_tensor(tmp, tmp, x, ALU.mult))
            V.mark(V.then().tensor_tensor(x, tmp, tmp, ALU.subtract))
            V.mark(V.then().tensor_scalar(oml, x, -1.0, 1.0, ALU.mult, ALU.add))
            barrier()

            def tt(out, x, y, op, *after):
                point()
                return V.mark(V.then(*after).tensor_tensor(out, x, y, op))

            def act(out, x, fn, *after, **kw):
                point()
                return A.mark(A.then(V.last(), *after).activation(out, x, fn, **kw))

            per = {V: 83, A: 34, G: 28, PE: 39, load: 64, stores[0]: 16, outs[0]: 96, outs[1]: 96,
                   pair_read[0]: 6, pair_read[1]: 6}
            with loop(nc, 2, per) as i, woven(i):
                for m in (V, A, G, PE):
                    SP.wait_ge(*m.last())
                for buf, row in ((q, BQ), (f, BF), (vi, BI), (g, BG)):
                    load.mark(SP.dma_start(buf[:], proj2[i + row]))
                got = load.last()
                V.after(got)
                lbc, omc = (lb[:, n, bass.ds(i, 1)] for n in range(2))
                act(q[:], q[:], ACT.Silu, got)
                act(g[:], g[:], ACT.Silu)
                act(kf[:], f[:], ACT.Sigmoid, scale=-1.0)
                a = act(f[:], f[:], ACT.Sigmoid)
                V.mark(V.then(a).tensor_scalar(kf[:], kf[:], omc, None, ALU.mult))
                V.mark(V.then().tensor_scalar(f[:], f[:], omc, lbc, ALU.mult, ALU.add))
                V.mark(V.then().tensor_scalar(t0[:], f[:], LOG_FLOOR, 2.0 ** -60, ALU.max, ALU.max))
                V.mark(V.then().tensor_scalar(t1[:], f[:], LOG_FLOOR, 2.0 ** 60, ALU.max, ALU.mult))
                V.mark(V.then().tensor_scalar(t1[:], t1[:], 1.0, None, ALU.min))
                act(t0[:], t0[:], ACT.Ln)
                a = act(t1[:], t1[:], ACT.Ln)
                tt(t0[:], t0[:], t1[:], ALU.add, a)
                V.mark(V.then().tensor_tensor_scan(b[:], reset[:], t0[:], 0.0, ALU.mult, ALU.add))
                for n in range(LEVELS + 1):
                    if n < LEVELS:
                        w = P >> (n + 1)
                        b4, e4 = (x[:].rearrange("p (a c w) -> p a c w", c=2, w=w) for x in (b, e))
                        mid = b4[:, :, 0, w - 1:w].to_broadcast([P, L // (2 * w), w])
                        PE_done = PE.last()
                        tt(e4[:, :, 1, :], b4[:, :, 1, :], mid, ALU.subtract)
                        tt(e4[:, :, 0, :], mid, b4[:, :, 0, :], ALU.subtract)
                        a = act(e[:], e[:], ACT.Exp)
                        tt(t0[:], q[:], e[:], ALU.mult, a, PE_done)
                        ready = tt(t1[:], kf[:], e[:], ALU.mult)
                        qx, kx = t0, t1
                    else:
                        ready, (qx, kx) = V.last(), (q, kf)
                    for n2 in range(4):
                        ps = (wide[:, 0:HALF], wide[:, HALF:L], bank[0][:], bank[1][:])[n2]
                        PE.after(ready, sc_read[n2] if n else None)
                        for m in range(4):
                            tile, h = 4 * (n2 // 2) + m, n2 % 2
                            last = nc.tensor.matmul(ps[:, m * P:(m + 1) * P],
                                                    kx[h * HD:(h + 1) * HD, tile * P:(tile + 1) * P],
                                                    qx[h * HD:(h + 1) * HD, tile * P:(tile + 1) * P],
                                                    start=True, stop=True)
                        pr = PE.mark(last)
                        dst = sc[:, 4 * (n2 // 2):4 * (n2 // 2) + 4, n2 % 2, :]
                        src = ps.rearrange("p (m n) -> p m n", n=P)
                        mk = masks[:, n, :].unsqueeze(1).to_broadcast([P, 4, P])
                        if n == 0:
                            sc_read[n2] = tt(dst, src, mk, ALU.mult, pr)
                        else:
                            part = o[:, (n2 % 2) * HALF:(n2 % 2 + 1) * HALF].rearrange("p (m n) -> p m n", n=P)
                            sc_read[n2] = tt(part, src, mk, ALU.mult, pr, sc_add[n2 % 2])
                            sc_add[n2 % 2] = G.mark(G.then(sc_read[n2]).tensor_tensor(dst, dst, part, ALU.add))
                    if n == 0:
                        sc_add[0] = sc_add[1] = V.last()
                b3, t3 = (x[:].rearrange("p (a n) -> p a n", n=P) for x in (b, t1))
                blast = b3[:, :, P - 1:P]
                tt(t3, blast.to_broadcast([P, NT, P]), b3, ALU.subtract, PE.last())
                act(t1[:], t1[:], ACT.Exp)
                act(e[:], b[:], ACT.Exp)
                a = act(dec[:], blast.rearrange("p a n -> p (a n)"), ACT.Exp)
                tt(t1[:], t1[:], kf[:], ALU.mult, a)
                ready = tt(t0[:], q[:], e[:], ALU.mult)
                transposes(vt, lambda j: vi[:, j * P:(j + 1) * P], NT, P, ready)
                done = transposes(kt, lambda j: t1[:, j * P:(j + 1) * P], NT, P, A.last())
                PE.after(done)
                for n in range(NT):
                    for h in range(2):
                        last = nc.tensor.matmul(bank[1][h * HD:(h + 1) * HD, n * HD:(n + 1) * HD],
                                                kt[:, n, h * HD:(h + 1) * HD], vt[:, n, h * HD:(h + 1) * HD],
                                                start=True, stop=True)
                pr = PE.mark(last)
                V.after(pr)
                for n in range(NT):
                    point()
                    V.mark(V.then().scalar_tensor_tensor(st[:, n + 1, :], st[:, n, :], dec[:, n:n + 1],
                                                         bank[1][:, n * HD:(n + 1) * HD], ALU.mult, ALU.add))
                PE.after(V.last(), sc_add[0], sc_add[1])
                for n in range(NT):
                    for h in range(2):
                        row = slice(h * HD, (h + 1) * HD)
                        nc.tensor.matmul(wide[row, n * P:(n + 1) * P], vt[:, n, row], sc[:, n, h, :],
                                         start=True, stop=False)
                        last = nc.tensor.matmul(wide[row, n * P:(n + 1) * P], st[row, n, :], t0[row, n * P:(n + 1) * P],
                                                start=False, stop=True)
                pr = PE.mark(last)
                v = V.mark(V.then(pr).tensor_copy(o[:], wide[:]))
                a = act(t1[:], o[:], ACT.Square)
                PE.after(a)
                for h in range(2):
                    last = nc.tensor.matmul(wide[:, h * HALF:(h + 1) * HALF], heads[:], t1[:, h * HALF:(h + 1) * HALF],
                                            start=True, stop=True)
                inv_sqrt(e[:], wide[:], 1.0 / HD, PE.mark(last))
                gain = vec[:, bass.ds(i + VEC["hgrn_g"][0], 1)]
                V.mark(V.then().scalar_tensor_tensor(o[:], o[:], gain, e[:], ALU.mult, ALU.mult))
                v = tt(o[:], o[:], g[:], ALU.mult)
                SP.wait_ge(*v)
                st_ = stores[0].mark(SP.dma_start(mixed2[i + 2], o[:]))
                V.after(st_)
            barrier()

    sc_read, sc_add = {}, {}

    def gmlp():
        barrier()
        NT = L // P
        with ExitStack() as at:
            u, v = sb(at, "gm_u", [P, 2, L]), sb(at, "gm_v", [P, 2, L])
            sq, rstd = sb(at, "gm_sq", [P, 2, L]), sb(at, "gm_r", [P, L])
            vt = sb(at, "gm_vt", [P, 2, NT, P])
            w, b = sb(at, "gm_w", [P, 4, P]), sb(at, "gm_b", [P, 2, P])
            load.mark(SP.dma_start(u[:], proj2[CU:CU + 2].rearrange("k p n -> p k n")))
            load.mark(SP.dma_start(v[:], proj2[CV:CV + 2].rearrange("k p n -> p k n")))
            load.mark(SP.dma_start(w[:], t["gm_w"].rearrange("g q p -> q g p")))
            for g in range(4):
                got = load.mark(SP.dma_start(b[(g % 2) * HD:(g % 2 + 1) * HD, g // 2, :],
                                             t["gm_b"][g].partition_broadcast(HD)))
            causal_w = G.mark(G.after(got).affine_select(out=w[:], in_=w[:], compare_op=ALU.is_ge, fill=0.0, base=0,
                                                         pattern=[[0, 4], [1, P]], channel_multiplier=-1))
            A.mark(A.after(got).activation(v[:], v[:], ACT.Gelu_apprx_tanh))
            a = A.mark(A.then().activation(u[:], u[:], ACT.Gelu_apprx_tanh))
            r = rms_scale([v[:, 0, :], v[:, 1, :]], sq, rstd, 1.0 / 256, a)
            for _ in range(6):
                point()
            for k in range(2):
                n = V.mark(V.after(r).scalar_tensor_tensor(v[:, k, :], v[:, k, :], col("gmlp_g", k), rstd[:],
                                                           ALU.mult, ALU.mult))
            vt_ready = None
            for k in range(2):
                vt_ready = transposes(vt[:, k, :, :], lambda j, k=k: v[:, k, j * P:(j + 1) * P], NT, P, n, free=vt_ready)
            PE.after(vt_ready, causal_w)
            for k in range(2):
                for n in range(NT):
                    for g in range(2):
                        last = nc.tensor.matmul(wide[g * HD:(g + 1) * HD, n * P:(n + 1) * P],
                                                vt[:, k, n, g * HD:(g + 1) * HD], w[:, 2 * k + g, :],
                                                start=True, stop=True)
                ready = PE.mark(last)
                for _ in range(4):
                    point()
                o = V.mark(V.after(ready).tensor_tensor(
                    sq[:, k, :].rearrange("p (n m) -> p n m", m=P), wide[:].rearrange("p (n m) -> p n m", m=P),
                    b[:, k, :].unsqueeze(1).to_broadcast([P, NT, P]), ALU.add))
                PE.after(o)
                o = V.mark(V.then().tensor_tensor(sq[:, k, :], sq[:, k, :], u[:, k, :], ALU.mult))
                SP.wait_ge(*o)
                store.mark(SP.dma_start(mixed2[4 + k], sq[:, k, :]))
            barrier()

    def lru():
        barrier()
        with ExitStack() as at:
            x, gate, xc, r, ig, la, m = (sb(at, "lr_" + n, [P, L]) for n in ("x", "g", "xc", "r", "i", "la", "m"))
            wa, wx = sb(at, "lr_wa", [P, 2, P]), sb(at, "lr_wx", [P, 2, P])
            sp = sb(at, "lr_sp", [P, 4, 2])
            load.mark(SP.dma_start(wa[:], t["lru_w"][0].rearrange("k p n -> p k n")))
            load.mark(SP.dma_start(wx[:], t["lru_w"][1].rearrange("k p n -> p k n")))
            for _ in range(4):
                point()
            lam = vec[:, VEC["lru_lam"][0]:VEC["lru_lam"][0] + 2]
            a = A.mark(nc.scalar.activation(sp[:, 0, :], lam, ACT.Abs))
            a = A.mark(A.then().activation(sp[:, 0, :], sp[:, 0, :], ACT.Exp, scale=-1.0))
            log1p(sp[:, 0, :], (sp[:, 1, :], sp[:, 2, :]), a)
            V.mark(V.then().tensor_scalar(sp[:, 1, :], lam, -1.0, 0.0, ALU.mult, ALU.max))
            V.mark(V.then().tensor_tensor(sp[:, 0, :], sp[:, 0, :], sp[:, 1, :], ALU.add))
            V.mark(V.then().tensor_scalar(sp[:, 3, :], sp[:, 0, :], -LRU_C, None, ALU.mult))
            for k in range(2):
                for mm in (V, A, PE):
                    SP.wait_ge(*mm.last())
                SP.wait_ge(*store.last())
                load.mark(SP.dma_start(x[:], proj2[DX + k]))
                got = load.mark(SP.dma_start(gate[:], proj2[DG + k]))
                V.after(got)
                V.mark(V.then().tensor_scalar(xc[:], x[:], col("lru_cw", 3 * 2 + k), col("lru_cb", k), ALU.mult, ALU.add))
                for back in (1, 2, 3):
                    V.mark(V.then().scalar_tensor_tensor(xc[:, back:], x[:, :L - back], col("lru_cw", (3 - back) * 2 + k),
                                                         xc[:, back:], ALU.mult, ALU.add))
                c = V.last()
                read = None
                for w, dst, bias in ((wa, r, "lru_ba"), (wx, ig, "lru_bx")):
                    for _ in range(6):
                        point()
                    PE.after(c, read)
                    for h in range(2):
                        last = nc.tensor.matmul(wide[:, h * HALF:(h + 1) * HALF], w[:, k, :],
                                                xc[:, h * HALF:(h + 1) * HALF], start=True, stop=True)
                    ready = PE.mark(last)
                    read = A.mark(A.then(ready).activation(dst[:], wide[:], ACT.Sigmoid, bias=col(bias, k)))
                decay = sp[:, 3, k:k + 1]
                A.mark(A.then(V.last()).activation(la[:], r[:], ACT.Tanh, scale=decay))
                a = A.mark(A.then().activation(r[:], r[:], ACT.Exp, scale=decay))
                V.mark(V.then(a).tensor_tensor(m[:], r[:], r[:], ALU.mult))
                V.mark(V.then().scalar_tensor_tensor(m[:], m[:], 1.0, la[:], ALU.add, ALU.mult))
                v = V.mark(V.then().tensor_scalar(m[:], m[:], -1.0, 0.0, ALU.mult, ALU.max))
                a = A.mark(A.then(v).activation(m[:], m[:], ACT.Sqrt))
                V.mark(V.then(a).memset(m[:, 0:1], 1.0))
                V.mark(V.then().tensor_tensor(ig[:], ig[:], xc[:], ALU.mult))
                V.mark(V.then().tensor_tensor(m[:], m[:], ig[:], ALU.mult))
                V.mark(V.then().tensor_tensor_scan(xc[:], r[:], m[:], 0.0, ALU.mult, ALU.add))
                a = A.mark(A.then().activation(gate[:], gate[:], ACT.Gelu_apprx_tanh))
                v = V.mark(V.then(a).tensor_tensor(xc[:], xc[:], gate[:], ALU.mult))
                SP.wait_ge(*v)
                store.mark(SP.dma_start(mixed2[6 + k], xc[:]))
            barrier()

    def merge(mixed, proj, gate_row, branches, name):
        tiles = 12 // branches if branches == 3 else 2
        blocks = 4 if branches == 3 else 2
        units = branches * tiles * blocks // 8
        n_in = branches * tiles
        barrier()
        with ExitStack() as at:
            mh, ml = sb(at, name + "h", [P, n_in, L], F32R), sb(at, name + "l", [P, n_in, L], F32R)
            split = []
            for n in range(n_in):
                x = (act_hi if n < KT else act_lo)[:, n % KT, :].bitcast(F32)
                if n > 1:
                    SP.wait_ge(*loads[n % 2].last())
                split.append(split_act(x, mh[:, n, :], ml[:, n, :], loads[n % 2].mark(SP.dma_start(x, mixed[n]))))
            gates = sb(at, name + "g", [P, branches, L])
            m, part = sb(at, name + "m", [P, L]), rs
            for br in range(branches):
                gate_in[br].mark(SP.dma_start(gates[:, br, :], proj[gate_row + 8 * br]))

            def rhs(o, k):
                n = (o % branches) * tiles + k
                if o < branches:
                    PE.after(split[n])
                return mh[:, n, :], ml[:, n, :]

            def evict(i, o, psum, ready, read):
                block, br = o // branches, o % branches
                if br == 0:
                    done = read(V.then(ready, gate_in[br].last()).tensor_tensor(m[:], gates[:, br, :], psum[:], ALU.mult))
                else:
                    done = read(V.after(ready, gate_in[br].last(), G.last())
                                .tensor_tensor(part[:], gates[:, br, :], psum[:], ALU.mult))
                    G.mark(G.then(done).tensor_tensor(m[:], m[:], part[:], ALU.add))
                SP.wait_ge(*done)
                gate_in[br].mark(SP.dma_start(gates[:, br, :], proj[i * blocks + (gate_row + 8 * br + block + 1)]))
                if br == branches - 1:
                    at_ = bass.ds(i * blocks + block, 1)
                    hi, lo = (x[:, at_, :].rearrange("p a n -> p (a n)") for x in (act_hi, act_lo))
                    a = A.mark(A.after(G.last()).copy(hi, m[:]))
                    V.mark(V.after(a).tensor_tensor(lo, m[:], hi.bitcast(F32), ALU.subtract))

            per = {G: blocks * (branches - 1), A: blocks, V: blocks, PE: blocks * branches - units}
            per.update({gate_in[br]: 16 * blocks for br in range(branches)})
            stage(KT // blocks, units, blocks * branches, tiles, rhs, evict, per=per)
            for br in range(branches):
                SP.wait_ge(*gate_in[br].last())
            barrier()

    gate_in = [Count(sem(f"gate_in{n}")) for n in range(4)]

    def mix_out(x_dram, gain, out_dram, next_gain, name, ahead_turns):
        with ExitStack() as at:
            y, sq, squares = (sb(at, name + n, w) for n, w in (("y", [P, KT, L]), ("q", [P, L]), ("ss", [P, L])))
            G.mark(G.then().memset(squares[:], 0.0))

            def evict(i, o, psum, ready, read):
                dst = y[:, bass.ds(i * 2 + o, 1), :].rearrange("p a n -> p (a n)")
                square_sum(dst, sq[:], squares[:], read(V.after(ready).tensor_copy(dst, psum[:])))

            stage(4, 2, 2, KT, act_rhs, evict, per={A: 2, G: 2})
            ahead = Ahead(ahead_turns)
            bridge(y, squares, x_dram, gain, out_dram, next_gain, name, ahead)
            return ahead

    def mlp(ahead, x_dram, gain, out_dram, next_gain, groups, gated, name, ahead_turns=0):
        with ExitStack() as at:
            acc, sq, squares = (sb(at, name + n, w) for n, w in (("acc", [P, KT, L]), ("q", [P, L]), ("ss", [P, L])))
            G.mark(G.then().memset(squares[:], 0.0))
            with ExitStack() as inner:
                hh, hl = sb(inner, name + "hh", [P, 8, L], F32R), sb(inner, name + "hl", [P, 8, L], F32R)
                x = sb(inner, name + "v", [P, 2, L])

                def hidden_done(index, s, mark):
                    hi, lo = (h[:, bass.ds(index, 1), :].rearrange("p a n -> p (a n)") for h in (hh, hl))
                    a = A.mark(A.after(mark).copy(hi, x[:, s, :]))
                    V.mark(V.after(a).tensor_tensor(lo, x[:, s, :], hi.bitcast(F32), ALU.subtract))

                def evict_relu2(i, o, psum, ready, read):
                    s = o % 2
                    a = read(V.then(ready).tensor_tensor(x[:, s, :], psum[:], rs[:], ALU.mult))
                    v = V.mark(V.after(a).scalar_tensor_tensor(x[:, s, :], x[:, s, :], 0.0, x[:, s, :],
                                                               ALU.max, ALU.mult))
                    hidden_done(i * 2 + o, s, v)

                def evict_swiglu(i, o, psum, ready, read):
                    v = read(V.then(ready).tensor_tensor(x[:, o, :], psum[:], rs[:], ALU.mult))
                    if o == 0:
                        A.mark(A.after(v).activation(x[:, 0, :], x[:, 0, :], ACT.Silu))
                    else:
                        v = V.mark(V.after(v, A.last()).tensor_tensor(x[:, 1, :], x[:, 0, :], x[:, 1, :], ALU.mult))
                        hidden_done(i, 1, v)

                for n, tiles in enumerate(groups):
                    turns, hidden = (tiles, evict_swiglu) if gated else (tiles // 2, evict_relu2)
                    per = {A: 2, V: 2 if gated else 4}
                    if n == 0:
                        ahead.run(hidden, per)
                    else:
                        stage(turns, 2, 2, KT, act_rhs, hidden, per=per)
                    nc.tensor.wait_ge(*V.last())
                    final = n == len(groups) - 1

                    def evict(i, o, psum, ready, read, n=n, final=final):
                        dst = acc[:, bass.ds(i * 2 + o, 1), :].rearrange("p a n -> p (a n)")
                        if n == 0:
                            done = read(V.after(ready).tensor_copy(dst, psum[:]))
                        else:
                            done = read(V.after(ready).tensor_tensor(dst, dst, psum[:], ALU.add))
                        if final:
                            square_sum(dst, sq[:], squares[:], done)

                    stage(4, 2, 2, tiles, lambda o, k: (hh[:, k, :], hl[:, k, :]), evict,
                          per={A: 2, G: 2} if final else None)
                    for e in (nc.scalar, nc.vector):
                        e.wait_ge(s_mm, used["units"] + 2)
            ahead = Ahead(ahead_turns) if ahead_turns else None
            bridge(acc, squares, x_dram, gain, out_dram, next_gain, name, ahead)
            return ahead

    x_in = t["x"]
    SP.wait_ge(*load.last())
    for n, d in enumerate((proj1[N1], proj2[N2])):
        stores[n].mark(SP.dma_start(d, x_in[0]))
    out_per = {outs[0]: 16, outs[1]: 16}
    with ExitStack() as at:
        buf = sb(at, "p1", [P, 2, L])
        rows = [F_] + [U_ + n for n in range(4)] + [Q_ + n for n in range(12)] + [X_ + n for n in range(12)]

        def evict(i, o, *rest):
            to_dram(proj1, rows[o] - o, buf)(i, o, *rest)

        n = len(rows)
        with Woven(products(0, used["units"], n, n, KT, act_rhs, evict), n * KT, 399) as w:
            norm_start(x_in, "g_pre_mix", "n1", lambda k, mark: (PE.after(mark), w.upto(k + 1)))
            s5(w)
        advance(n, n)
        barrier()
        gates = to_dram(proj1, GATE1, buf, gate="b_gate", n=6)
        first = dict(used)

        fox(lambda i: Woven(products(i, first["units"], 6, 6, KT, act_rhs, gates), 6 * KT, 48))
        advance(24, 24)
        barrier()
    merge(mixed1, proj1, GATE1, 3, "m1")
    ahead = mix_out(x_in, "g_post_mix", x1, "g_pre_mlp", "o1", 4)
    ahead = mlp(ahead, x1, "g_post_mlp", x2, "norm_mix_pre", (8, 8, 8, 8), False, "f1", 3)

    with ExitStack() as at:
        buf = sb(at, "p2", [P, 2, L])
        ahead.run(to_dram(proj2, AQ, buf), out_per)
        barrier()
        first = dict(used)
        rest = to_dram(proj2, BQ, buf, n=8)
        band(lambda i: Woven(products(i, first["units"], 8, 8, KT, act_rhs, rest), 8 * KT, 48))
        advance(16, 16)
        barrier()
        gates = to_dram(proj2, GATE2, buf, gate="", n=12)
        base = dict(used)
        hgrn(lambda i: Woven(products(i, base["units"], 12, 12, KT, act_rhs, gates), 12 * KT, 90))
        advance(24, 24)
        barrier()
        with Woven(products(0, used["units"], 8, 8, KT, act_rhs, to_dram(proj2, GATE2 + 24, buf, gate="")), 8 * KT, 42):
            gmlp()
            lru()
        advance(8, 8)
        barrier()
    merge(mixed2, proj2, GATE2, 4, "m2")
    ahead = mix_out(x2, "norm_mix_post", x3, "norm_ffn_pre", "o2", 8)
    mlp(ahead, x3, "norm_ffn_post", out, None, (8, 8, 6), True, "f2")

    for s, n in ((0, (used["units"] + 4) // 2), (1, (used["units"] + 3) // 2)):
        SP.wait_ge(s_raw[s], 16 * n)
    barrier()


def _tiles(w):
    k, n = w.shape
    return w.reshape(k // P, P, n // P, P).transpose(2, 0, 1, 3)


def _units(tiles):
    n = tiles.shape[0] // 8
    return tiles.reshape(n, 8, P, P).transpose(0, 2, 1, 3).reshape(n, P, 8 * P)


def _stream(x):
    w_in = x["w_in"][0]
    n_f = F_ * P
    f = np.pad(w_in[:, n_f:n_f + FOX_HEADS], ((0, 0), (0, P - FOX_HEADS)))
    w = _tiles(w_in[:, :n_f])
    parts = [_tiles(f), w[U_:X_], w[Q_:F_], w[X_:Q_], _tiles(w_in[:, n_f + FOX_HEADS:])]
    wb = _tiles(x["w_branch"][0])
    parts += [wb, _tiles(x["w_out"][0])]
    w1, w2 = _tiles(x["w_ff1"][0]), _tiles(x["w_ff2"][0])
    for g in range(4):
        parts += [w1[8 * g:8 * g + 8], w2[:, 8 * g:8 * g + 8]]
    parts.append(_tiles(x["w_in_2"][0]))
    parts.append(_tiles(x["w_branch_2"][0].reshape(D, D)))
    parts.append(_tiles(x["w_out_2"][0]))
    w1, w2 = _tiles(x["w_ffn_in_2"][0]), _tiles(x["w_ffn_out_2"][0])
    n = HID2 // P
    w1 = np.stack([w1[:n], w1[n:]], 1)
    for g in (0, 8, 16):
        m = min(8, n - g)
        parts += [w1[g:g + m], np.pad(w2[:, g:g + m], ((0, 0), (0, 8 - m), (0, 0), (0, 0)))]
    tiles = np.concatenate([p.reshape(-1, P, P) for p in parts] + [np.zeros((3 * 8, P, P), np.float32)])
    return _units(tiles)


def _lay_out(x):
    def cols(v):
        return v.reshape(-1, P).T

    pairs = lambda v: v.reshape(PAIRS, P).T
    v = {
        "g_pre_mix": cols(x["g_pre_mix"]), "g_post_mix": cols(x["g_post_mix"]), "g_pre_mlp": cols(x["g_pre_mlp"]),
        "g_post_mlp": cols(x["g_post_mlp"]), "b_gate": cols(x["b_gate"]), "conv_w": cols(x["conv_w"]),
        "a_re": pairs(x["s5_a_re"]), "a_im": pairs(x["s5_a_im"]),
        "log_dt": np.repeat(x["s5_log_dt"].reshape(PAIRS, 2).T, S5_P, axis=0),
        "norm_mix_pre": cols(x["norm_mix_pre_2"]), "norm_mix_post": cols(x["norm_mix_post_2"]),
        "norm_ffn_pre": cols(x["norm_ffn_pre_2"]), "norm_ffn_post": cols(x["norm_ffn_post_2"]),
        "lb": cols(x["hgrn_lb_logits_2"]), "hgrn_g": cols(x["hgrn_norm_g_2"]), "gmlp_g": cols(x["gmlp_norm_g_2"]),
        "lru_cw": cols(x["lru_conv_w_2"]), "lru_cb": cols(x["lru_conv_b_2"]), "lru_ba": cols(x["lru_ba_2"]),
        "lru_bx": cols(x["lru_bx_2"]), "lru_lam": cols(x["lru_lambda_2"]),
        "b_f": np.repeat(x["fox_b_f"].reshape(FOX_HEADS, 1), P // FOX_HEADS, axis=0),
    }

    def diagonal(blocks, n):
        m, k, _ = blocks.shape
        out = np.zeros((m // n, n, k, n, k), np.float32)
        for i in range(n):
            out[:, i, :, i, :] = blocks.reshape(m // n, n, k, k)[:, i]
        return out.reshape(m // n, n * k, n * k)

    dist = np.clip(LEFT + np.arange(P)[:, None] - np.arange(BAND)[None, :], -63, 256) + 63
    b = np.stack([x["s5_b_re"][0], x["s5_b_im"][0]])
    c = np.stack([x["s5_c_re"][0], x["s5_c_im"][0]]).transpose(0, 1, 3, 2)

    def by_pair(v):
        return v.reshape(2, PAIRS, P, S5_H).transpose(2, 0, 1, 3)

    return {
        "x": x["x"][0].T.reshape(KT, P, L),
        "vec": np.concatenate([v[n] for n, _ in VEC_NAMES], axis=1),
        "stream": _stream(x),
        "s5_b": by_pair(b), "s5_c": by_pair(c),
        "s5_d": x["s5_d"][0].T,
        "glu": diagonal(x["s5_w_glu"][0], 8),
        "rel": x["attn_rel_bias_2"][0][:, dist],
        "gm_w": x["gmlp_ws_2"][0].transpose(0, 2, 1), "gm_b": x["gmlp_bs_2"][0],
        "lru_w": np.stack([diagonal(x["lru_wa_2"][0], 2), diagonal(x["lru_wx_2"][0], 2)]),
    }


def kernel(**inputs):
    import concourse.bacc as bacc
    from concourse.bass_utils import run_bass_kernel_spmd

    nc = bacc.Bacc("TRN2", target_bir_lowering=False, num_devices=1)
    arrays, t = {}, {}
    for name, a in _lay_out({n: np.asarray(v) for n, v in inputs.items()}).items():
        a = np.ascontiguousarray(a)
        arrays["in_" + name] = a
        t[name] = nc.dram_tensor("in_" + name, a.shape, mybir.dt.from_np(a.dtype), kind="ExternalInput").ap()
    out = nc.dram_tensor("out", (KT, P, L), F32, kind="ExternalOutput").ap()
    build(nc, t, out)
    r = run_bass_kernel_spmd(nc, [arrays], core_ids=[0])
    y = r.results[0]["out"]
    return np.ascontiguousarray(y.reshape(D, L).T).reshape(1, L, D)
```

```python
import math
from contextlib import ExitStack, contextmanager

import numpy as np
import concourse.bass as bass
from concourse import mybir
from concourse.alu_op_type import AluOpType as ALU

P = 128
L = 1024
D = 1024
KT = D // P
HALF = 512
HD = 64
EPS = 1e-6
S5_G, S5_P, S5_H = 32, 64, 16
PAIRS = S5_G // 2
T = 8
CH = L // T
FOX_HEADS = 8
FF1 = 4096
BAND_HEADS = 4
LEFT = 512
BAND = LEFT + P
HID2 = 2816
LOG_FLOOR = 1e-30
LRU_C = 8.0
LEVELS = 7

F32 = mybir.dt.float32
F32R = mybir.dt.float32r
ACT = mybir.ActivationFunctionType
AX = mybir.AxisListType

U_, X_, B_, C_, Q_, K_, V_, F_, GATE1 = 0, 4, 8, 12, 16, 20, 24, 28, 29
N1 = 53
AQ, AK, AV, BQ, BF, BI, BG, CU, CV, DX, DG, GATE2 = 0, 2, 4, 6, 8, 10, 12, 14, 16, 18, 20, 22
N2 = 54

VEC_NAMES = (("g_pre_mix", 8), ("g_post_mix", 8), ("g_pre_mlp", 8), ("g_post_mlp", 8), ("b_gate", 24),
             ("conv_w", 12), ("a_re", 16), ("a_im", 16), ("log_dt", 16),
             ("norm_mix_pre", 8), ("norm_mix_post", 8), ("norm_ffn_pre", 8), ("norm_ffn_post", 8),
             ("lb", 2), ("hgrn_g", 2), ("gmlp_g", 2), ("lru_cw", 8), ("lru_cb", 2), ("lru_ba", 2),
             ("lru_bx", 2), ("lru_lam", 2), ("b_f", 1))
VEC = {}
for _name, _n in VEC_NAMES:
    VEC[_name] = sum(VEC[m][1] for m in VEC), _n
NVEC = sum(n for _, n in VEC_NAMES)


COUNTERS = []


class Lane:

    def __init__(self, engine, sem, start):
        self.engine, self.sem = engine, sem
        self.n = start
        self.here = self.per = 0
        self.unit = 1
        COUNTERS.append(self)
        engine.sem_inc(sem, start)

    def after(self, *marks):
        for m in marks:
            if m is not None:
                self.engine.wait_ge(m[0], m[1])
        return self.engine

    def then(self, *marks):
        return self.after((self.sem, self.n), *marks)

    def mark(self, instruction):
        instruction.then_inc(self.sem, self.unit)
        self.n = self.n + self.unit
        self.here += self.unit
        return (self.sem, self.n)

    def last(self):
        return (self.sem, self.n)

    def turn_ago(self, mark):
        return (self.sem, mark[1] - self.per)


class Count(Lane):

    def __init__(self, sem, unit=16):
        self.sem, self.unit = sem, unit
        COUNTERS.append(self)
        self.n = self.here = self.per = 0


@contextmanager
def loop(nc, turns, per):
    start = {c: c.n for c in per}
    fixed = {c: c.n for c in COUNTERS if c not in per}
    with nc.Fori(0, turns) as i:
        for c in per:
            c.n, c.here, c.per = start[c] + i * per[c], 0, per[c]
        yield i
        assert all(c.here == per[c] for c in per), [(c.sem.name, c.here) for c in per]
        assert all(c.n is fixed[c] for c in fixed), [c.sem.name for c in fixed if c.n is not fixed[c]]
    for c in per:
        c.n, c.per = start[c] + turns * per[c], 0


def build(nc, t, out):
    COUNTERS.clear()
    with ExitStack() as ctx:
        _build(nc, ctx, t, out)


def _build(nc, ctx, t, out):
    def sb(at, name, shape, dt=F32):
        return at.enter_context(nc.sbuf_tensor(name, shape, dt))

    def sem(name):
        return ctx.enter_context(nc.semaphore(name))

    def scratch(name, shape):
        return nc.dram_tensor(name, shape, F32, kind="Internal").ap()

    proj1, proj2 = scratch("proj1", (N1 + 1, P, L)), scratch("proj2", (N2 + 1, P, L))
    mixed1 = scratch("mixed1", (12, P, L))
    mixed2 = scratch("mixed2", (8, P, L))
    x1, x2, x3 = (scratch(n, (KT, P, L)) for n in ("x1", "x2", "x3"))
    fox_cum = scratch("fox_cum", (FOX_HEADS, L))
    fox_log = scratch("fox_log", (P, L * FOX_HEADS // P))
    s5_u, s5_y = scratch("s5_u", (4 * P, T, CH)), scratch("s5_y", (4 * P, T, CH))

    V = Lane(nc.vector, sem("vector"), 1024)
    A = Lane(nc.scalar, sem("scalar"), 1024)
    G = Lane(nc.gpsimd, sem("gpsimd"), 1024)
    PE = Lane(nc.tensor, sem("tensor"), 1024)
    load = Count(sem("load"))
    store = Count(sem("store"))
    loads = [Count(sem(f"load{n}")) for n in range(2)]
    stores = [Count(sem(f"store{n}")) for n in range(2)]
    outs = [Count(sem(f"out{n}")) for n in range(2)]
    SP = nc.sync

    background = []

    class Woven:

        def __init__(self, tiles, n_tiles, points):
            self.tiles, self.n_tiles, self.points = tiles, n_tiles, points
            self.done = self.passed = 0

        def __enter__(self):
            background.append(self)
            return self

        def point(self, n):
            self.passed += n
            self.upto(self.n_tiles * self.passed // self.points)

        def upto(self, n):
            while self.done < min(n, self.n_tiles):
                next(self.tiles)
                self.done += 1

        def __exit__(self, *failed):
            if not failed[0]:
                self.upto(self.n_tiles)
                for _ in self.tiles:
                    raise AssertionError("tiles left over")
            background.pop()

    def point(n=1):
        for b in background:
            b.point(n)

    def barrier():
        marks = [x.last() for x in (V, A, G, PE, load, store, *loads, *stores)]
        if not background:
            marks += [x.last() for x in (*pair_read, *outs)] + [(s_mm, used["units"] + 2)]
        for e in (nc.vector, nc.scalar, nc.gpsimd, nc.sync):
            for s, n in marks:
                e.wait_ge(s, n)

    raw = sb(ctx, "w_raw", [P, 2, KT * P])
    whi = sb(ctx, "w_hi", [P, 2, KT * P], F32R)
    wlo = sb(ctx, "w_lo", [P, 2, KT * P], F32R)
    vec = sb(ctx, "vec", [P, NVEC])
    ident = sb(ctx, "ident", [P, P])
    causal = sb(ctx, "causal", [P, P])
    ones = sb(ctx, "ones", [P, P])
    pair = [ctx.enter_context(nc.psum_tensor(f"pair{i}", [P, L], F32)) for i in range(2)]
    wide = ctx.enter_context(nc.psum_tensor("wide", [P, L], F32))
    bank = [ctx.enter_context(nc.psum_tensor(f"bank{i}", [P, HALF], F32)) for i in (6, 7)]
    act_hi = sb(ctx, "act_hi", [P, KT, L], F32R)
    act_lo = sb(ctx, "act_lo", [P, KT, L], F32R)
    tok = sb(ctx, "tok", [P, 2 * L // P])
    rs = sb(ctx, "rs", [P, L])

    def col(name, i):
        at = VEC[name][0]
        return vec[:, at + i:at + i + 1]

    load.mark(SP.dma_start(vec[:], t["vec"]))
    G.mark(G.then().memset(ident[:], 0.0))
    G.mark(G.then().affine_select(out=ident[:], in_=ident[:], compare_op=ALU.not_equal, fill=1.0, base=0,
                                  pattern=[[-1, P]], channel_multiplier=1))
    G.mark(G.then().memset(causal[:], 0.0))
    G.mark(G.then().affine_select(out=causal[:], in_=causal[:], compare_op=ALU.is_ge, fill=-1e30, base=0,
                                  pattern=[[-1, P]], channel_multiplier=1))
    G.mark(G.then().memset(ones[:], 1.0))

    s_raw = [sem("raw0"), sem("raw1")]
    s_whi = sem("whi")
    s_split = sem("split")
    s_mm = sem("mm")
    for s, e in ((s_whi, nc.scalar), (s_split, nc.gpsimd), (s_mm, nc.tensor)):
        e.sem_inc(s, 2)
    used = {"units": 0, "blocks": 0}

    def split_unit(b, slot, fills):
        nc.scalar.wait_ge(s_raw[slot], 16 * fills)
        nc.scalar.wait_ge(s_mm, b + 1)
        nc.scalar.copy(whi[:, slot, :], raw[:, slot, :]).then_inc(s_whi, 1)
        nc.gpsimd.wait_ge(s_whi, b + 3)
        nc.gpsimd.tensor_tensor(wlo[:, slot, :], raw[:, slot, :], whi[:, slot, :].bitcast(F32),
                                ALU.subtract).then_inc(s_split, 1)

    def fetch_unit(b, slot):
        SP.wait_ge(s_split, b + 1)
        SP.dma_start(raw[:, slot, :], t["stream"][b]).then_inc(s_raw[slot], 16)

    for n in range(2):
        fetch_unit(n, n)
    split_unit(0, 0, 1)
    fetch_unit(2, 0)

    def products(i, base, per_turn, n_out, tiles, rhs, evict):
        packed = n_out * tiles == 8 * per_turn
        for o in range(n_out):
            at = (used["blocks"] + o) % 2
            reads, out_pair = pair_read[at], pair[at]
            for k in range(tiles):
                n = o * tiles + k if packed else 8 * o + k
                w, slot = n % 8, (base + n // 8) % 2
                b = i * per_turn + (base + n // 8)
                if w == 0:
                    split_unit(b + 1, 1 - slot, i * (per_turn // 2) + ((base + n // 8 + 1) // 2 + 1))
                    fetch_unit(b + 3, 1 - slot)
                    nc.tensor.wait_ge(s_split, b + 3)
                if k == 0:
                    nc.tensor.wait_ge(reads.sem, reads.n)
                hi, lo = rhs(o, k)
                w_hi, w_lo = (x[:, slot, w * P:(w + 1) * P] for x in (whi, wlo))
                for n_pass, (wt, a) in enumerate(((w_hi, hi), (w_hi, lo), (w_lo, hi))):
                    for h in range(2):
                        last = nc.tensor.matmul(out_pair[:, h * HALF:(h + 1) * HALF], wt, a[:, h * HALF:(h + 1) * HALF],
                                                start=k == 0 and n_pass == 0, stop=k == tiles - 1 and n_pass == 2)
                if w == 7 or (not packed and k == tiles - 1):
                    last.then_inc(s_mm, 1)
                    ready = (s_mm, b + 3)
                elif k == tiles - 1:
                    ready = PE.mark(last)
                yield
            evict(i, o, out_pair, ready, reads.mark)

    def stage(turns, per_turn, n_out, tiles, rhs, evict, per=None):
        if turns == 1:
            for _ in products(0, used["units"], per_turn, n_out, tiles, rhs, evict):
                pass
        else:
            assert per_turn % 2 == 0 and n_out % 2 == 0
            per = dict(per or {})
            per.update({c: n_out // 2 for c in pair_read})
            with loop(nc, turns, per) as i:
                for _ in products(i, used["units"], per_turn, n_out, tiles, rhs, evict):
                    pass
        advance(turns * per_turn, turns * n_out)

    class Ahead:

        def __init__(self, turns):
            self.turns = turns
            self.tiles = products(0, used["units"], 2, 2, KT, act_rhs, lambda *a: self.evict(*a))

        def tile(self, mark):
            PE.after(mark)
            next(self.tiles)

        def run(self, evict, per):
            self.evict = evict
            for _ in self.tiles:
                pass
            advance(2, 2)
            stage(self.turns - 1, 2, 2, KT, act_rhs, lambda i, *a: evict(i + 1, *a), per=per)

    def advance(units, blocks):
        used["units"] += units
        used["blocks"] += blocks

    pair_read = [Count(sem(f"pair_read{n}"), 1) for n in range(2)]
    for c in pair_read:
        nc.vector.sem_inc(c.sem, 1)
        c.n = 1

    def act_rhs(o, k):
        return act_hi[:, k, :], act_lo[:, k, :]

    def split_act(src, hi, lo, mark):
        a = A.mark(A.after(mark).copy(hi, src))
        return V.mark(V.after(a).tensor_tensor(lo, src, hi.bitcast(F32), ALU.subtract))

    def row_sums(sq, k, tiles, mark):
        PE.after(mark)
        for h in range(2):
            last = nc.tensor.matmul(wide[:, h * HALF:(h + 1) * HALF], ones[:], sq[:, h * HALF:(h + 1) * HALF],
                                    start=k == 0, stop=k == tiles - 1)
        return PE.mark(last)

    def token_sums(sq, mark, groups):
        g = groups.shape[-1]
        PE.after(mark)
        for j in range(L // P):
            last = nc.tensor.matmul(wide[:, j * g:(j + 1) * g], sq[:, j * P:(j + 1) * P], groups, start=True, stop=True)
        return PE.mark(last)

    def spread_inv_sqrt(rstd, scale, mark, g=1, rows=False):
        t_ = tok[:, 0:L // P * g]
        if rows:
            r3 = rstd[:].rearrange("p (j n) -> p j n", n=P)
            V.mark(V.after(mark).tensor_tensor(r3, wide[:].rearrange("p (j n) -> p j n", n=P),
                                               ident[:].unsqueeze(1).to_broadcast([P, L // P, P]), ALU.mult))
            V.mark(V.then().reduce_sum(t_, r3, AX.X))
            V.mark(V.then().tensor_scalar(t_, t_, scale, EPS, ALU.mult, ALU.add))
        else:
            V.mark(V.after(mark).tensor_scalar(t_, wide[:, 0:L // P * g], scale, EPS, ALU.mult, ALU.add))
        a = A.mark(A.after(V.last()).activation(t_, t_, ACT.Sqrt))
        v = V.mark(V.after(a).reciprocal(t_, t_))
        for h in range(2):
            PE.after(v)
            for j in range(h * 4, h * 4 + 4):
                for n in range(g):
                    r = tok[:, j * g + n:j * g + n + 1].to_broadcast([P, P // g])
                    last = nc.tensor.matmul(wide[n * (P // g):(n + 1) * (P // g), j * P:(j + 1) * P], r, ident[:],
                                            start=True, stop=True)
            spread = A.mark(A.after(PE.mark(last)).copy(rstd[:, h * HALF:(h + 1) * HALF],
                                                        wide[:, h * HALF:(h + 1) * HALF]))
        return spread

    def norm_start(x_dram, gain, name, ahead):
        with ExitStack() as at:
            x, sq = sb(at, name + "x", [P, KT, L]), sb(at, name + "s", [P, 2, L])
            arrived = []
            for k in range(KT):
                if k > 1:
                    SP.wait_ge(*arrived[k - 2])
                arrived.append(loads[k % 2].mark(SP.dma_start(x[:, k, :], x_dram[k])))
            done = []
            for k in range(KT):
                split = scaled_split(x[:, k, :], gain, k, arrived[k], sq, done)
                ahead(k, split)
            spread_inv_sqrt(rs, 1.0 / D, done[-1], rows=True)
            barrier()

    def scaled_split(x, gain, k, mark, sq, done):
        g = col(gain, k)
        a = A.mark(A.after(mark).activation(act_hi[:, k, :], x, ACT.Copy, scale=g))
        split = V.mark(V.after(a).scalar_tensor_tensor(act_lo[:, k, :], x, g, act_hi[:, k, :].bitcast(F32),
                                                       ALU.mult, ALU.subtract))
        a = A.mark(A.after(done[k - 2] if k > 1 else None).activation(sq[:, k % 2, :], x, ACT.Square))
        done.append(row_sums(sq[:, k % 2, :], k, KT, a))
        return split

    def bridge(y, squares, x_dram, gain, out_dram, next_gain, name, ahead=None):
        barrier()
        with ExitStack() as at:
            x, r = sb(at, name + "x", [P, 4, L]), sb(at, name + "r", [P, L])
            sq = sb(at, name + "s", [P, 2, L])
            scaled, added, split, stored = [], [], [], []

            def fetch(k):
                if k > 3 and next_gain:
                    SP.wait_ge(*split[k - 4])
                    SP.wait_ge(*done[k - 4])
                return loads[k % 2].mark(SP.dma_start(x[:, k % 4, :], x_dram[k]))

            done = []
            arrived = [fetch(0), fetch(1)]
            y_scale = spread_inv_sqrt(r, 1.0 / D, token_sums(squares, G.last(), ones[:, 0:1]))

            def scale(k):
                scaled.append(V.mark(V.after(y_scale).scalar_tensor_tensor(y[:, k, :], y[:, k, :], col(gain, k), r[:],
                                                                           ALU.mult, ALU.mult)))

            scale(0)
            for k in range(KT):
                xk = x[:, k % 4, :]
                if k < KT - 1:
                    scale(k + 1)
                lane = G if k > 1 else V
                added.append(lane.mark(lane.after(scaled[k], arrived[k]).tensor_tensor(xk, xk, y[:, k, :], ALU.add)))
                if next_gain:
                    split.append(scaled_split(xk, next_gain, k, added[k], sq, done))
                    ahead.tile(split[k])
                if k > 1:
                    SP.wait_ge(*stored[k - 2])
                SP.wait_ge(*added[k])
                if k + 2 < KT:
                    arrived.append(fetch(k + 2))
                stored.append(stores[k % 2].mark(SP.dma_start(out_dram[k], xk)))
            if next_gain:
                spread_inv_sqrt(rs, 1.0 / D, done[-1], rows=True)
            barrier()

    def square_sum(y, sq, squares, mark):
        a = A.mark(A.after(mark, G.last()).activation(sq, y, ACT.Square))
        G.mark(G.after(a).tensor_tensor(squares, squares, sq, ALU.add))

    def to_dram(dst, row, buf, gate=None, n=2, first=0):
        def evict(i, o, psum, ready, read):
            slot = o % 2
            stored = outs[slot].last()
            done = read(V.after(ready, stored).tensor_tensor(buf[:, slot, :], psum[:], rs[:], ALU.mult))
            if gate is not None:
                bias = vec[:, bass.ds(i * n + (VEC[gate][0] + first + o), 1)] if gate else 0.0
                done = A.mark(A.after(done).activation(buf[:, slot, :], buf[:, slot, :], ACT.Sigmoid, bias=bias))
            SP.wait_ge(*done)
            outs[slot].mark(SP.dma_start(dst[i * n + (row + o)], buf[:, slot, :]))
        return evict

    def log1p(x, tmp, mark):
        z, z2 = tmp
        V.mark(V.after(mark).tensor_scalar_add(z, x, 2.0))
        V.mark(V.then().reciprocal(z, z))
        V.mark(V.then().tensor_tensor(z, z, x, ALU.mult))
        V.mark(V.then().tensor_tensor(z2, z, z, ALU.mult))
        V.mark(V.then().memset(x, 2.0 / 17))
        for n in range(15, 0, -2):
            V.mark(V.then().tensor_tensor(x, x, z2, ALU.mult))
            V.mark(V.then().tensor_scalar_add(x, x, 2.0 / n))
        return V.mark(V.then().tensor_tensor(x, x, z, ALU.mult))

    def transposes(dst, src, n, width, src_mark, rows=P, free=None, between=None):
        done = free
        for j0 in range(0, n, 4):
            m = min(4, n - j0)
            if between:
                between()
            PE.after(src_mark, done)
            for j in range(m):
                dst_j = bank[0][:, j * width:(j + 1) * width]
                if rows == P:
                    last = nc.tensor.transpose(dst_j, src(j0 + j), ident[:])
                else:
                    last = nc.tensor.matmul(dst_j, src(j0 + j), ident[0:rows, 0:rows], start=True, stop=True)
            ready = PE.mark(last)
            done = A.mark(A.after(ready).copy(dst[:, j0:j0 + m, :], bank[0][:, 0:m * width]
                                              .rearrange("p (j n) -> p j n", j=m)))
        return done

    def short_conv(at):
        xin, gb, gc = (sb(at, "cv" + n, [P, L]) for n in "xbc")
        y = sb(at, "cvy", [P, L])

        def fetch(i):
            for buf, row in ((xin, X_), (gb, B_), (gc, C_)):
                loads[0].mark(SP.dma_start(buf[:], proj1[i + row]))

        def tile(i):
            arrived = loads[0].last()

            def w(tap):
                return vec[:, bass.ds(i + (VEC["conv_w"][0] + tap * 4), 1)]

            V.mark(V.after(arrived).tensor_tensor(xin[:], gc[:], xin[:], ALU.mult))
            V.mark(V.then(stores[1].last()).tensor_scalar(y[:], xin[:], w(2), None, ALU.mult))
            for back in (1, 2):
                V.mark(V.then().scalar_tensor_tensor(y[:, back:], xin[:, :L - back], w(2 - back), y[:, back:],
                                                     ALU.mult, ALU.add))
            v = V.mark(V.then().tensor_tensor(y[:], y[:], gb[:], ALU.mult))
            SP.wait_ge(*v)
            stores[1].mark(SP.dma_start(mixed1[i + 4], y[:]))
        return fetch, tile

    def attention(heads, in_turn, tiles, src, rows, mixed, row0, head_bias, add_bias, name, per, woven, extra=None):
        barrier()
        halves = src.rearrange("b (h p) n -> (b h) p n", h=2)
        out_h = mixed.rearrange("b (h p) n -> (b h) p n", h=2)
        with ExitStack() as at:
            q, k, v = (sb(at, name + n, [HD, L]) for n in "qkv")
            vt = sb(at, name + "vt", [P, L // P, HD])
            s = sb(at, name + "s", [P, 2, L])
            pt = sb(at, name + "pt", [P, 2, L])
            ot = sb(at, name + "ot", [P, L // P, HD])
            o = sb(at, name + "o", [HD, L])
            st = sb(at, name + "st", [P, 2, 3])
            bias = head_bias(at)

            def head(i, aside=None):
                for buf, row in ((q, rows[0]), (k, rows[1]), (v, rows[2])):
                    load.mark(SP.dma_start(buf[:], halves[i + 2 * row]))
                bias_ready = bias[1](i)
                arrived = load.last()
                if aside:
                    aside()
                point(4)
                copied = transposes(vt, lambda j: v[:, j * P:(j + 1) * P], L // P, HD, arrived, rows=HD)
                scores_read, o_read, pend = None, None, None
                pv_done = []

                def weigh(n, k0, nk, e):
                    sl = n % 2
                    copied = weigh.copied = transposes(pt[:, sl, :].rearrange("p (j n) -> p j n", n=P),
                                        lambda j: s[:, sl, j * P:(j + 1) * P], nk, P, e, free=weigh.copied, between=point)
                    if nk > 3:
                        point()
                    PE.after(copied, o_read)
                    for j in range(nk):
                        last = nc.tensor.matmul(bank[1][:, 0:HD], pt[:, sl, j * P:(j + 1) * P], vt[:, k0 // P + j, :],
                                                start=j == 0, stop=j == nk - 1)
                    pv_done.append(PE.mark(last))

                def scale(n):
                    sl = n % 2
                    V.mark(V.after(pv_done[n]).reciprocal(st[:, sl, 2:3], st[:, sl, 1:2]))
                    return V.mark(V.then().tensor_scalar(ot[:, n, :], bank[1][:, 0:HD], st[:, sl, 2:3], None, ALU.mult))

                weigh.copied = copied
                for n, (q0, k0, k1) in enumerate(tiles):
                    w, sl = k1 - k0, n % 2
                    PE.after(arrived, scores_read)
                    for c in range(0, w, HALF):
                        e = min(w, c + HALF)
                        last = nc.tensor.matmul(wide[:, c:e], q[:, q0:q0 + P], k[:, k0 + c:k0 + e], start=True, stop=True)
                    ready = PE.mark(last)
                    if pend:
                        weigh(*pend)
                    sc = s[:, sl, 0:w]
                    V.after(ready, bias_ready, pv_done[n - 2] if n > 1 else None)
                    scores_read = add_bias(sc, wide[:, 0:w], bias[0], q0, k0, k1)
                    V.mark(V.then().reduce_max(st[:, sl, 0:1], sc, AX.X))
                    x = V.mark(V.then().tensor_scalar(st[:, sl, 0:1], st[:, sl, 0:1], -1.0, None, ALU.mult))
                    if pend:
                        o_read = scale(n - 1)
                    x = A.mark(A.after(x).activation(sc, sc, ACT.Exp, bias=st[:, sl, 0:1], accum_out=st[:, sl, 1:2]))
                    pend = (n, k0, w // P, x)
                point(3)
                weigh(*pend)
                scaled = scale(n)
                PE.after(scaled, scores_read)
                for n in range(L // P):
                    last = nc.tensor.matmul(wide[0:HD, n * P:(n + 1) * P], ot[:, n, :], ident[:], start=True, stop=True)
                v_o = V.mark(V.after(PE.mark(last), stores[0].last()).tensor_copy(o[:], wide[0:HD, :]))
                SP.wait_ge(*v_o)
                stores[0].mark(SP.dma_start(out_h[i + 2 * row0], o[:]))
                PE.after(v_o)

            beside = extra(at) if extra else None
            with loop(nc, heads // in_turn, per) as i, woven(i):
                for n in range(in_turn):
                    head(i * in_turn + n, (lambda n=n: beside[n](i)) if beside else None)
            barrier()

    def fox_logs():
        barrier()
        n_log = L * FOX_HEADS // P
        with ExitStack() as at:
            f, e, z, z2 = (sb(at, "fx" + n, [P, n_log]) for n in ("f", "e", "z", "y"))
            cum, one = sb(at, "fx_cum", [FOX_HEADS, L]), sb(at, "fx_one", [FOX_HEADS, L])
            for o in outs:
                SP.wait_ge(*o.last())
            a = load.mark(SP.dma_start(f[:], proj1[F_, 0:FOX_HEADS, :].rearrange("h (a n) -> (h a) n", a=16)))
            point(6)
            v = V.mark(V.after(a).tensor_scalar(f[:], f[:], col("b_f", 0), None, ALU.add))
            a = A.mark(A.after(v).activation(e[:], f[:], ACT.Abs))
            a = A.mark(A.then().activation(e[:], e[:], ACT.Exp, scale=-1.0))
            log1p(e[:], (z[:], z2[:]), a)
            V.mark(V.then().tensor_scalar(f[:], f[:], 0.0, None, ALU.min))
            v = V.mark(V.then().tensor_tensor(f[:], f[:], e[:], ALU.subtract))
            SP.wait_ge(*v)
            s = store.mark(SP.dma_start(fox_log, f[:]))
            point(6)
            SP.wait_ge(*s)
            a = load.mark(SP.dma_start(cum[:], fox_log.rearrange("(h a) n -> h (a n)", h=FOX_HEADS)))
            V.mark(V.then().memset(one[:], 1.0))
            v = V.mark(V.then(a).tensor_tensor_scan(cum[:], one[:], cum[:], 0.0, ALU.mult, ALU.add))
            SP.wait_ge(*v)
            store.mark(SP.dma_start(fox_cum, cum[:]))
            barrier()

    def fox(woven):
        def head_bias(at):
            cb = sb(at, "fx_cb", [P, L])
            return cb, lambda i: load.mark(SP.dma_start(cb[:], fox_cum[i].partition_broadcast(P)))

        def add_bias(sc, psum, cb, q0, k0, k1):
            v = V.mark(nc.vector.scalar_tensor_tensor(sc, psum, HD ** -0.5, cb[:, k0:k1], ALU.mult, ALU.subtract))
            V.mark(V.then().tensor_tensor(sc[:, k1 - k0 - P:], sc[:, k1 - k0 - P:], causal[:], ALU.add))
            return v

        attention(FOX_HEADS, 2, [(n * P, 0, (n + 1) * P) for n in range(8)], proj1, (Q_, K_, V_), mixed1, 8,
                  head_bias, add_bias, "fox", {V: 103, A: 50, PE: 62, load: 128, loads[0]: 48, stores[0]: 32,
                                               stores[1]: 16, outs[0]: 48, outs[1]: 48, pair_read[0]: 3,
                                               pair_read[1]: 3}, woven, short_conv)

    def band(woven):
        with ExitStack() as outer:
            edge = sb(outer, "bd_edge", [P, BAND])
            barrier()
            G.mark(G.then().memset(edge[:], 0.0))
            G.mark(G.then().memset(edge[0:64, LEFT + 64:], -1e30))
            G.mark(G.then().memset(edge[64:P, 0:64], -1e30))
            barrier()

            def head_bias(at):
                rel = sb(at, "bd_rel", [P, BAND])

                def ready(i):
                    got = load.mark(SP.dma_start(rel[:], t["rel"][i]))
                    return V.mark(V.after(got).tensor_tensor(rel[:], rel[:], edge[:], ALU.add))
                return rel, ready

            def add_bias(sc, psum, rel, q0, k0, k1):
                off = k0 - (q0 - LEFT)
                return V.mark(nc.vector.scalar_tensor_tensor(sc, psum, HD ** -0.5, rel[:, off:], ALU.mult, ALU.add))

            attention(BAND_HEADS, 2, [(n * P, max(0, n * P - LEFT), (n + 1) * P) for n in range(8)], proj2,
                      (AQ, AK, AV), mixed2, 0, head_bias, add_bias, "band",
                      {V: 84, A: 44, PE: 62, load: 128, stores[0]: 32, outs[0]: 64, outs[1]: 64, pair_read[0]: 4,
                       pair_read[1]: 4}, woven)

    def s5(w):
        barrier()
        RE, IM = 0, 1
        with ExitStack() as keep:
            wl = sb(keep, "s5_wl", [P, PAIRS, 2, P])
            cl = sb(keep, "s5_cl", [P, PAIRS, 2, T + 1, S5_H])
            dl = sb(keep, "s5_dl", [P, S5_G, P])
            scan = sb(keep, "s5_scan", [P, LEVELS, 3, PAIRS])
            with ExitStack() as at:
                pw = sb(at, "s5_pw", [P, T + 1, 2, PAIRS])
                tm = sb(at, "s5_tm", [P, 12, PAIRS])
                bb = sb(at, "s5_b", [P, 4, PAIRS, S5_H])
                cc = sb(at, "s5_c", [P, 2, PAIRS, S5_H])
                tmp = sb(at, "s5_tmp", [P, 2, PAIRS, S5_H])
                dg = sb(at, "s5_dg", [S5_H, S5_G])
                load.mark(SP.dma_start(bb[:, 0:2, :, :], t["s5_b"]))
                load.mark(SP.dma_start(cc[:], t["s5_c"]))
                got = load.mark(SP.dma_start(dg[:], t["s5_d"]))
                a_re, a_im, log_dt = (vec[:, VEC[n][0]:VEC[n][0] + PAIRS] for n in ("a_re", "a_im", "log_dt"))

                def tt(o, x, y, op):
                    point(0.35)
                    return V.mark(V.then().tensor_tensor(o, x, y, op))

                def ts(o, x, s1, op, s2=None, op2=None):
                    if op2 is None:
                        return V.mark(V.then().tensor_scalar(o, x, s1, None, op))
                    return V.mark(V.then().tensor_scalar(o, x, s1, s2, op, op2))

                def cmul(ore, oim, xre, xim, yre, yim, t0, t1):
                    tt(t0, xre, yre, ALU.mult)
                    tt(t1, xim, yim, ALU.mult)
                    tt(ore, t0, t1, ALU.subtract)
                    tt(t0, xre, yim, ALU.mult)
                    tt(t1, xim, yre, ALU.mult)
                    return tt(oim, t0, t1, ALU.add)

                r = [tm[:, n, :] for n in range(12)]
                V.after(got)
                lre, dt, ang, turn, mag, cos, sin = r[0:7]
                ts(lre, a_re, -1e-4, ALU.min)
                a = A.mark(A.after(V.last()).activation(dt, log_dt, ACT.Exp))
                V.after(a)
                tt(mag, lre, dt, ALU.mult)
                a = A.mark(A.after(V.last()).activation(mag, mag, ACT.Exp))
                tt(ang, a_im, dt, ALU.mult)
                ts(turn, ang, 1.0 / (2 * math.pi), ALU.mult)
                ts(turn, turn, 12582912.0, ALU.add)
                ts(turn, turn, 12582912.0, ALU.subtract)
                for part in (6.28125, 1.9353071693331003e-3, 1.0253259e-11):
                    V.mark(V.then().scalar_tensor_tensor(ang, turn, -part, ang, ALU.mult, ALU.add))
                ts(ang, ang, 3.1415925, ALU.min, -3.1415925, ALU.max)
                a = A.mark(A.after(V.last()).activation(sin, ang, ACT.Sin))
                a = A.mark(A.then().activation(cos, ang, ACT.Abs))
                V.after(a)
                ts(cos, cos, -1.0, ALU.mult, math.pi / 2, ALU.add)
                a = A.mark(A.after(V.last()).activation(cos, cos, ACT.Sin))
                V.after(a)
                V.mark(V.then().memset(pw[:, 0, RE, :], 1.0))
                V.mark(V.then().memset(pw[:, 0, IM, :], 0.0))
                tt(pw[:, 1, RE, :], mag, cos, ALU.mult)
                tt(pw[:, 1, IM, :], mag, sin, ALU.mult)
                for j in range(2, T + 1):
                    cmul(pw[:, j, RE, :], pw[:, j, IM, :], pw[:, j - 1, RE, :], pw[:, j - 1, IM, :],
                         pw[:, 1, RE, :], pw[:, 1, IM, :], r[7], r[8])
                V.mark(V.then().tensor_copy(scan[:, 0, 0:2, :], pw[:, T, :, :]))
                for n in range(1, LEVELS):
                    cmul(scan[:, n, RE, :], scan[:, n, IM, :], scan[:, n - 1, RE, :], scan[:, n - 1, IM, :],
                         scan[:, n - 1, RE, :], scan[:, n - 1, IM, :], r[7], r[8])
                nre, d, cre, cim, nim = r[7], r[8], r[9], r[10], r[11]
                tt(d, lre, lre, ALU.mult)
                tt(nim, a_im, a_im, ALU.mult)
                tt(d, d, nim, ALU.add)
                V.mark(V.then().reciprocal(d, d))
                ts(nre, pw[:, 1, RE, :], 1.0, ALU.subtract)
                tt(cre, nre, lre, ALU.mult)
                tt(nim, pw[:, 1, IM, :], a_im, ALU.mult)
                tt(cre, cre, nim, ALU.add)
                tt(cim, pw[:, 1, IM, :], lre, ALU.mult)
                tt(nim, nre, a_im, ALU.mult)
                tt(cim, cim, nim, ALU.subtract)
                tt(cre, cre, d, ALU.mult)
                tt(cim, cim, d, ALU.mult)

                def over_h(x):
                    return x.unsqueeze(2).to_broadcast([P, PAIRS, S5_H])

                t0, t1 = tmp[:, 0, :, :], tmp[:, 1, :, :]
                cmul(bb[:, 2, :, :], bb[:, 3, :, :], bb[:, 0, :, :], bb[:, 1, :, :], over_h(cre), over_h(cim), t0, t1)
                short = ExitStack()
                wp = sb(short, "s5_wp", [P, 2, PAIRS, T, S5_H])
                for j in range(T):
                    cmul(wp[:, RE, :, j, :], wp[:, IM, :, j, :], bb[:, 2, :, :], bb[:, 3, :, :],
                         over_h(pw[:, T - 1 - j, RE, :]), over_h(pw[:, T - 1 - j, IM, :]), t0, t1)
                wp_ready = V.last()
                for j in range(T + 1):
                    cmul(cl[:, :, RE, j, :], cl[:, :, IM, j, :], cc[:, 0, :, :], cc[:, 1, :, :],
                         over_h(pw[:, j, RE, :]), over_h(pw[:, j, IM, :]), t0, t1)
                    ts(cl[:, :, IM, j, :], cl[:, :, IM, j, :], -1.0, ALU.mult)
                v = V.last()
                wl_ready = transposes(wl[:].rearrange("p a c n -> p (a c) n"),
                                      lambda j: wp[:, j % 2, j // 2, :, :].rearrange("p a b -> p (a b)"),
                                      2 * PAIRS, P, wp_ready)
                short.close()
                kp = sb(at, "s5_kp", [S5_H, S5_G, 2 * T - 1, S5_H])
                V.mark(V.then(wl_ready).memset(kp[:, :, 0:T - 1, :], 0.0))
                copied = wl_ready
                for p0 in range(0, PAIRS, 4):
                    PE.after(v, copied)
                    for pr in range(p0, p0 + 4):
                        for g in range(2):
                            row = S5_P * g
                            for c in (RE, IM):
                                last = nc.tensor.matmul(bank[g][0:S5_H, (pr - p0) * P:(pr - p0 + 1) * P],
                                                        bb[row:row + S5_P, 2 + c, pr, :],
                                                        cl[row:row + S5_P, pr, c, 0:T, :].rearrange("p a b -> p (a b)"),
                                                        start=c == RE, stop=c == IM)
                    ready = PE.mark(last)
                    for g in range(2):
                        copied = V.mark(V.after(ready).tensor_copy(
                            kp[:, 2 * p0 + g:2 * p0 + 8:2, T - 1:, :].rearrange("p g a b -> p g (a b)"),
                            bank[g][0:S5_H, :].rearrange("p (g n) -> p g n", g=4)))
                skip = tmp[0:S5_H, :, :, :].rearrange("p a b c -> p (a b) c")
                tt(skip, ident[0:S5_H, 0:S5_H].unsqueeze(1).to_broadcast([S5_H, S5_G, S5_H]),
                   dg[:].unsqueeze(2).to_broadcast([S5_H, S5_G, S5_H]), ALU.mult)
                v = tt(kp[:, :, T - 1, :], kp[:, :, T - 1, :], skip, ALU.add)
                SP.wait_ge(*v)
                for j in range(T):
                    load.mark(SP.dma_start(dl[j * S5_H:(j + 1) * S5_H, :, :].rearrange("p g (a b) -> p g a b", a=T),
                                           kp[:, :, T - 1 - j:2 * T - 1 - j, :]))
                barrier()
            w.upto(5 * KT + 1)
            fox_logs()
            point(8)
            with ExitStack() as at:
                u = sb(at, "s5_ut", [P, 2, L])
                uc = sb(at, "s5_uc", [P, S5_G, CH])
                tg = [sb(at, f"s5_t{n}", [P, 5, CH]) for n in range(2)]
                x = [[sb(at, f"s5_x{c}", [P, PAIRS, CH]) for c in "ri"], [wl[:, :, c, :] for c in range(2)]]
                for o in outs:
                    SP.wait_ge(*o.last())
                for n in range(4):
                    s = n % 2
                    SP.wait_ge(*stores[s].last())
                    a = loads[s].mark(SP.dma_start(u[:, s, :], proj1[U_ + n]))
                    v = V.mark(V.after(a).tensor_copy(x[0][s][:, 0:T, :], u[:, s, :].rearrange("p (m j) -> p j m", j=T)))
                    SP.wait_ge(*v)
                    stores[s].mark(SP.dma_start(s5_u.rearrange("(n p) j m -> n p j m", p=P)[n], x[0][s][:, 0:T, :]))
                for s in stores:
                    SP.wait_ge(*s.last())
                for j in range(T):
                    got = load.mark(SP.dma_start(uc[j * S5_H:(j + 1) * S5_H, :, :],
                                                 s5_u[:, j, :].rearrange("(g h) m -> h g m", h=S5_H)))
                point(20)
                read = V.last()
                for pr in range(0, PAIRS, 4):
                    for c in (RE, IM):
                        point()
                        PE.after(got, read)
                        for n in range(4):
                            for g in range(2):
                                last = nc.tensor.matmul(bank[c][g * S5_P:(g + 1) * S5_P, n * CH:(n + 1) * CH],
                                                        wl[:, pr + n, c, g * S5_P:(g + 1) * S5_P],
                                                        uc[:, 2 * (pr + n) + g, :], start=True, stop=True)
                        ready = PE.mark(last)
                        read = V.mark(V.after(ready).tensor_copy(
                            x[0][c][:, pr:pr + 4, :], bank[c][:].rearrange("p (n m) -> p n m", n=4)))
                tv = [u[:, n, :].rearrange("p (a b) -> p a b", a=8) for n in range(2)]
                G.after(V.last())
                for n in range(LEVELS):
                    sh = 1 << n
                    old, new = x[n % 2], x[(n + 1) % 2]
                    w = CH - sh
                    for lane, (t0, t1), parts in ((G, tg, ((11, 16),)), (V, tv, ((0, 6), (6, 11)))):
                        lo, hi = parts[0][0], parts[-1][1]
                        for c in range(2):
                            lane.mark(lane.then().tensor_copy(new[c][:, lo:hi, 0:sh], old[c][:, lo:hi, 0:sh]))
                        for p0, p1 in parts:
                            m = p1 - p0
                            ar, ai = (scan[:, n, c, p0:p1].unsqueeze(2).to_broadcast([P, m, w]) for c in range(2))
                            xr, xi = (old[c][:, p0:p1, 0:w] for c in range(2))
                            s0, s1 = t0[:, 0:m, 0:w], t1[:, 0:m, 0:w]
                            for c, (f0, f1, op) in enumerate((((xr, ar), (xi, ai), ALU.subtract),
                                                              ((xi, ar), (xr, ai), ALU.add))):
                                if lane is V:
                                    point(2.1)
                                lane.mark(lane.then().tensor_tensor(s0, *f0, ALU.mult))
                                lane.mark(lane.then().tensor_tensor(s1, *f1, ALU.mult))
                                lane.mark(lane.then().tensor_tensor(s0, s0, s1, op))
                                lane.mark(lane.then().tensor_tensor(new[c][:, p0:p1, sh:], old[c][:, p0:p1, sh:],
                                                                    s0, ALU.add))
                state = x[LEVELS % 2]
                scanned = V.last()
                PE.after(G.last())
                y = [x[(LEVELS + 1) % 2][c][:] for c in range(2)]
                read = None
                for p0 in range(0, PAIRS, 4):
                    point(2)
                    PE.after(scanned, read)
                    for pr in range(p0, p0 + 4):
                        for g in range(2):
                            row, o, ps = S5_P * g, (pr - p0) * CH, bank[g]
                            nc.tensor.matmul(ps[:, o:o + CH], dl[:, 2 * pr + g, :], uc[:, 2 * pr + g, :],
                                             start=True, stop=False)
                            for c in (RE, IM):
                                last = nc.tensor.matmul(ps[:, o + 1:o + CH],
                                                        cl[row:row + S5_P, pr, c, 1:, :].rearrange("p a b -> p (a b)"),
                                                        state[c][row:row + S5_P, pr, 0:CH - 1],
                                                        start=False, stop=c == IM)
                    ready = PE.mark(last)
                    for g in range(2):
                        g0 = 2 * p0 % 16 + g
                        read = V.mark(V.after(ready).tensor_copy(y[p0 // 8][:, g0:g0 + 7:2, :],
                                                                 bank[g][:].rearrange("p (n m) -> p n m", n=4)))
                SP.wait_ge(*read)
                s5_y_v = s5_y.rearrange("(c g h) j m -> c j h g m", c=2, h=S5_H)
                for c in range(2):
                    for j in range(T):
                        store.mark(SP.dma_start(s5_y_v[c, j], y[c][j * S5_H:(j + 1) * S5_H, :, :]))
                SP.wait_ge(*store.last())
                barrier()
                point(10)
                z, gates = ([uc[:, g + T * c:g + T * c + T, :].rearrange("p a b -> p (a b)") for c in range(2)]
                            for g in (0, 2 * T))
                glu = sb(at, "s5_glu", [P, 4, P])
                w_here = load.mark(SP.dma_start(glu[:], t["glu"].rearrange("n p k -> p n k")))
                read = None
                for n in range(4):
                    s = n % 2
                    point(8)
                    SP.wait_ge(*V.last())
                    a = loads[s].mark(SP.dma_start(z[s], s5_y.rearrange("(n p) j m -> n p (j m)", p=P)[n]))
                    a = A.mark(A.after(a).activation(z[s], z[s], ACT.Gelu_apprx_tanh))
                    PE.after(a, w_here, read)
                    for h in range(2):
                        last = nc.tensor.matmul(wide[:, h * HALF:(h + 1) * HALF], glu[:, n, :],
                                                z[s][:, h * HALF:(h + 1) * HALF], start=True, stop=True)
                    ready = PE.mark(last)
                    read = A.mark(A.after(ready).activation(gates[s], wide[:], ACT.Sigmoid))
                    v = V.mark(V.after(read, stores[s].last()).tensor_tensor(
                        u[:, s, :].rearrange("p (m j) -> p j m", j=T), z[s].rearrange("p (j m) -> p j m", j=T),
                        gates[s].rearrange("p (j m) -> p j m", j=T), ALU.mult))
                    SP.wait_ge(*v)
                    stores[s].mark(SP.dma_start(mixed1[n], u[:, s, :]))
                point(8)
                barrier()

    def hgrn_constants(at):
        masks = sb(at, "hg_mask", [P, LEVELS + 1, P])
        reset = sb(at, "hg_reset", [P, L])
        heads = sb(at, "hg_heads", [P, P])
        lb = sb(at, "hg_lb", [P, 3, 2])
        for n in range(LEVELS):
            w = P >> (n + 1)
            m = masks[:, n, :].rearrange("p (a b c) -> p a b c", b=2, c=w)[:, :, 1, :]
            G.mark(G.then().memset(masks[:, n, :], 0.0))
            G.mark(G.then().memset(m, 1.0))
            G.mark(G.then().affine_select(out=m, in_=m, compare_op=ALU.is_ge, fill=0.0, base=0,
                                          pattern=[[-2 * w, P // (2 * w)], [0, w]], channel_multiplier=1))
            G.mark(G.then().affine_select(out=m, in_=m, compare_op=ALU.is_ge, fill=0.0, base=w - 1,
                                          pattern=[[2 * w, P // (2 * w)], [0, w]], channel_multiplier=-1))
        G.mark(G.then().tensor_copy(masks[:, LEVELS, :], ident[:]))
        G.mark(G.then().memset(reset[:], 1.0))
        G.mark(G.then().memset(reset[:].rearrange("p (a b) -> p a b", b=P)[:, :, 0:1], 0.0))
        G.mark(G.then().memset(heads[:], 0.0))
        G.mark(G.then().memset(heads[0:HD, 0:HD], 1.0))
        G.mark(G.then().memset(heads[HD:P, HD:P], 1.0))
        G.then()
        x, oml, tmp = lb[:, 0, :], lb[:, 1, :], lb[:, 2, :]
        logits = vec[:, VEC["lb"][0]:VEC["lb"][0] + 2]
        v = V.mark(nc.vector.tensor_tensor(x, logits, logits, ALU.subtract))
        a = A.mark(A.after(v).activation(x, x, ACT.Exp))
        V.mark(V.after(a).reciprocal(tmp, x))
        V.mark(V.then().tensor_tensor(tmp, tmp, x, ALU.mult))
        V.mark(V.then().tensor_tensor(x, tmp, tmp, ALU.subtract))
        V.mark(V.then().tensor_scalar(oml, x, -1.0, 1.0, ALU.mult, ALU.add))
        return masks, reset, heads, lb

    def hgrn(constants, woven):
        barrier()
        NT = L // P
        with ExitStack() as at:
            q, f, vi, g, kf, b, e, t0, t1, o = (sb(at, "hg_" + n, [P, L]) for n in
                                                ("q", "f", "v", "g", "k", "b", "e", "t0", "t1", "o"))
            sc = sb(at, "hg_sc", [P, NT, 2, P])
            vt, kt = sb(at, "hg_vt", [P, NT, P]), sb(at, "hg_kt", [P, NT, P])
            st = sb(at, "hg_st", [P, NT + 1, HD])
            dec = sb(at, "hg_dec", [P, NT])
            masks, reset, heads, lb = constants
            G.mark(G.then().memset(st[:, 0, :], 0.0))
            barrier()

            def tt(out, x, y, op, *after):
                return V.mark(V.then(*after).tensor_tensor(out, x, y, op))

            def act(out, x, fn, *after, **kw):
                return A.mark(A.then(V.last(), *after).activation(out, x, fn, **kw))

            per = {V: 83, A: 34, G: 28, PE: 41, load: 64, stores[0]: 16, outs[0]: 80, outs[1]: 80,
                   pair_read[0]: 5, pair_read[1]: 5}
            with loop(nc, 2, per) as i, woven(i):
                for m in (V, A, G, PE):
                    SP.wait_ge(*m.last())
                for buf, row in ((q, BQ), (f, BF), (vi, BI), (g, BG)):
                    load.mark(SP.dma_start(buf[:], proj2[i + row]))
                got = load.last()
                point(10)
                V.after(got, stores[0].last())
                lbc, omc = (lb[:, n, bass.ds(i, 1)] for n in range(2))
                act(q[:], q[:], ACT.Silu, got)
                act(g[:], g[:], ACT.Silu)
                act(kf[:], f[:], ACT.Sigmoid, scale=-1.0)
                a = act(f[:], f[:], ACT.Sigmoid)
                V.mark(V.then(a).tensor_scalar(kf[:], kf[:], omc, None, ALU.mult))
                V.mark(V.then().tensor_scalar(f[:], f[:], omc, lbc, ALU.mult, ALU.add))
                V.mark(V.then().tensor_scalar(t0[:], f[:], LOG_FLOOR, 2.0 ** -60, ALU.max, ALU.max))
                V.mark(V.then().tensor_scalar(t1[:], f[:], LOG_FLOOR, 2.0 ** 60, ALU.max, ALU.mult))
                V.mark(V.then().tensor_scalar(t1[:], t1[:], 1.0, None, ALU.min))
                act(t0[:], t0[:], ACT.Ln)
                a = act(t1[:], t1[:], ACT.Ln)
                tt(t0[:], t0[:], t1[:], ALU.add, a)
                V.mark(V.then().tensor_tensor_scan(b[:], reset[:], t0[:], 0.0, ALU.mult, ALU.add))
                def exponents(n):
                    w = P >> (n + 1)
                    b4, e4 = (x[:].rearrange("p (a c w) -> p a c w", c=2, w=w) for x in (b, e))
                    mid = b4[:, :, 0, w - 1:w].to_broadcast([P, L // (2 * w), w])
                    tt(e4[:, :, 1, :], b4[:, :, 1, :], mid, ALU.subtract)
                    tt(e4[:, :, 0, :], mid, b4[:, :, 0, :], ALU.subtract)
                    return act(e[:], e[:], ACT.Exp)

                def factors(exps, used_up):
                    tt(t0[:], q[:], e[:], ALU.mult, exps, used_up)
                    return tt(t1[:], kf[:], e[:], ALU.mult)

                ready, (qx, kx) = factors(exponents(0), PE.last()), (t0, t1)
                for n in range(LEVELS + 1):
                    point(6)
                    if n == LEVELS:
                        ready, (qx, kx) = V.last(), (q, kf)
                    done = []
                    banks = (wide[:, 0:HALF], wide[:, HALF:L], bank[0][:], bank[1][:])
                    for n2, ps in enumerate(banks):
                        PE.after(ready, sc_read[n2] if n else None)
                        for m in range(4):
                            tile, h = 4 * (n2 // 2) + m, n2 % 2
                            last = nc.tensor.matmul(ps[:, m * P:(m + 1) * P],
                                                    kx[h * HD:(h + 1) * HD, tile * P:(tile + 1) * P],
                                                    qx[h * HD:(h + 1) * HD, tile * P:(tile + 1) * P],
                                                    start=True, stop=True)
                        done.append(PE.mark(last))
                    if n + 1 < LEVELS:
                        exps = exponents(n + 1)
                    for n2, ps in enumerate(banks):
                        dst = sc[:, 4 * (n2 // 2):4 * (n2 // 2) + 4, n2 % 2, :]
                        src = ps.rearrange("p (m n) -> p m n", n=P)
                        mk = masks[:, n, :].unsqueeze(1).to_broadcast([P, 4, P])
                        if n == 0:
                            sc_read[n2] = tt(dst, src, mk, ALU.mult, done[n2])
                        else:
                            part = o[:, (n2 % 2) * HALF:(n2 % 2 + 1) * HALF].rearrange("p (m n) -> p m n", n=P)
                            sc_read[n2] = tt(part, src, mk, ALU.mult, done[n2], sc_add[n2 % 2])
                            sc_add[n2 % 2] = G.mark(G.then(sc_read[n2]).tensor_tensor(dst, dst, part, ALU.add))
                    if n == 0:
                        sc_add[0] = sc_add[1] = V.last()
                    if n + 1 < LEVELS:
                        ready = factors(exps, done[-1])
                b3, t3 = (x[:].rearrange("p (a n) -> p a n", n=P) for x in (b, t1))
                blast = b3[:, :, P - 1:P]
                tt(t3, blast.to_broadcast([P, NT, P]), b3, ALU.subtract, PE.last())
                act(t1[:], t1[:], ACT.Exp)
                act(e[:], b[:], ACT.Exp)
                a = act(dec[:], blast.rearrange("p a n -> p (a n)"), ACT.Exp)
                tt(t1[:], t1[:], kf[:], ALU.mult, a)
                ready = tt(t0[:], q[:], e[:], ALU.mult)
                point(4)
                transposes(vt, lambda j: vi[:, j * P:(j + 1) * P], NT, P, ready)
                done = transposes(kt, lambda j: t1[:, j * P:(j + 1) * P], NT, P, A.last())
                point(3)
                PE.after(done)
                for n in range(NT):
                    for h in range(2):
                        last = nc.tensor.matmul(bank[1][h * HD:(h + 1) * HD, n * HD:(n + 1) * HD],
                                                kt[:, n, h * HD:(h + 1) * HD], vt[:, n, h * HD:(h + 1) * HD],
                                                start=True, stop=True)
                pr = PE.mark(last)
                V.after(pr)
                point(5)
                for n in range(NT):
                    V.mark(V.then().scalar_tensor_tensor(st[:, n + 1, :], st[:, n, :], dec[:, n:n + 1],
                                                         bank[1][:, n * HD:(n + 1) * HD], ALU.mult, ALU.add))
                point(3)
                PE.after(V.last(), sc_add[0], sc_add[1])
                for n in range(NT):
                    for h in range(2):
                        row = slice(h * HD, (h + 1) * HD)
                        nc.tensor.matmul(wide[row, n * P:(n + 1) * P], vt[:, n, row], sc[:, n, h, :],
                                         start=True, stop=False)
                        last = nc.tensor.matmul(wide[row, n * P:(n + 1) * P], st[row, n, :], t0[row, n * P:(n + 1) * P],
                                                start=False, stop=True)
                pr = PE.mark(last)
                v = V.mark(V.then(pr).tensor_copy(o[:], wide[:]))
                a = act(t1[:], o[:], ACT.Square)
                point(2)
                spread = spread_inv_sqrt(e, 1.0 / HD, token_sums(t1[:], a, heads[:, 0:P:HD]), g=2)
                point(5)
                gain = vec[:, bass.ds(i + VEC["hgrn_g"][0], 1)]
                V.mark(V.then(spread).scalar_tensor_tensor(o[:], o[:], gain, e[:], ALU.mult, ALU.mult))
                v = tt(o[:], o[:], g[:], ALU.mult)
                SP.wait_ge(*v)
                stores[0].mark(SP.dma_start(mixed2[i + 2], o[:]))
            barrier()

    sc_read, sc_add = {}, {}

    def gmlp():
        barrier()
        NT = L // P
        with ExitStack() as at:
            u, v = sb(at, "gm_u", [P, 2, L]), sb(at, "gm_v", [P, 2, L])
            sq, rstd = sb(at, "gm_sq", [P, 2, L]), sb(at, "gm_r", [P, L])
            vt = sb(at, "gm_vt", [P, 2, NT, P])
            w, b = sb(at, "gm_w", [P, 4, P]), sb(at, "gm_b", [P, 2, P])
            load.mark(SP.dma_start(u[:], proj2[CU:CU + 2].rearrange("k p n -> p k n")))
            load.mark(SP.dma_start(v[:], proj2[CV:CV + 2].rearrange("k p n -> p k n")))
            load.mark(SP.dma_start(w[:], t["gm_w"].rearrange("g q p -> q g p")))
            for g in range(4):
                got = load.mark(SP.dma_start(b[(g % 2) * HD:(g % 2 + 1) * HD, g // 2, :],
                                             t["gm_b"][g].partition_broadcast(HD)))
            point(8)
            causal_w = G.mark(G.after(got).affine_select(out=w[:], in_=w[:], compare_op=ALU.is_ge, fill=0.0, base=0,
                                                         pattern=[[0, 4], [1, P]], channel_multiplier=-1))
            A.mark(A.after(got).activation(v[:], v[:], ACT.Gelu_apprx_tanh))
            a = A.mark(A.then().activation(u[:], u[:], ACT.Gelu_apprx_tanh))
            point(6)
            for k in range(2):
                a = A.mark(A.then().activation(sq[:, k, :], v[:, k, :], ACT.Square))
                sums = row_sums(sq[:, k, :], k, 2, a)
            r = spread_inv_sqrt(rstd, 1.0 / 256, sums, rows=True)
            point(8)
            for k in range(2):
                n = V.mark(V.after(r).scalar_tensor_tensor(v[:, k, :], v[:, k, :], col("gmlp_g", k), rstd[:],
                                                           ALU.mult, ALU.mult))
            vt_ready = None
            for k in range(2):
                vt_ready = transposes(vt[:, k, :, :], lambda j, k=k: v[:, k, j * P:(j + 1) * P], NT, P, n, free=vt_ready)
            PE.after(vt_ready, causal_w)
            for k in range(2):
                for n in range(NT):
                    for g in range(2):
                        last = nc.tensor.matmul(wide[g * HD:(g + 1) * HD, n * P:(n + 1) * P],
                                                vt[:, k, n, g * HD:(g + 1) * HD], w[:, 2 * k + g, :],
                                                start=True, stop=True)
                ready = PE.mark(last)
                point(3)
                o = V.mark(V.after(ready).tensor_tensor(
                    sq[:, k, :].rearrange("p (n m) -> p n m", m=P), wide[:].rearrange("p (n m) -> p n m", m=P),
                    b[:, k, :].unsqueeze(1).to_broadcast([P, NT, P]), ALU.add))
                PE.after(o)
                o = V.mark(V.then().tensor_tensor(sq[:, k, :], sq[:, k, :], u[:, k, :], ALU.mult))
                SP.wait_ge(*o)
                store.mark(SP.dma_start(mixed2[4 + k], sq[:, k, :]))
            barrier()

    def lru():
        barrier()
        with ExitStack() as at:
            x, gate, xc, r, ig, la, m = (sb(at, "lr_" + n, [P, 2, L]) for n in ("x", "g", "xc", "r", "i", "la", "m"))
            wa, wx = sb(at, "lr_wa", [P, 2, P]), sb(at, "lr_wx", [P, 2, P])
            sp = sb(at, "lr_sp", [P, 4, 2])
            load.mark(SP.dma_start(wa[:], t["lru_w"][0].rearrange("k p n -> p k n")))
            load.mark(SP.dma_start(wx[:], t["lru_w"][1].rearrange("k p n -> p k n")))
            load.mark(SP.dma_start(x[:], proj2[DX:DX + 2].rearrange("k p n -> p k n")))
            got = load.mark(SP.dma_start(gate[:], proj2[DG:DG + 2].rearrange("k p n -> p k n")))
            point(8)
            lam = vec[:, VEC["lru_lam"][0]:VEC["lru_lam"][0] + 2]
            a = A.mark(nc.scalar.activation(sp[:, 0, :], lam, ACT.Abs))
            a = A.mark(A.then().activation(sp[:, 0, :], sp[:, 0, :], ACT.Exp, scale=-1.0))
            log1p(sp[:, 0, :], (sp[:, 1, :], sp[:, 2, :]), a)
            V.mark(V.then().tensor_scalar(sp[:, 1, :], lam, -1.0, 0.0, ALU.mult, ALU.max))
            V.mark(V.then().tensor_tensor(sp[:, 0, :], sp[:, 0, :], sp[:, 1, :], ALU.add))
            V.mark(V.then().tensor_scalar(sp[:, 3, :], sp[:, 0, :], -LRU_C, None, ALU.mult))
            V.after(got)
            convolved, sigmoids, read = [], [], None
            for k in range(2):
                V.mark(V.then().tensor_scalar(xc[:, k, :], x[:, k, :], col("lru_cw", 3 * 2 + k), col("lru_cb", k),
                                              ALU.mult, ALU.add))
                for back in (1, 2, 3):
                    V.mark(V.then().scalar_tensor_tensor(xc[:, k, back:], x[:, k, :L - back],
                                                         col("lru_cw", (3 - back) * 2 + k), xc[:, k, back:],
                                                         ALU.mult, ALU.add))
                convolved.append(V.last())
            for k in range(2):
                point(8 if k else 6)
                for w, dst, bias in ((wa, r, "lru_ba"), (wx, ig, "lru_bx")):
                    PE.after(convolved[k], read)
                    for h in range(2):
                        last = nc.tensor.matmul(wide[:, h * HALF:(h + 1) * HALF], w[:, k, :],
                                                xc[:, k, h * HALF:(h + 1) * HALF], start=True, stop=True)
                    ready = PE.mark(last)
                    point(2)
                    read = A.mark(A.then(ready).activation(dst[:, k, :], wide[:], ACT.Sigmoid, bias=col(bias, k)))
            for fn, dst in ((ACT.Tanh, la), (ACT.Exp, r)):
                for k in range(2):
                    a = A.mark(A.then(V.last()).activation(dst[:, k, :], r[:, k, :], fn, scale=sp[:, 3, k:k + 1]))
            V.mark(V.then(a).tensor_tensor(m[:], r[:], r[:], ALU.mult))
            V.mark(V.then().scalar_tensor_tensor(m[:], m[:], 1.0, la[:], ALU.add, ALU.mult))
            v = V.mark(V.then().tensor_scalar(m[:], m[:], -1.0, 0.0, ALU.mult, ALU.max))
            root = A.mark(A.then(v).activation(m[:], m[:], ACT.Sqrt))
            gelu = A.mark(A.then().activation(gate[:], gate[:], ACT.Gelu_apprx_tanh))
            V.mark(V.then().tensor_tensor(ig[:], ig[:], xc[:], ALU.mult))
            V.mark(V.then(root).memset(m[:, :, 0:1], 1.0))
            V.mark(V.then().tensor_tensor(m[:], m[:], ig[:], ALU.mult))
            for k in range(2):
                V.mark(V.then().tensor_tensor_scan(xc[:, k, :], r[:, k, :], m[:, k, :], 0.0, ALU.mult, ALU.add))
                v = V.mark(V.then(gelu).tensor_tensor(xc[:, k, :], xc[:, k, :], gate[:, k, :], ALU.mult))
                SP.wait_ge(*v)
                store.mark(SP.dma_start(mixed2[6 + k], xc[:, k, :]))
            point(24)
            barrier()

    def merge(mixed, proj, gate_row, branches, name):
        tiles = 12 // branches if branches == 3 else 2
        blocks = 4 if branches == 3 else 2
        units = branches * tiles * blocks // 8
        n_in = branches * tiles
        barrier()
        with ExitStack() as at:
            mh, ml = sb(at, name + "h", [P, n_in, L], F32R), sb(at, name + "l", [P, n_in, L], F32R)
            split = []
            for n in range(n_in):
                x = (act_hi if n < KT else act_lo)[:, n % KT, :].bitcast(F32)
                if n > 1:
                    SP.wait_ge(*loads[n % 2].last())
                split.append(split_act(x, mh[:, n, :], ml[:, n, :], loads[n % 2].mark(SP.dma_start(x, mixed[n]))))
            gates = sb(at, name + "g", [P, branches, L])
            m = sb(at, name + "m", [P, L])
            parts = [rs, rs]
            if branches == 4:
                parts[1] = sb(at, name + "p", [P, L])
            for br in range(branches):
                gate_in[br].mark(SP.dma_start(gates[:, br, :], proj[gate_row + 8 * br]))

            def rhs(o, k):
                n = (o % branches) * tiles + k
                if o < branches:
                    PE.after(split[n])
                return mh[:, n, :], ml[:, n, :]

            def evict(i, o, psum, ready, read):
                block, br = o // branches, o % branches
                part = parts[br % 2]
                if br == 0:
                    done = read(V.then(ready, gate_in[br].last()).tensor_tensor(m[:], gates[:, br, :], psum[:], ALU.mult))
                else:
                    free = (G.sem, G.n - (parts[0] is not parts[1] and br > 1))
                    done = read(V.then(ready, gate_in[br].last(), free)
                                .tensor_tensor(part[:], gates[:, br, :], psum[:], ALU.mult))
                    if br < branches - 1:
                        G.mark(G.then(done).tensor_tensor(m[:], m[:], part[:], ALU.add))
                    else:
                        V.mark(V.after(done, G.last()).tensor_tensor(m[:], m[:], part[:], ALU.add))
                SP.wait_ge(*done)
                gate_in[br].mark(SP.dma_start(gates[:, br, :], proj[i * blocks + (gate_row + 8 * br + block + 1)]))
                if br == branches - 1:
                    at_ = bass.ds(i * blocks + block, 1)
                    hi, lo = (x[:, at_, :].rearrange("p a n -> p (a n)") for x in (act_hi, act_lo))
                    a = A.mark(A.after(V.last()).copy(hi, m[:]))
                    V.mark(V.after(a).tensor_tensor(lo, m[:], hi.bitcast(F32), ALU.subtract))

            per = {G: blocks * (branches - 2), A: blocks, V: 2 * blocks, PE: blocks * branches - units}
            per.update({gate_in[br]: 16 * blocks for br in range(branches)})
            stage(KT // blocks, units, blocks * branches, tiles, rhs, evict, per=per)
            for br in range(branches):
                SP.wait_ge(*gate_in[br].last())
            barrier()

    gate_in = [Count(sem(f"gate_in{n}")) for n in range(4)]

    def mix_out(x_dram, gain, out_dram, next_gain, name, ahead_turns):
        with ExitStack() as at:
            y, sq, squares = (sb(at, name + n, w) for n, w in (("y", [P, KT, L]), ("q", [P, L]), ("ss", [P, L])))
            G.mark(G.then().memset(squares[:], 0.0))
            merged = V.last()
            nc.tensor.wait_ge(V.sem, V.n - 2)

            def rhs(o, k):
                if o == 0 and k == KT - 1:
                    PE.after(merged)
                return act_rhs(o, k)

            def evict(i, o, psum, ready, read):
                dst = y[:, bass.ds(i * 2 + o, 1), :].rearrange("p a n -> p (a n)")
                square_sum(dst, sq[:], squares[:], read(V.after(ready).tensor_copy(dst, psum[:])))

            stage(4, 2, 2, KT, rhs, evict, per={A: 2, G: 2})
            ahead = Ahead(ahead_turns)
            bridge(y, squares, x_dram, gain, out_dram, next_gain, name, ahead)
            return ahead

    def mlp(ahead, x_dram, gain, out_dram, next_gain, groups, gated, name, ahead_turns=0):
        with ExitStack() as at:
            acc, sq, squares = (sb(at, name + n, w) for n, w in (("acc", [P, KT, L]), ("q", [P, L]), ("ss", [P, L])))
            G.mark(G.then().memset(squares[:], 0.0))
            with ExitStack() as inner:
                hh, hl = sb(inner, name + "hh", [P, 8, L], F32R), sb(inner, name + "hl", [P, 8, L], F32R)
                x = sb(inner, name + "v", [P, 2, L])

                def hidden_done(index, s, mark):
                    hi, lo = (h[:, bass.ds(index, 1), :].rearrange("p a n -> p (a n)") for h in (hh, hl))
                    a = A.mark(A.after(mark).copy(hi, x[:, s, :]))
                    V.mark(V.after(a).tensor_tensor(lo, x[:, s, :], hi.bitcast(F32), ALU.subtract))

                def evict_relu2(i, o, psum, ready, read):
                    s = o % 2
                    a = read(V.then(ready).tensor_tensor(x[:, s, :], psum[:], rs[:], ALU.mult))
                    v = V.mark(V.after(a).scalar_tensor_tensor(x[:, s, :], x[:, s, :], 0.0, x[:, s, :],
                                                               ALU.max, ALU.mult))
                    hidden_done(i * 2 + o, s, v)

                def evict_swiglu(i, o, psum, ready, read):
                    v = read(V.then(ready).tensor_tensor(x[:, o, :], psum[:], rs[:], ALU.mult))
                    if o == 0:
                        A.mark(A.after(v).activation(x[:, 0, :], x[:, 0, :], ACT.Silu))
                    else:
                        v = V.mark(V.after(v, A.last()).tensor_tensor(x[:, 1, :], x[:, 0, :], x[:, 1, :], ALU.mult))
                        hidden_done(i, 1, v)

                for n, tiles in enumerate(groups):
                    turns, hidden = (tiles, evict_swiglu) if gated else (tiles // 2, evict_relu2)
                    per = {A: 2, V: 2 if gated else 4}
                    if n == 0:
                        ahead.run(hidden, per)
                    else:
                        stage(turns, 2, 2, KT, act_rhs, hidden, per=per)
                    hidden_last = V.last()
                    nc.tensor.wait_ge(V.sem, V.n - 2)
                    final = n == len(groups) - 1

                    def evict(i, o, psum, ready, read, n=n, final=final):
                        dst = acc[:, bass.ds(i * 2 + o, 1), :].rearrange("p a n -> p (a n)")
                        if n == 0:
                            done = read(V.after(ready).tensor_copy(dst, psum[:]))
                        else:
                            done = read(V.after(ready).tensor_tensor(dst, dst, psum[:], ALU.add))
                        if final:
                            square_sum(dst, sq[:], squares[:], done)

                    def hidden_rhs(o, k, last=hidden_last, tiles=tiles):
                        if o == 0 and k == tiles - 1:
                            PE.after(last)
                        return hh[:, k, :], hl[:, k, :]

                    stage(4, 2, 2, tiles, hidden_rhs, evict,
                          per={A: 2, G: 2} if final else None)
                    for e in (nc.scalar, nc.vector):
                        e.wait_ge(s_mm, used["units"] + 2)
            ahead = Ahead(ahead_turns) if ahead_turns else None
            bridge(acc, squares, x_dram, gain, out_dram, next_gain, name, ahead)
            return ahead

    x_in = t["x"]
    SP.wait_ge(*load.last())
    for n, d in enumerate((proj1[N1], proj2[N2])):
        stores[n].mark(SP.dma_start(d, x_in[0]))
    out_per = {outs[0]: 16, outs[1]: 16}
    with ExitStack() as at:
        buf = sb(at, "p1", [P, 2, L])
        rows = [F_] + [U_ + n for n in range(4)] + [Q_ + n for n in range(12)] + [X_ + n for n in range(12)]

        def evict(i, o, *rest):
            to_dram(proj1, rows[o] - o, buf)(i, o, *rest)

        n = len(rows)
        with Woven(products(0, used["units"], n, n, KT, act_rhs, evict), n * KT, 235.8) as w:
            norm_start(x_in, "g_pre_mix", "n1", lambda k, mark: (PE.after(mark), w.upto(k + 1)))
            s5(w)
        advance(n, n)
        barrier()
        gates = to_dram(proj1, GATE1, buf, gate="b_gate", n=6)
        first = dict(used)

        fox(lambda i: Woven(products(i, first["units"], 6, 6, KT, act_rhs, gates), 6 * KT, 48))
        advance(24, 24)
        barrier()
    merge(mixed1, proj1, GATE1, 3, "m1")
    ahead = mix_out(x_in, "g_post_mix", x1, "g_pre_mlp", "o1", 4)
    ahead = mlp(ahead, x1, "g_post_mlp", x2, "norm_mix_pre", (8, 8, 8, 8), False, "f1", 3)

    with ExitStack() as at:
        buf = sb(at, "p2", [P, 2, L])
        hgrn_const = hgrn_constants(at)
        ahead.run(to_dram(proj2, AQ, buf), out_per)
        barrier()
        first = dict(used)
        rest = to_dram(proj2, BQ, buf, n=8)
        band(lambda i: Woven(products(i, first["units"], 8, 8, KT, act_rhs, rest), 8 * KT, 48))
        advance(16, 16)
        barrier()
        gates = to_dram(proj2, GATE2, buf, gate="", n=10)
        base = dict(used)
        hgrn(hgrn_const, lambda i: Woven(products(i, base["units"], 10, 10, KT, act_rhs, gates), 10 * KT, 80))
        advance(20, 20)
        barrier()
        gates = to_dram(proj2, GATE2 + 20, buf, gate="")
        with Woven(products(0, used["units"], 12, 12, KT, act_rhs, gates), 12 * KT, 82):
            gmlp()
            lru()
        advance(12, 12)
        barrier()
    merge(mixed2, proj2, GATE2, 4, "m2")
    ahead = mix_out(x2, "norm_mix_post", x3, "norm_ffn_pre", "o2", 8)
    mlp(ahead, x3, "norm_ffn_post", out, None, (8, 8, 6), True, "f2")

    for s, n in ((0, (used["units"] + 4) // 2), (1, (used["units"] + 3) // 2)):
        SP.wait_ge(s_raw[s], 16 * n)
    barrier()


def _tiles(w):
    k, n = w.shape
    return w.reshape(k // P, P, n // P, P).transpose(2, 0, 1, 3)


def _units(tiles):
    n = tiles.shape[0] // 8
    return tiles.reshape(n, 8, P, P).transpose(0, 2, 1, 3).reshape(n, P, 8 * P)


def _stream(x):
    w_in = x["w_in"][0]
    n_f = F_ * P
    f = np.pad(w_in[:, n_f:n_f + FOX_HEADS], ((0, 0), (0, P - FOX_HEADS)))
    w = _tiles(w_in[:, :n_f])
    parts = [_tiles(f), w[U_:X_], w[Q_:F_], w[X_:Q_], _tiles(w_in[:, n_f + FOX_HEADS:])]
    wb = _tiles(x["w_branch"][0])
    parts += [wb, _tiles(x["w_out"][0])]
    w1, w2 = _tiles(x["w_ff1"][0]), _tiles(x["w_ff2"][0])
    for g in range(4):
        parts += [w1[8 * g:8 * g + 8], w2[:, 8 * g:8 * g + 8]]
    parts.append(_tiles(x["w_in_2"][0]))
    parts.append(_tiles(x["w_branch_2"][0].reshape(D, D)))
    parts.append(_tiles(x["w_out_2"][0]))
    w1, w2 = _tiles(x["w_ffn_in_2"][0]), _tiles(x["w_ffn_out_2"][0])
    n = HID2 // P
    w1 = np.stack([w1[:n], w1[n:]], 1)
    for g in (0, 8, 16):
        m = min(8, n - g)
        parts += [w1[g:g + m], np.pad(w2[:, g:g + m], ((0, 0), (0, 8 - m), (0, 0), (0, 0)))]
    tiles = np.concatenate([p.reshape(-1, P, P) for p in parts] + [np.zeros((3 * 8, P, P), np.float32)])
    return _units(tiles)


def _lay_out(x):
    def cols(v):
        return v.reshape(-1, P).T

    pairs = lambda v: v.reshape(PAIRS, P).T
    v = {
        "g_pre_mix": cols(x["g_pre_mix"]), "g_post_mix": cols(x["g_post_mix"]), "g_pre_mlp": cols(x["g_pre_mlp"]),
        "g_post_mlp": cols(x["g_post_mlp"]), "b_gate": cols(x["b_gate"]), "conv_w": cols(x["conv_w"]),
        "a_re": pairs(x["s5_a_re"]), "a_im": pairs(x["s5_a_im"]),
        "log_dt": np.repeat(x["s5_log_dt"].reshape(PAIRS, 2).T, S5_P, axis=0),
        "norm_mix_pre": cols(x["norm_mix_pre_2"]), "norm_mix_post": cols(x["norm_mix_post_2"]),
        "norm_ffn_pre": cols(x["norm_ffn_pre_2"]), "norm_ffn_post": cols(x["norm_ffn_post_2"]),
        "lb": cols(x["hgrn_lb_logits_2"]), "hgrn_g": cols(x["hgrn_norm_g_2"]), "gmlp_g": cols(x["gmlp_norm_g_2"]),
        "lru_cw": cols(x["lru_conv_w_2"]), "lru_cb": cols(x["lru_conv_b_2"]), "lru_ba": cols(x["lru_ba_2"]),
        "lru_bx": cols(x["lru_bx_2"]), "lru_lam": cols(x["lru_lambda_2"]),
        "b_f": np.repeat(x["fox_b_f"].reshape(FOX_HEADS, 1), P // FOX_HEADS, axis=0),
    }

    def diagonal(blocks, n):
        m, k, _ = blocks.shape
        out = np.zeros((m // n, n, k, n, k), np.float32)
        for i in range(n):
            out[:, i, :, i, :] = blocks.reshape(m // n, n, k, k)[:, i]
        return out.reshape(m // n, n * k, n * k)

    dist = np.clip(LEFT + np.arange(P)[:, None] - np.arange(BAND)[None, :], -63, 256) + 63
    b = np.stack([x["s5_b_re"][0], x["s5_b_im"][0]])
    c = np.stack([x["s5_c_re"][0], x["s5_c_im"][0]]).transpose(0, 1, 3, 2)

    def by_pair(v):
        return v.reshape(2, PAIRS, P, S5_H).transpose(2, 0, 1, 3)

    return {
        "x": x["x"][0].T.reshape(KT, P, L),
        "vec": np.concatenate([v[n] for n, _ in VEC_NAMES], axis=1),
        "stream": _stream(x),
        "s5_b": by_pair(b), "s5_c": by_pair(c),
        "s5_d": x["s5_d"][0].T,
        "glu": diagonal(x["s5_w_glu"][0], 8),
        "rel": x["attn_rel_bias_2"][0][:, dist],
        "gm_w": x["gmlp_ws_2"][0].transpose(0, 2, 1), "gm_b": x["gmlp_bs_2"][0],
        "lru_w": np.stack([diagonal(x["lru_wa_2"][0], 2), diagonal(x["lru_wx_2"][0], 2)]),
    }


def kernel(**inputs):
    import concourse.bacc as bacc
    from concourse.bass_utils import run_bass_kernel_spmd

    nc = bacc.Bacc("TRN2", target_bir_lowering=False, num_devices=1)
    arrays, t = {}, {}
    for name, a in _lay_out({n: np.asarray(v) for n, v in inputs.items()}).items():
        a = np.ascontiguousarray(a)
        arrays["in_" + name] = a
        t[name] = nc.dram_tensor("in_" + name, a.shape, mybir.dt.from_np(a.dtype), kind="ExternalInput").ap()
    out = nc.dram_tensor("out", (KT, P, L), F32, kind="ExternalOutput").ap()
    build(nc, t, out)
    r = run_bass_kernel_spmd(nc, [arrays], core_ids=[0])
    y = r.results[0]["out"]
    return np.ascontiguousarray(y.reshape(D, L).T).reshape(1, L, D)
```
